# Optimizing a Trainium2 kernel written in Bass

```python
import jax, jax.numpy as jnp
from jax import lax
import numpy as np

D_MODEL = 1024
BATCH = 1
SEQ = 512
DEPTH = 1

CHUNK = 64
HEAD_DIM = 64
SB_HEADS = 8
FOX_HEADS = 8
SB_WIDTH = SB_HEADS * HEAD_DIM
FOX_WIDTH = FOX_HEADS * HEAD_DIM
MIX_WIDTH = SB_WIDTH + FOX_WIDTH
FFN_HIDDEN = 2816
Q_BLOCK = 128
N_SUBLAYERS = 3
EPS = 1e-6
IN_COLS = 3 * SB_WIDTH + 4 * FOX_WIDTH + FOX_HEADS

kernel_name = 'hybrid_stickbreak_forgetting_macaron_block'

def rmsnorm(x, g):
    xf = x.astype(jnp.float32)
    y = xf * lax.rsqrt(jnp.mean(xf * xf, axis=-1, keepdims=True) + EPS)
    return (y * g.astype(jnp.float32)).astype(x.dtype)

def modulate(x, g, shift, scale):
    return rmsnorm(x, g) * (1.0 + scale[:, None, :]) + shift[:, None, :]

def swiglu(h, w_up, w_down):
    gate, up = jnp.split(h @ w_up, 2, axis=-1)
    return (jax.nn.silu(gate) * up) @ w_down

def _to_blocks(a):
    b, s = a.shape[:2]
    return jnp.moveaxis(a.reshape(b, s // Q_BLOCK, Q_BLOCK, *a.shape[2:]), 1, 0)

def _from_blocks(o):
    o = jnp.moveaxis(o, 0, 1)
    b, nb, qb, h, dh = o.shape
    return o.reshape(b, nb * qb, h, dh)

def stick_breaking_attention(q, k, v):
    s_len = q.shape[1]
    scale = HEAD_DIM ** -0.5
    kf = k.astype(jnp.float32)
    vf = v.astype(jnp.float32)
    key_pos = jnp.arange(s_len)

    def block(args):
        q_blk, t0 = args
        z = jnp.einsum('bqhd,bkhd->bhqk', q_blk.astype(jnp.float32), kf) * scale
        q_pos = t0 + jnp.arange(Q_BLOCK)
        strict = key_pos[None, :] < q_pos[:, None]
        log_beta = jax.nn.log_sigmoid(z)
        log_keep = jnp.where(strict, log_beta - z, 0.0)
        suffix = lax.cumsum(log_keep, axis=3, reverse=True) - log_keep
        w = jnp.where(strict, jnp.exp(log_beta + suffix), 0.0)
        return jnp.einsum('bhqk,bkhd->bqhd', w, vf)

    t0s = jnp.arange(s_len // Q_BLOCK, dtype=jnp.int32) * Q_BLOCK
    o = lax.map(block, (_to_blocks(q), t0s))
    return _from_blocks(o).astype(v.dtype)

def forgetting_attention(q, k, v, log_f_cum):
    s_len = q.shape[1]
    scale = HEAD_DIM ** -0.5
    kf = k.astype(jnp.float32)
    vf = v.astype(jnp.float32)
    key_pos = jnp.arange(s_len)
    f_keys = jnp.moveaxis(log_f_cum, 1, 2)

    def block(args):
        q_blk, f_q, t0 = args
        z = jnp.einsum('bqhd,bkhd->bhqk', q_blk.astype(jnp.float32), kf) * scale
        z = z + jnp.moveaxis(f_q, 1, 2)[..., None] - f_keys[:, :, None, :]
        q_pos = t0 + jnp.arange(Q_BLOCK)
        causal = key_pos[None, :] <= q_pos[:, None]
        p = jax.nn.softmax(jnp.where(causal, z, -jnp.inf), axis=-1)
        return jnp.einsum('bhqk,bkhd->bqhd', p, vf)

    t0s = jnp.arange(s_len // Q_BLOCK, dtype=jnp.int32) * Q_BLOCK
    o = lax.map(block, (_to_blocks(q), _to_blocks(log_f_cum), t0s))
    return _from_blocks(o).astype(v.dtype)

def setup_inputs(seed: int = 0) -> dict:
    key = jax.random.key(seed)
    ks = jax.random.split(key, 24)
    f32 = jnp.float32

    def nrm(k, shape, s):
        return jax.random.normal(k, shape, f32) * s

    def gain(k, shape):
        return 1.0 + 0.05 * jax.random.normal(k, shape, f32)

    d = D_MODEL
    return {
        'x': jax.random.normal(ks[0], (BATCH, SEQ, d), f32),
        'c': jax.random.normal(ks[1], (BATCH, d), f32),
        'w_ada': nrm(ks[2], (DEPTH, d, 3 * N_SUBLAYERS * d), 0.5 * d ** -0.5),
        'b_ada': nrm(ks[3], (DEPTH, 3 * N_SUBLAYERS * d), 0.02),
        'g_ffn1': gain(ks[4], (DEPTH, d)),
        'w_ffn1_up': nrm(ks[5], (DEPTH, d, 2 * FFN_HIDDEN), d ** -0.5),
        'w_ffn1_down': nrm(ks[6], (DEPTH, FFN_HIDDEN, d), FFN_HIDDEN ** -0.5),
        'g_mix': gain(ks[7], (DEPTH, d)),
        'w_in': nrm(ks[8], (DEPTH, d, IN_COLS), d ** -0.5),
        'b_forget': 2.0 + 0.5 * jax.random.normal(ks[9], (DEPTH, FOX_HEADS), f32),
        'g_fox_q': gain(ks[10], (DEPTH, HEAD_DIM)),
        'g_fox_k': gain(ks[11], (DEPTH, HEAD_DIM)),
        'g_sb_out': gain(ks[12], (DEPTH, SB_WIDTH)),
        'g_fox_out': gain(ks[13], (DEPTH, FOX_WIDTH)),
        'w_out': nrm(ks[14], (DEPTH, MIX_WIDTH, d), MIX_WIDTH ** -0.5),
        'g_ffn2': gain(ks[15], (DEPTH, d)),
        'w_ffn2_up': nrm(ks[16], (DEPTH, d, 2 * FFN_HIDDEN), d ** -0.5),
        'w_ffn2_down': nrm(ks[17], (DEPTH, FFN_HIDDEN, d), FFN_HIDDEN ** -0.5),
        'g_final': gain(ks[18], (d,)),
    }

def reference(x, c, w_ada, b_ada, g_ffn1, w_ffn1_up, w_ffn1_down, g_mix, w_in, b_forget,
              g_fox_q, g_fox_k, g_sb_out, g_fox_out, w_out, g_ffn2, w_ffn2_up, w_ffn2_down,
              g_final):
    b, s, _ = x.shape
    cond = jax.nn.silu(c)
    split_pts = [3 * SB_WIDTH, 3 * SB_WIDTH + 3 * FOX_WIDTH, 3 * SB_WIDTH + 4 * FOX_WIDTH]
    for l in range(DEPTH):
        ada = (cond @ w_ada[l] + b_ada[l]).reshape(b, N_SUBLAYERS, 3, D_MODEL)
        shift, scale, gate = ada[:, :, 0], ada[:, :, 1], ada[:, :, 2]

        h = modulate(x, g_ffn1[l], shift[:, 0], scale[:, 0])
        x = x + 0.5 * gate[:, 0][:, None, :] * swiglu(h, w_ffn1_up[l], w_ffn1_down[l])

        h = modulate(x, g_mix[l], shift[:, 1], scale[:, 1])
        proj = h @ w_in[l]
        sb_qkv, fox_qkv, fox_gate, f_logit = jnp.split(proj, split_pts, axis=-1)
        sb_q, sb_k, sb_v = [t.reshape(b, s, SB_HEADS, HEAD_DIM) for t in jnp.split(sb_qkv, 3, axis=-1)]
        fx_q, fx_k, fx_v = [t.reshape(b, s, FOX_HEADS, HEAD_DIM) for t in jnp.split(fox_qkv, 3, axis=-1)]
        fx_q = rmsnorm(fx_q, g_fox_q[l])
        fx_k = rmsnorm(fx_k, g_fox_k[l])
        log_f = jax.nn.log_sigmoid(f_logit.astype(jnp.float32) + b_forget[l].astype(jnp.float32))
        log_f_cum = jnp.cumsum(log_f, axis=1)

        o_sb = stick_breaking_attention(sb_q, sb_k, sb_v)
        o_fx = forgetting_attention(fx_q, fx_k, fx_v, log_f_cum)
        o_sb = rmsnorm(o_sb, g_sb_out[l].reshape(SB_HEADS, HEAD_DIM)).reshape(b, s, SB_WIDTH)
        o_fx = rmsnorm(o_fx, g_fox_out[l].reshape(FOX_HEADS, HEAD_DIM)).reshape(b, s, FOX_WIDTH)
        o_fx = o_fx * jax.nn.sigmoid(fox_gate)
        mix = jnp.concatenate([o_sb, o_fx], axis=-1) @ w_out[l]
        x = x + gate[:, 1][:, None, :] * mix

        h = modulate(x, g_ffn2[l], shift[:, 2], scale[:, 2])
        x = x + 0.5 * gate[:, 2][:, None, :] * swiglu(h, w_ffn2_up[l], w_ffn2_down[l])
    return rmsnorm(x, g_final)


_drawn_inputs = setup_inputs


def setup_inputs(seed=0):
    import zlib

    import numpy as np

    out = dict(_drawn_inputs(seed))
    spreads = {}
    factors = {'g_ffn1': 7.599,
     'g_mix': 3.992,
     'g_fox_q': 8.0,
     'g_fox_k': 8.0,
     'g_sb_out': 27.889,
     'g_fox_out': 42.478,
     'g_ffn2': 7.903}
    for name, (base, spread) in spreads.items():
        noise = np.random.default_rng([zlib.crc32(name.encode()), seed]).standard_normal(out[name].shape)
        drawn = base * np.exp(spread * noise) if base else spread * noise
        out[name] = __import__('jax').numpy.asarray(drawn.astype(out[name].dtype))
    for name, factor in factors.items():
        out[name] = (out[name] * factor).astype(out[name].dtype)
    return out
```

```python
from contextlib import ExitStack

import concourse.bass as bass
from concourse import mybir

ALU = mybir.AluOpType
ACT = mybir.ActivationFunctionType
F32 = mybir.dt.float32
F32R = mybir.dt.float32r
BF16 = mybir.dt.bfloat16
AX_X = mybir.AxisListType.X
EXP_LN_SET = "natural_log_exp_and_others"

P = 128
SEQ = 512
TB = SEQ // P
D = 1024
KC = D // P
FFN = 2816
FC = FFN // P
HD = 64
JOBS = 8
SBJ = 4
EPS = 1e-6
N_CONSTS = 17
NEG = -(2.0 ** 126)
WS = 1024
DOWN_PARTS = ((0, 8), (8, 8), (16, 6))
NAT_PARTS = ((0, 2), (2, 2), (4, 1), (5, 1)) + tuple((k, 2) for k in range(6, 22, 2))
NADA = 9 * KC
ADA0 = 2 * KC

T_UP1 = 0
T_DOWN1 = T_UP1 + 2 * FC
T_MIX = T_DOWN1 + 3 * KC
N_MIX = 4 * 2 + 2 * JOBS + (JOBS - SBJ)
T_OUT = T_MIX + N_MIX
T_UP2 = T_OUT + KC
T_DOWN2 = T_UP2 + 2 * FC
N_TILES = T_DOWN2 + 2 * len(NAT_PARTS)
RAW = 4
SPLIT = 2

UNITS = (
    ((0, 3, 0),),
    ((0, 2, 0), (0, 0, 384)),
    ((0, 1, 0), (1, 1, 256)),
    ((1, 2, 0), (1, 0, 384)),
    ((1, 3, 0),),
)
PT_BLOCKS = 13
ZERO_BLOCK = 11


def chunks():
    order = [("v", 0), ("q", 0), ("k", 0)]
    for j in range(JOBS):
        if j + 1 < JOBS:
            order += [("q", j + 1), ("k", j + 1)]
            if j + 1 >= SBJ:
                order.append(("g", j + 1))
        if j % 2 == 0 and j // 2 + 1 < 4:
            order.append(("v", j // 2 + 1))
    out, tile = [], T_MIX
    for kind, n in order:
        out.append((kind, n, {"v": 0, "q": 0, "k": 1, "g": 0}[kind], tile))
        tile += 2 if kind == "v" else 1
    assert tile == T_MIX + N_MIX
    return out


CHUNKS = chunks()


def mixer_steps():
    steps, norms, pending = [], [], []

    def flush():
        while pending:
            steps.append(("norm", pending.pop(0)))

    def square(kind, n, chunk=None):
        flush()
        norms.append((kind, n, chunk))
        steps.append(("square", len(norms) - 1))
        pending.append(len(norms) - 1)

    def proj(c, part, half):
        kind, n, _, tile = CHUNKS[c]
        steps.append(("proj", tile + part, c, half))
        flush()
        if half == 1:
            steps.append(("split", tile + part + SPLIT))
            if kind != "v" or part == 1:
                if kind in "qk" and n >= SBJ:
                    square(kind, n, c)
                else:
                    steps.append(("evac", c))

    def halves(c):
        return [(c, part, half) for part in range(2 if CHUNKS[c][0] == "v" else 1) for half in range(2)]

    for c in range(3):
        for item in halves(c):
            proj(*item)
    ahead = 3
    for j in range(JOBS):
        items = []
        while ahead < len(CHUNKS) and (CHUNKS[ahead][1] == (j // 2 + 1 if CHUNKS[ahead][0] == "v" else j + 1)
                                       and not (CHUNKS[ahead][0] == "v" and j % 2)):
            items += halves(ahead)
            ahead += 1
        per = -(-len(items) // 5)
        gaps = [items[g * per:(g + 1) * per] for g in range(5)]

        def gap(g):
            for item in gaps[g]:
                proj(*item)
            flush()

        steps += [("scores", j, 0), ("scores", j, 1)]
        if j:
            steps.append(("values", j - 1, 1))
            square("o", j - 1)
        steps.append(("weigh", j, 0))
        gap(0)
        steps += [("weigh", j, 1), ("exp", j, 0), ("turn", j, 0), ("scores", j, 2)]
        gap(1)
        steps += [("weigh", j, 2), ("exp", j, 1), ("turn", j, 1), ("scores", j, 3)]
        gap(2)
        steps += [("weigh", j, 3), ("exp", j, 2), ("turn", j, 2), ("scores", j, 4)]
        gap(3)
        steps += [("values", j, 0), ("weigh", j, 4), ("exp", j, 3), ("turn", j, 3)]
        gap(4)
        more = j + 1 < JOBS and j + 1 >= SBJ
        if more:
            steps.append(("decay", j + 1, 0))
        steps += [("exp", j, 4), ("turn", j, 4)]
        if more:
            steps.append(("decay", j + 1, 1))
    steps.append(("values", JOBS - 1, 1))
    square("o", JOBS - 1)
    flush()
    assert ahead == len(CHUNKS)
    return steps, norms


STEPS, NORMS = mixer_steps()


def hybrid_block_kernel(
    nc: bass.Bass, x, c, w_ada, b_ada, g_ffn1, w_ffn1_up, w_ffn1_down, g_mix, w_in, b_forget,
    g_fox_q, g_fox_k, g_sb_out, g_fox_out, w_out, g_ffn2, w_ffn2_up, w_ffn2_down, g_final, out,
):
    ctx = ExitStack()
    with ctx:
        def sem(name):
            return ctx.enter_context(nc.semaphore(name))

        slab = ctx.enter_context(nc.sbuf_tensor("slab", [P, 207 * 256], F32))
        top = [0]

        def size(shape, dt):
            n = 2 if dt == BF16 else 4
            for s in shape[1:]:
                n *= s
            return -(-n // 32) * 32

        def at(name, shape, dt, offset):
            return nc.alloc_sbuf_tensor_at(name, shape, dt, offset=slab_base + offset)

        def keep(name, shape, dt=F32):
            t = at(name, shape, dt, top[0])
            top[0] += size(shape, dt)
            return t

        slab_base = nc.sbuf_base - 207 * 1024

        xT = keep("xT", [P, KC, SEQ])
        w_raw = keep("w_raw", [P, RAW, WS])
        w_hi = keep("w_hi", [P, SPLIT, WS], F32R)
        w_lo = keep("w_lo", [P, SPLIT, WS], F32R)
        ident = keep("ident", [P, P])
        ident_bf = keep("ident_bf", [P, P], BF16)
        mask_strict = keep("mask_strict", [P, P], BF16)
        mask_causal = keep("mask_causal", [P, P], BF16)
        pair_mean = keep("pair_mean", [P, P])
        ones = keep("ones", [P, 1])
        rowsel_f = keep("rowsel_f", [HD, JOBS])
        rowsel = keep("rowsel", [HD, JOBS], F32R)
        vcol = keep("vcol", [P, P])
        ada_raw = keep("ada_raw", [P, NADA])
        ada = keep("ada", [P, NADA])
        amp = keep("amp", [P, KC])
        gate = keep("gate", [P, KC])
        cond = keep("cond", [P, KC])
        gq8 = keep("gq8", [P, 1])
        b_f = keep("b_f", [JOBS, 1])
        small = keep("small", [P, 32])
        tmp_a = keep("tmp_a", [P, 2, SEQ])
        tmp_b = keep("tmp_b", [P, 2, SEQ])
        ssum = keep("ssum", [P, SEQ])
        rstd = keep("rstd", [P, SEQ])
        h_offset = top[0]
        h_hi = keep("h_hi", [P, KC, SEQ], F32R)
        h_lo = keep("h_lo", [P, KC, SEQ], F32R)
        region = top[0]

        hid_hi = at("hid_hi", [P, FC, SEQ], F32R, region)
        hid_lo = at("hid_lo", [P, FC, SEQ], F32R, region + FC * SEQ * 4)
        ada_w = at("ada_w", [P, 2, KC, P], F32, region + 2 * FC * SEQ * 4)
        ada_acc = at("ada_acc", [P, 2, P], F32, region + 2 * FC * SEQ * 4 + 2 * D * 4)
        x_nat = at("x_nat", [P, TB, D], F32, region)
        vecs = at("vecs", [P, P], F32, region + TB * D * 4)
        x2_nat = at("x2_nat", [P, TB, D], F32, h_offset)
        gate_row = at("gate_row", [P, D], F32, h_offset + TB * D * 4)
        gfin_row = at("gfin_row", [P, D], F32, h_offset + (TB + 1) * D * 4)
        diag = at("diag", [P, KC, P], F32, h_offset + (TB + 2) * D * 4)

        top[0] = region
        v_hi = keep("v_hi", [P, 2, 2 * TB, 3, HD], F32R)
        v_lo = keep("v_lo", [P, 2, 2 * TB, 3, HD], F32R)
        qk_hi = keep("qk_hi", [P, 2, 2, SEQ], F32R)
        qk_lo = keep("qk_lo", [P, 2, 2, SEQ], F32R)
        pt_hi = keep("pt_hi", [P, 2, PT_BLOCKS, P], F32R)
        pt_lo = keep("pt_lo", [P, 2, PT_BLOCKS, P], F32R)
        o_hi = keep("o_hi", [P, JOBS, SEQ], F32R)
        o_lo = keep("o_lo", [P, JOBS, SEQ], F32R)
        beyond = top[0]
        f_keys = keep("f_keys", [P, 2, SEQ])
        f_cum = keep("f_cum", [HD, SEQ], F32R)
        sig = keep("sig", [P, 2, SEQ])
        nrm = keep("nrm", [P, SEQ])
        assert beyond >= region + 2 * FC * SEQ * 4 + 2 * D * 4 + 2 * P * 4
        wf_hi = at("wf_hi", [P, KC, P], F32R, beyond)
        wf_lo = at("wf_lo", [P, KC, P], F32R, beyond + 3 * SEQ * 4)
        wf_raw = at("wf_raw", [P, KC, JOBS], F32, beyond + 5 * SEQ * 4)
        assert top[0] <= 207 * 1024 and region + 2 * FC * SEQ * 4 + 2 * D * 4 + P * 8 <= 207 * 1024, top

        bank = [ctx.enter_context(nc.psum_tensor(f"bank{i}", [P, SEQ], F32)) for i in range(8)]

        vec_zero, vec_in, fbias_in, wf_in = sem("vec_zero"), sem("vec_in"), sem("fbias_in"), sem("wf_in")
        x_in = [sem("x_in0"), sem("x_in1")]
        w_in_sem = [sem(f"w_loaded{i}") for i in range(RAW)]
        ada_in = [sem("ada_loaded0"), sem("ada_loaded1")]
        gfin_in = sem("gfin_in")
        consts = sem("consts")
        w_hi_done, w_lo_done, w_used = sem("w_hi_done"), sem("w_lo_done"), sem("w_used")
        vec_turned, vec_cols = sem("vec_turned"), sem("vec_cols")
        cond_ready = sem("cond_ready")
        x_turned = sem("x_turned")
        x_upd, sq_done, sq_added = sem("x_upd"), sem("sq_done"), sem("sq_added")
        sum_done, ln_done, rstd_done = sem("sum_done"), sem("ln_done"), sem("rstd_done")
        xn_done, h_full, h_hi_done, h_done = sem("xn_done"), sem("h_full"), sem("h_hi_done"), sem("h_done")
        ada_prod, ada_red, ada_col, ada_out, coef, coef_dve = (
            sem("ada_prod"), sem("ada_red"), sem("ada_col"), sem("ada_out"), sem("coef"), sem("coef_dve"))
        silu_done, hid_f32, hid_hi_done, hid_done = (
            sem("silu_done"), sem("hid_f32"), sem("hid_hi_done"), sem("hid_done"))
        mix_zero = sem("mix_zero")
        wf_split, wf_split_hi, f_logit, f_act, f_dve = (
            sem("wf_split"), sem("wf_split_hi"), sem("f_logit"), sem("f_act"), sem("f_dve"))
        chunk_hi, qk_ready, v_ready = (
            sem("chunk_hi"), sem("qk_ready"), sem("v_ready"))
        g_copy, g_exp, g_plus, g_ready = sem("g_copy"), sem("g_exp"), sem("g_plus"), sem("g_ready")
        s_done, relu_done, abs_done, eneg_done, e_ready, scan_done, d_ready, p_ready_sb = (
            sem("s_done"), sem("relu_done"), sem("abs_done"), sem("eneg_done"), sem("e_ready"),
            sem("scan_done"), sem("d_ready"), sem("p_ready_sb"))
        even_scored = sem("even_scored")
        max_done, zf_ready, exp_done, inv_done, p_ready_fx = (
            sem("max_done"), sem("zf_ready"), sem("exp_done"), sem("inv_done"), sem("p_ready_fx"))
        t_done, pt_hi_done, pt_ready, pv_done = sem("t_done"), sem("pt_hi_done"), sem("pt_ready"), sem("pv_done")
        nsq_done, stat_done, stat_read, nrstd_done, nrm_f32, nrm_gated, nrm_hi, nrm_lo = (
            sem("nsq_done"), sem("stat_done"), sem("stat_read"), sem("nrstd_done"), sem("nrm_f32"),
            sem("nrm_gated"), sem("nrm_hi"), sem("nrm_lo"))
        fk_ready = sem("fk_ready")
        out_acc, gacc_done, diag_done, row_done, row_copied = (
            sem("out_acc"), sem("gacc_done"), sem("diag_done"), sem("row_done"), sem("row_copied"))
        x2_turned, x2_copied = sem("x2_turned"), sem("x2_copied")
        scaled, x3_done, ssq_done, ms_done, fln_done, frstd_done, y_done, stored = (
            sem("scaled"), sem("x3_done"), sem("ssq_done"), sem("ms_done"), sem("fln_done"), sem("frstd_done"),
            sem("y_done"), sem("stored"))

        up_v = [w.rearrange("o (k p) n -> (o p) k n", p=P) for w in (w_ffn1_up, w_ffn2_up)]
        down_v = [w.rearrange("o (k p) n -> (o p) k n", p=P) for w in (w_ffn1_down, w_ffn2_down)]
        in_v = w_in.rearrange("o (k p) n -> (o p) k n", p=P)
        out_v = w_out.rearrange("o (k p) n -> (o p) k n", p=P)
        ada_v = w_ada.rearrange("o (k p) n -> (o p) k n", p=P)

        def col(row, n=1):
            return vcol[:, row:row + n]

        R_BADA, R_G = 0, (NADA, NADA + KC, NADA + 2 * KC)
        R_GO = NADA + 3 * KC
        R_C = R_GO + JOBS
        R_GQ, R_GK = R_C + KC, R_C + KC + 1

        def tile8(buf, slot, k=KC):
            return buf[:, slot, 0:WS].rearrange("p (k n) -> p k n", k=KC)[:, 0:k, :]

        def tile4(buf, slot):
            return buf[:, slot, :].rearrange("p (k n) -> p k n", k=4)

        def tile2(buf, slot):
            return buf[:, slot, :].rearrange("p (k n) -> p k n", k=2)

        def turned(u):
            if u in (0, 4):
                return [(u // 4, slice(3, 13, 3), slice(0, 4))]
            if u in (1, 3):
                return [(u // 3, slice(2, 9, 3), slice(0, 3)), (u // 3, slice(0, 1), slice(3, 4))]
            return [(0, slice(1, 5, 3), slice(0, 2)), (1, slice(1, 5, 3), slice(2, 4))]

        def blocks(b, which):
            return b[:].rearrange("p (b n) -> p b n", n=P)[:, which, :]


        def norm_of(what, j):
            return [n for n, e in enumerate(NORMS) if e[0:2] == (what, j)][0]

        def chunk_read(ci):
            what, n, _, _ = CHUNKS[ci]
            if what == "v":
                return v_ready, 2 * n + 2
            if what == "g":
                return g_copy, n - SBJ + 1
            if n < SBJ:
                return qk_ready, 2 * n + 1 + int(what == "k")
            return nrm_f32, norm_of(what, n) + 1

        def z_read(unit):
            return (d_ready, unit + 1) if unit < 5 * SBJ else (max_done, unit - 5 * SBJ + 1)

        def tile_used(t):
            half, n = divmod(t - T_DOWN2, len(NAT_PARTS))
            if half >= 0 and n == len(NAT_PARTS) - 1:
                return out_acc, TB * (half + 1)
            return w_used, t + 1 - max(half, 0)

        def stat_uses(until):
            n = 0
            for step in STEPS:
                n += step[0] in ("norm", "decay")
                if step == until:
                    return n

        block = ctx.enter_context(nc.Block())

        @block.gpsimd
        def _(pool):
            g = nc.gpsimd
            made = [0]

            def link(ins):
                made[0] += 1
                ins.then_inc(consts, 1)
                pool.wait_ge(consts, made[0])

            def select(buf, compare, fill, base, width):
                link(g.affine_select(out=buf[:], in_=buf[:], compare_op=compare, fill=fill, base=base,
                                     pattern=[[-1, width]], channel_multiplier=1))

            g.memset(vecs[:], 0.0).then_inc(vec_zero, 1)
            pool.wait_ge(vec_zero, 1)
            for buf in (ident, ident_bf, mask_strict, mask_causal, pair_mean, rowsel_f):
                link(g.memset(buf[:], 0.0))
            link(g.memset(ones[:], 1.0))
            for buf in (ident, ident_bf):
                select(buf, ALU.not_equal, 1.0, 0, P)
            select(mask_strict, ALU.is_gt, NEG, 0, P)
            select(mask_causal, ALU.is_ge, NEG, 0, P)
            for h in range(2):
                link(g.memset(pair_mean[h * HD:(h + 1) * HD, h * HD:(h + 1) * HD], 1.0 / HD))
            for base in (0, -32):
                select(rowsel_f, ALU.not_equal, 1.0, base, JOBS)
            for buf in (wf_hi, wf_lo):
                link(g.memset(buf[:].bitcast(F32), 0.0))
            assert made[0] == N_CONSTS
            pool.wait_ge(w_used, T_MIX)
            for n, part in enumerate((v_hi[:, :, :, 1, :], v_lo[:, :, :, 1, :], pt_hi[:, :, ZERO_BLOCK, :],
                                      pt_lo[:, :, ZERO_BLOCK, :], f_cum[:])):
                g.memset(part.bitcast(F32), 0.0).then_inc(mix_zero, 1)
                pool.wait_ge(mix_zero, n + 1)

        @block.sync
        def _(sp):
            def load_w(t, slot, dst, src, first=False):
                if not first:
                    sp.wait_ge(w_lo_done, t - RAW + 1)
                sp.dma_start(dst, src).then_inc(w_in_sem[slot], 16)

            def load_up(ffn, base, f, j, first=False):
                for half in range(2):
                    load_w(base + 2 * f + half, 2 * j + half, tile8(w_raw, 2 * j + half),
                           up_v[ffn][:, :, bass.ds(f * P + half * FFN, P)], first)

            def load_ada(a, slot, first=False):
                if not first:
                    sp.wait_ge(ada_red, a - 1)
                sp.dma_start(ada_w[:, slot, :, :], ada_v[:, :, bass.ds(a * P, P)]).then_inc(ada_in[slot], 16)

            sp.wait_ge(vec_zero, 1)
            n = 0
            for src, row, rows in ((b_ada, R_BADA, NADA), (g_ffn1, R_G[0], KC), (g_mix, R_G[1], KC),
                                   (g_ffn2, R_G[2], KC), (g_sb_out, R_GO, SBJ), (g_fox_out, R_GO + SBJ, SBJ),
                                   (c, R_C, KC)):
                sp.dma_start(vecs[row:row + rows, :], src.rearrange("o (r p) -> (o r) p", p=P)).then_inc(vec_in, 16)
                n += 1
            for src, row in ((g_fox_q, R_GQ), (g_fox_k, R_GK)):
                for h in range(2):
                    sp.dma_start(vecs[row:row + 1, h * HD:(h + 1) * HD], src).then_inc(vec_in, 16)
                    n += 1
            assert n == 11
            sp.dma_start(b_f[:], b_forget.rearrange("o h -> h o")).then_inc(fbias_in, 16)
            sp.dma_start(wf_raw[:], in_v[:, :, 7 * 512:7 * 512 + JOBS]).then_inc(wf_in, 16)
            for half in range(2):
                sp.dma_start(x_nat[:, :, half * 512:(half + 1) * 512],
                             x.rearrange("o (t p) d -> (o p) t d", p=P)[:, :, half * 512:(half + 1) * 512])\
                  .then_inc(x_in[half], 16)
            for a in range(2):
                load_ada(a, a, True)
            for j in range(2):
                load_up(0, T_UP1, j, j, True)
            with sp.Fori(1, ADA0 // 2) as i:
                for s in range(2):
                    load_ada(2 * i + s, s)
            for s in range(4):
                load_ada(ADA0 + s, s % 2)
            with sp.Fori(1, FC // 2) as i:
                for j in range(2):
                    load_up(0, T_UP1, 2 * i + j, j)
                    for s in range(2):
                        load_ada(ADA0 + 4 * i + 2 * j + s, s)
            with sp.Fori(0, 2) as i:
                for j in range(4):
                    for part, (k0, nk) in enumerate(DOWN_PARTS):
                        t = T_DOWN1 + 3 * j + part
                        load_w(12 * i + t, t % RAW, tile8(w_raw, t % RAW, nk),
                               down_v[0][:, k0:k0 + nk, bass.ds((4 * i + j) * P, P)])
                        if (3 * j + part) % 2 == 0:
                            a = (3 * j + part) // 2
                            load_ada(6 * i + ADA0 + 2 * FC + a, a % 2)
            for kind, n, _, tile in CHUNKS:
                if kind == "v":
                    c0 = (2 if n < 2 else 5) * 512 + (n % 2) * 256
                    for part in range(2):
                        t = tile + part
                        load_w(t, t % RAW, tile4(w_raw, t % RAW), in_v[:, 4 * part:4 * part + 4, c0:c0 + 256])
                else:
                    c0 = (3 * 512 if n >= SBJ else 0) + (n % SBJ) * P + {"q": 0, "k": 512, "g": 3 * 512}[kind]
                    load_w(tile, tile % RAW, tile8(w_raw, tile % RAW), in_v[:, :, c0:c0 + P])
            with sp.Fori(0, KC // RAW) as i:
                for j in range(RAW):
                    load_w(T_OUT + RAW * i + j, j, tile8(w_raw, j), out_v[:, :, bass.ds((RAW * i + j) * P, P)])
            with sp.Fori(0, FC // 2) as i:
                for j in range(2):
                    load_up(1, T_UP2, 2 * i + j, j)
            with sp.Fori(0, 2) as i:
                for n, (k0, nk) in enumerate(NAT_PARTS):
                    load_w(len(NAT_PARTS) * i + T_DOWN2 + n, n % RAW, tile2(w_raw, n % RAW)[:, 0:nk, :],
                           down_v[1][:, k0:k0 + nk, bass.ds(i * 512, 512)])
                    if n == RAW - 1:
                        sp.wait_ge(w_used, T_DOWN2)
                        sp.dma_start(gfin_row[:, bass.ds(i * 512, 512)],
                                     g_final[bass.ds(i * 512, 512)].partition_broadcast(P)).then_inc(gfin_in, 16)
            for t in range(TB):
                sp.wait_ge(y_done, t + 1)
                sp.dma_start(out[0, t * P:(t + 1) * P, :], x2_nat[:, t, :]).then_inc(stored, 16)
            sp.wait_ge(stored, 16 * TB)

        @block.tensor
        def _(pe):
            mm = nc.tensor.matmul

            def three(dst, wh, wl, xh, xl, start, stop, skip=False):
                mm(dst, wh, xh, start=start, stop=False, skip_group_check=skip)
                mm(dst, wh, xl, start=False, stop=False, skip_group_check=skip)
                return mm(dst, wl, xh, start=False, stop=stop, skip_group_check=skip)

            def split_ready(t):
                pe.wait_ge(w_lo_done, t + 1)

            pe.wait_ge(consts, N_CONSTS)
            pe.wait_ge(vec_in, 16 * 11)
            nc.tensor.transpose(bank[6][:, 0:P], vecs[:], ident[:]).then_inc(vec_turned, 1)
            for k in range(KC):
                if k % 4 == 0:
                    pe.wait_ge(x_in[k // 4], 16)
                if k >= 2:
                    pe.wait_ge(x_upd, k - 1)
                for t in range(TB):
                    last = nc.tensor.transpose(bank[k % 2][:, t * P:(t + 1) * P], x_nat[:, t, k * P:(k + 1) * P],
                                               ident[:])
                last.then_inc(x_turned, 1)

            def sum_squares(s):
                pe.wait_ge(sq_added, KC * (s + 1))
                if s == 0:
                    pe.wait_ge(vec_cols, 1)
                mm(bank[6][:], ones[:, 0:1].broadcast_to([P, P]), ssum[:], start=True, stop=True).then_inc(sum_done, 1)

            def ada_column(a, slot, first=False):
                pe.wait_ge(ada_red, a + 1)
                if not first:
                    pe.wait_ge(ada_out, a - 1)
                mm(bank[4 + slot][:, 0:1], ada_acc[:, slot, :], ones[:], start=True, stop=True).then_inc(ada_col, 1)

            sum_squares(0)
            for a in range(2):
                ada_column(a, a, True)
            with pe.Fori(1, ADA0 // 2) as i:
                for s in range(2):
                    ada_column(2 * i + s, s)

            def up_pair(base, f, j, hid0, h0, with_ada, first):
                if first and j == 0:
                    split_ready(base + 1)
                    for k in range(KC):
                        pe.wait_ge(h_done, h0 + k + 1)
                        for half in range(2):
                            last = three(bank[2 * half][:], tile8(w_hi, half)[:, k, :], tile8(w_lo, half)[:, k, :],
                                         h_hi[:, k, :], h_lo[:, k, :], k == 0, k == KC - 1)
                            if k == KC - 1:
                                last.then_inc(w_used, 1)
                    if with_ada:
                        for s in range(2):
                            ada_column(ADA0 + s, s)
                    return
                for half in range(2):
                    split_ready(base + 2 * f + half)
                    if half == 0 and not first:
                        pe.wait_ge(hid_f32, hid0 + f - 1)
                    for k in range(KC):
                        last = three(bank[2 * half + j][:], tile8(w_hi, half)[:, k, :], tile8(w_lo, half)[:, k, :],
                                     h_hi[:, k, :], h_lo[:, k, :], k == 0, k == KC - 1)
                    last.then_inc(w_used, 1)
                    if with_ada:
                        ada_column(ADA0 + 2 * f + half, half)

            def ffn_up(base, hid0, h0, with_ada):
                for j in range(2):
                    up_pair(base, j, j, hid0, h0, with_ada, True)
                with pe.Fori(1, FC // 2) as i:
                    for j in range(2):
                        up_pair(base, 2 * i + j, j, hid0, h0, with_ada, False)

            ffn_up(T_UP1, 0, 0, True)

            pe.wait_ge(hid_done, FC)
            with pe.Fori(0, 2) as i:
                for j in range(4):
                    n = 4 * i + j
                    pe.wait_ge(x_upd, n + KC - 1)
                    for part, (k0, nk) in enumerate(DOWN_PARTS):
                        t = T_DOWN1 + 3 * j + part
                        split_ready(12 * i + t)
                        for k in range(nk):
                            last = three(bank[j % 2][:], tile8(w_hi, t % 2)[:, k, :], tile8(w_lo, t % 2)[:, k, :],
                                         hid_hi[:, k0 + k, :], hid_lo[:, k0 + k, :],
                                         part == 0 and k == 0, k0 + k == FC - 1)
                        last.then_inc(w_used, 1)
                        if (3 * j + part) % 2 == 0:
                            a = (3 * j + part) // 2
                            ada_column(6 * i + ADA0 + 2 * FC + a, a % 2)
            sum_squares(1)

            pe.wait_ge(wf_split, 1)
            pe.wait_ge(ada_out, NADA)
            for k in range(KC):
                pe.wait_ge(h_done, KC + k + 1)
                last = three(bank[5][:], wf_hi[:, k, :], wf_lo[:, k, :], h_hi[:, k, :], h_lo[:, k, :],
                             k == 0, k == KC - 1)
            last.then_inc(f_logit, 1)

            pe.wait_ge(f_act, 1)
            stats = 0
            last_on_bank = {}
            for step in STEPS:
                kind = step[0]
                if kind == "proj":
                    _, t, ci, half = step
                    what, n, b, first_tile = CHUNKS[ci]
                    if half == 0:
                        split_ready(t)
                        if t == first_tile:
                            used = [last_on_bank[x] for x in ((0, 1) if what == "v" else (b,)) if x in last_on_bank]
                            for prior in sorted(set(used)):
                                pe.wait_ge(*chunk_read(prior))
                            for x in ((0, 1) if what == "v" else (b,)):
                                last_on_bank[x] = ci
                    if what == "v":
                        part = t - first_tile
                        for kk in range(2 * half, 2 * half + 2):
                            k = 4 * part + kk
                            for tb in range(TB):
                                dst = bank[tb // 2][:, (tb % 2) * 256:(tb % 2) * 256 + 256]
                                last = three(dst, h_hi[:, k, tb * P:(tb + 1) * P], h_lo[:, k, tb * P:(tb + 1) * P],
                                             tile4(w_hi, t % 2)[:, kk, :], tile4(w_lo, t % 2)[:, kk, :],
                                             k == 0 and tb % 2 == 0, k == KC - 1, skip=True)
                    else:
                        for k in range(4 * half, 4 * half + 4):
                            last = three(bank[b][:], tile8(w_hi, t % 2)[:, k, :], tile8(w_lo, t % 2)[:, k, :],
                                         h_hi[:, k, :], h_lo[:, k, :], k == 0, k == KC - 1)
                    if half == 1:
                        last.then_inc(w_used, 1)
                elif kind == "scores":
                    _, j, u = step
                    unit = 5 * j + u
                    if u == 0:
                        if j < SBJ:
                            pe.wait_ge(qk_ready, 2 * j + 2)
                        else:
                            pe.wait_ge(nrm_lo, norm_of("k", j) + 1)
                    if unit >= 2:
                        pe.wait_ge(*z_read(unit - 2))
                    zb = bank[2 + unit % 2]
                    for h, i, c0 in UNITS[u]:
                        n = (i + 1) * P
                        rows = slice(h * HD, (h + 1) * HD)
                        q_h, q_l = (q[rows, j % 2, 0, i * P:(i + 1) * P] for q in (qk_hi, qk_lo))
                        k_h, k_l = (k[rows, j % 2, 1, 0:n] for k in (qk_hi, qk_lo))
                        three(zb[:, c0:c0 + n], q_h, q_l, k_h, k_l, True, False)
                        last = mm(zb[:, c0 + i * P:c0 + n], ident_bf[:], (mask_strict if j < SBJ else mask_causal)[:],
                                  start=False, stop=True)
                        if u == 2 and h == 0:
                            last.then_inc(even_scored, 1)
                            pe.wait_ge(even_scored, j + 1)
                    last.then_inc(s_done, 1)
                elif kind == "turn":
                    _, j, u = step
                    unit = 5 * j + u
                    if j < SBJ:
                        pe.wait_ge(p_ready_sb, unit + 1)
                    else:
                        pe.wait_ge(p_ready_fx, unit - 5 * SBJ + 1)
                    if unit >= 2:
                        pe.wait_ge(pt_ready, unit - 1)
                    for b in range(4):
                        last = nc.tensor.transpose(bank[4 + unit % 2][:, b * P:(b + 1) * P],
                                                   tmp_b[:, unit % 2, b * P:(b + 1) * P], ident[:])
                    last.then_inc(t_done, 1)
                elif kind == "values":
                    _, j, h = step
                    pe.wait_ge(pt_ready, 5 * j + (3 if h == 0 else 5))
                    pe.wait_ge(v_ready, 2 * (j // 2 + 1))
                    if j == 0 and h == 0:
                        pe.wait_ge(mix_zero, 5)
                    if h == 0 and j:
                        pe.wait_ge(nrm_f32, norm_of("o", j - 1) + 1)
                    slot, pl = (j // 2) % 2, j % 2
                    for kb in range(TB):
                        q0 = min(kb, 2)
                        blocks = slice(3 * kb + q0, 3 * kb + TB)
                        vh, vl = (v[:, slot, 2 * kb + pl, h:h + 2, :] for v in (v_hi, v_lo))
                        ph, pl_ = (p[:, h, blocks, :] for p in (pt_hi, pt_lo))
                        last = three(bank[6][:, q0 * P:], vh, vl, ph, pl_, h == 0 and kb == 0,
                                     h == 1 and kb == TB - 1)
                    last.then_inc(pv_done, 1)
                elif kind == "norm":
                    m = step[1]
                    pe.wait_ge(nsq_done, m + 1)
                    if stats:
                        pe.wait_ge(stat_read, stats)
                    mm(bank[7][:], pair_mean[:], ssum[:], start=True, stop=True).then_inc(stat_done, 1)
                    stats += 1
                elif kind == "decay":
                    _, j, h = step
                    if stats:
                        pe.wait_ge(stat_read, stats)
                    if j == SBJ and h == 0:
                        pe.wait_ge(f_dve, 4)
                    head = 2 * (j - SBJ) + h
                    mm(bank[7][:], rowsel[:, head:head + 1].broadcast_to([HD, P]), f_cum[:], start=True, stop=True)\
                        .then_inc(stat_done, 1)
                    stats += 1

            pe.wait_ge(nrm_lo, len(NORMS))
            with pe.Fori(0, KC // 4) as i:
                for j in range(4):
                    n = 4 * i + j
                    pe.wait_ge(x_upd, n + 2 * KC - 1)
                    split_ready(n + T_OUT)
                    for k in range(KC):
                        last = three(bank[j % 2][:], tile8(w_hi, j % 2)[:, k, :], tile8(w_lo, j % 2)[:, k, :],
                                     o_hi[:, k, :], o_lo[:, k, :], k == 0, k == KC - 1)
                    last.then_inc(w_used, 1)
            sum_squares(2)
            ffn_up(T_UP2, FC, 2 * KC, False)

            pe.wait_ge(hid_done, 2 * FC)
            pe.wait_ge(diag_done, KC)
            for k in range(KC):
                last = mm(bank[4 + k // 4][:, (k % 4) * P:(k % 4 + 1) * P], ones[:, 0:1].broadcast_to([P, P]),
                          diag[:, k, :], start=True, stop=True)
                if k % 4 == 3:
                    last.then_inc(row_done, 1)
            for n in range(2 * TB):
                if n >= 2:
                    pe.wait_ge(x2_copied, n - 1)
                for b in range(4):
                    last = nc.tensor.transpose(bank[6 + n % 2][:, b * P:(b + 1) * P],
                                               xT[:, 4 * (n % 2) + b, (n // 2) * P:(n // 2 + 1) * P], ident[:])
                last.then_inc(x2_turned, 1)
            with pe.Fori(0, 2) as i:
                for n, (k0, nk) in enumerate(NAT_PARTS):
                    split_ready(len(NAT_PARTS) * i + T_DOWN2 + n)
                    for tb in range(TB):
                        if n == 0:
                            pe.wait_ge(scaled, (tb + 1) * i + 1)
                        for k in range(nk):
                            last = three(bank[tb][:], hid_hi[:, k0 + k, tb * P:(tb + 1) * P],
                                         hid_lo[:, k0 + k, tb * P:(tb + 1) * P],
                                         tile2(w_hi, n % 2)[:, k, :], tile2(w_lo, n % 2)[:, k, :],
                                         k0 + k == 0, k0 + k == FC - 1)
                        if n == len(NAT_PARTS) - 1:
                            last.then_inc(out_acc, 1)
                    if n < len(NAT_PARTS) - 1:
                        last.then_inc(w_used, 1)

        @block.scalar
        def _(act):
            a = nc.scalar.activation

            def split_hi(t, slot=None, raw=None, gate_used=True):
                s = t % SPLIT if slot is None else slot
                r = t % RAW if raw is None else raw
                act.wait_ge(w_in_sem[r], turns(t, r))
                if gate_used:
                    act.wait_ge(*(tile_used(t - SPLIT) if isinstance(t, int) else (w_used, t - SPLIT + 1)))
                a(w_hi[:, s, :], w_raw[:, r, :], ACT.Copy).then_inc(w_hi_done, 1)

            def turns(t, r):
                return 4 * t + 16 - 4 * r

            act.wait_ge(vec_turned, 1)
            a(vcol[:], bank[6][:, 0:P], ACT.Copy).then_inc(vec_cols, 1)
            act.wait_ge(vec_cols, 1)
            a(cond[:], col(R_C, KC), ACT.Silu).then_inc(cond_ready, 1)
            nc.scalar.preload_act_table_set(EXP_LN_SET)
            for k in range(KC):
                act.wait_ge(x_turned, k + 1)
                a(xT[:, k, :], bank[k % 2][:], ACT.Copy).then_inc(x_upd, 1)
                act.wait_ge(x_upd, k + 1)
                if k >= 2:
                    act.wait_ge(sq_added, k - 1)
                a(tmp_a[:, k % 2, :], xT[:, k, :], ACT.Square).then_inc(sq_done, 1)

            def make_rstd(s):
                act.wait_ge(sum_done, s + 1)
                a(rstd[:], bank[6][:], ACT.Ln, bias=EPS, scale=1.0 / D).then_inc(ln_done, 1)
                act.wait_ge(ln_done, s + 1)
                a(rstd[:], rstd[:], ACT.Exp, scale=-0.5).then_inc(rstd_done, 1)

            def make_h(s):
                act.wait_ge(coef, s + 1)
                for k in range(KC):
                    n = KC * s + k
                    act.wait_ge(xn_done, n + 1)
                    if k >= 2:
                        act.wait_ge(h_done, n - 1)
                    a(tmp_b[:, k % 2, :], tmp_a[:, k % 2, :], ACT.Identity, scale=amp[:, k:k + 1],
                      bias=ada[:, 3 * KC * s + k:3 * KC * s + k + 1]).then_inc(h_full, 1)
                    act.wait_ge(h_full, n + 1)
                    a(h_hi[:, k, :], tmp_b[:, k % 2, :], ACT.Copy).then_inc(h_hi_done, 1)

            def ada_copy(n, slot):
                act.wait_ge(ada_col, n + 1)
                a(ada_raw[:, bass.ds(n, 1)], bank[4 + slot][:, 0:1], ACT.Copy).then_inc(ada_out, 1)

            make_rstd(0)
            for t in range(2):
                split_hi(t, gate_used=False)
            with act.Fori(0, ADA0 // 2) as i:
                for s in range(2):
                    ada_copy(2 * i + s, s)
            make_h(0)

            def up_chunk(base, f, j, hid0, with_ada):
                for half in range(2):
                    t = base + 2 * f + half
                    split_hi(t + SPLIT, half, (2 * j + half + SPLIT) % RAW)
                    if half == 0:
                        a(tmp_a[:, j, :], bank[j][:], ACT.Silu).then_inc(silu_done, 1)
                    if with_ada:
                        ada_copy(ADA0 + 2 * f + half, half)
                act.wait_ge(hid_f32, hid0 + f + 1)
                a(hid_hi[:, bass.ds(f, 1), :], tmp_b[:, j:j + 1, :], ACT.Copy).then_inc(hid_hi_done, 1)

            def ffn_up(base, hid0, with_ada):
                nc.scalar.preload_act_table_set("silu_and_others")
                for j in range(2):
                    up_chunk(base, j, j, hid0, with_ada)
                with act.Fori(1, FC // 2) as i:
                    for j in range(2):
                        up_chunk(base, 2 * i + j, j, hid0, with_ada)

            ffn_up(T_UP1, 0, True)

            with act.Fori(0, 2) as i:
                for j in range(4):
                    for part in range(3):
                        t = T_DOWN1 + 3 * j + part
                        split_hi(12 * i + t + SPLIT, (t + SPLIT) % SPLIT, (t + SPLIT) % RAW)
                        if (3 * j + part) % 2 == 0:
                            m = (3 * j + part) // 2
                            ada_copy(6 * i + ADA0 + 2 * FC + m, m % 2)
                    n = 4 * i + j
                    act.wait_ge(x_upd, n + KC + 1)
                    act.wait_ge(sq_added, n + KC - 1)
                    a(tmp_a[:, j % 2:j % 2 + 1, :], xT[:, bass.ds(n, 1), :], ACT.Square).then_inc(sq_done, 1)
            nc.scalar.preload_act_table_set(EXP_LN_SET)
            make_rstd(1)
            make_h(1)

            act.wait_ge(f_logit, 1)
            act.wait_ge(fbias_in, 16)
            f_z, f_e = ssum[0:JOBS, :], nrm[0:JOBS, :]
            a(f_z, bank[5][0:JOBS, :], ACT.Identity, bias=b_f[:]).then_inc(f_act, 1)
            act.wait_ge(f_act, 1)
            a(f_e, f_z, ACT.Abs).then_inc(f_act, 1)
            act.wait_ge(f_act, 2)
            a(f_e, f_e, ACT.Exp, scale=-1.0).then_inc(f_act, 1)
            act.wait_ge(f_act, 3)
            a(f_e, f_e, ACT.Ln, bias=1.0).then_inc(f_act, 1)
            act.wait_ge(f_dve, 3)
            a(f_cum[0:JOBS, :], f_e, ACT.Copy).then_inc(f_act, 1)

            stats = 0
            n_hi = 0
            gates = 0
            for step in STEPS:
                kind = step[0]
                if kind == "split":
                    split_hi(step[1])
                elif kind == "evac":
                    ci = step[1]
                    what, n, b, tile = CHUNKS[ci]
                    act.wait_ge(w_used, tile + (2 if what == "v" else 1))
                    if what == "v":
                        if n >= 2:
                            act.wait_ge(pv_done, 4 * n - 4)
                        for half in range(2):
                            a(v_hi[:, n % 2, 4 * half:4 * half + 4, 0:3:2, :],
                              bank[half][:].rearrange("p (t h d) -> p t h d", h=2, d=HD), ACT.Copy)\
                                .then_inc(chunk_hi, 1)
                            n_hi += 1
                    elif what == "g":
                        act.wait_ge(g_copy, gates + 1)
                        a(sig[:, n % 2, :], sig[:, n % 2, :], ACT.Exp, scale=-1.0).then_inc(g_exp, 1)
                        gates += 1
                    else:
                        if n >= 2:
                            act.wait_ge(s_done, 5 * (n - 1))
                        a(qk_hi[:, n % 2, int(what == "k"), :], bank[b][:], ACT.Copy,
                          scale=0.125 if what == "q" else 1.0).then_inc(chunk_hi, 1)
                        n_hi += 1
                elif kind == "square":
                    m = step[1]
                    what, n, ci = NORMS[m]
                    if what == "o":
                        act.wait_ge(pv_done, 2 * n + 2)
                    else:
                        act.wait_ge(w_used, CHUNKS[ci][3] + 1)
                    if m:
                        act.wait_ge(stat_done, stats)
                    else:
                        act.wait_ge(f_dve, 3)
                    a(ssum[:], bank[6 if what == "o" else CHUNKS[ci][2]][:], ACT.Square).then_inc(nsq_done, 1)
                elif kind == "norm":
                    m = step[1]
                    what, n, ci = NORMS[m]
                    stats += 1
                    act.wait_ge(stat_done, stats)
                    if m:
                        act.wait_ge(nrm_f32, m)
                    a(rstd[:], bank[7][:], ACT.Ln, bias=EPS).then_inc(stat_read, 1)
                    act.wait_ge(stat_read, stats)
                    a(rstd[:], rstd[:], ACT.Exp, scale=-0.5).then_inc(nrstd_done, 1)
                    if what == "o":
                        if n >= SBJ:
                            act.wait_ge(nrm_gated, n - SBJ + 1)
                        else:
                            act.wait_ge(nrm_f32, m + 1)
                        a(o_hi[:, n, :], nrm[:], ACT.Copy, scale=col(R_GO + n)).then_inc(nrm_hi, 1)
                    else:
                        act.wait_ge(nrm_f32, m + 1)
                        act.wait_ge(s_done, 5 * (n - 1))
                        a(qk_hi[:, n % 2, int(what == "k"), :], nrm[:], ACT.Copy,
                          scale=gq8[:] if what == "q" else col(R_GK)).then_inc(nrm_hi, 1)
                elif kind == "decay":
                    _, j, h = step
                    stats += 1
                    act.wait_ge(stat_done, stats)
                    if j > SBJ:
                        act.wait_ge(*z_read(5 * j - 1))
                    a(f_keys[:, h, :], bank[7][:], ACT.Copy).then_inc(stat_read, 1)
                elif kind == "weigh" and step[1] < SBJ:
                    unit = 5 * step[1] + step[2]
                    buf = tmp_a[:, unit % 2, :]
                    act.wait_ge(relu_done, unit + 1)
                    if unit >= 2:
                        act.wait_ge(scan_done, unit - 1)
                    a(buf, bank[2 + unit % 2][:], ACT.Abs).then_inc(abs_done, 1)
                    act.wait_ge(abs_done, unit + 1)
                    a(buf, buf, ACT.Exp, scale=-1.0).then_inc(eneg_done, 1)
                    act.wait_ge(eneg_done, unit + 1)
                    a(buf, buf, ACT.Ln, bias=1.0).then_inc(e_ready, 1)
                elif kind == "exp":
                    _, j, u = step
                    unit = 5 * j + u
                    buf = tmp_b[:, unit % 2, :]
                    if j < SBJ:
                        act.wait_ge(d_ready, unit + 1)
                        a(buf, buf, ACT.Exp).then_inc(p_ready_sb, 1)
                    else:
                        fx = unit - 5 * SBJ
                        act.wait_ge(zf_ready, fx + 1)
                        for s, (h, i, c0) in enumerate(UNITS[u]):
                            seg = buf[:, c0:c0 + (i + 1) * P]
                            last = a(seg, seg, ACT.Exp, bias=small[:, 4 * (unit % 2) + s:4 * (unit % 2) + s + 1],
                                     accum_out=small[:, 8 + 4 * (unit % 2) + s:9 + 4 * (unit % 2) + s])
                        last.then_inc(exp_done, 1)
                elif kind == "turn":
                    _, j, u = step
                    unit = 5 * j + u
                    act.wait_ge(t_done, unit + 1)
                    for h, dst, src in turned(u):
                        if j:
                            act.wait_ge(pv_done, 2 * (j - 1) + h + 1)
                        last = a(pt_hi[:, h, dst, :], blocks(bank[4 + unit % 2], src), ACT.Copy)
                    last.then_inc(pt_hi_done, 1)

            with act.Fori(0, KC // 4) as i:
                for j in range(4):
                    split_hi(4 * i + j + T_OUT + SPLIT, j % SPLIT, (j + SPLIT) % RAW)
                    n = 4 * i + j
                    act.wait_ge(x_upd, n + 2 * KC + 1)
                    act.wait_ge(sq_added, n + 2 * KC - 1)
                    a(tmp_a[:, j % 2:j % 2 + 1, :], xT[:, bass.ds(n, 1), :], ACT.Square).then_inc(sq_done, 1)
            make_rstd(2)
            make_h(2)
            ffn_up(T_UP2, FC, False)

            nc.scalar.preload_act_table_set(EXP_LN_SET)
            for h in range(2):
                act.wait_ge(row_done, h + 1)
                a(gate_row[:, h * 512:(h + 1) * 512], bank[4 + h][:], ACT.Copy).then_inc(row_copied, 1)
            for n in range(2 * TB):
                act.wait_ge(x2_turned, n + 1)
                a(x2_nat[:, n // 2, (n % 2) * 512:(n % 2) * 512 + 512], bank[6 + n % 2][:], ACT.Copy)\
                    .then_inc(x2_copied, 1)

            def square_out(i, tb):
                act.wait_ge(x3_done, TB * i + tb + 1)
                if TB * i + tb >= 2:
                    act.wait_ge(ssq_done, TB * i + tb - 1)
                a(tmp_b[:, tb % 2, :], x2_nat[:, tb, i * 512:(i + 1) * 512], ACT.Square,
                  accum_out=small[:, 16 + TB * i + tb:17 + TB * i + tb]).then_inc(ssq_done, 1)

            def down_tiles(i, parts):
                for n in parts:
                    t = T_DOWN2 + n + SPLIT
                    split_hi(len(NAT_PARTS) * i + t, t % SPLIT, t % RAW)

            down_tiles(0, range(len(NAT_PARTS) - 2))
            for part in (len(NAT_PARTS) - 2, len(NAT_PARTS) - 1):
                down_tiles(0, [part])
            for tb in range(TB):
                square_out(0, tb)
            down_tiles(1, range(len(NAT_PARTS) - 2))
            for tb in range(TB):
                square_out(1, tb)
                act.wait_ge(ms_done, tb + 1)
                a(small[:, 28 + tb:29 + tb], small[:, 24 + tb:25 + tb], ACT.Ln, bias=EPS, scale=1.0 / D)\
                    .then_inc(fln_done, 1)
                act.wait_ge(fln_done, tb + 1)
                a(small[:, 24 + tb:25 + tb], small[:, 28 + tb:29 + tb], ACT.Exp, scale=-0.5).then_inc(frstd_done, 1)

        @block.vector
        def _(dve):
            v = nc.vector

            def split_lo(t, slot=None, raw=None):
                s = t % SPLIT if slot is None else slot
                r = t % RAW if raw is None else raw
                dve.wait_ge(w_hi_done, t + 1)
                v.tensor_tensor(w_lo[:, s, :], w_raw[:, r, :], w_hi[:, s, :].bitcast(F32), ALU.subtract)\
                    .then_inc(w_lo_done, 1)

            def add_square(n, j):
                dve.wait_ge(sq_done, n + 1)
                dve.wait_ge(sq_added, n)
                v.tensor_tensor(ssum[:], ssum[:], tmp_a[:, j % 2, :], ALU.add).then_inc(sq_added, 1)

            dve.wait_ge(consts, N_CONSTS)
            v.tensor_copy(rowsel[:], rowsel_f[:]).then_inc(coef_dve, 1)
            dve.wait_ge(sq_done, 1)
            v.tensor_copy(ssum[:], tmp_a[:, 0, :]).then_inc(sq_added, 1)
            for k in range(1, KC):
                add_square(k, k)

            def ada_tile(n, slot, first=False):
                dve.wait_ge(ada_in[slot], 8 * n + 16 - 8 * slot)
                v.tensor_tensor(ada_w[:, slot, :, :], ada_w[:, slot, :, :],
                                cond[:].rearrange("p (k o) -> p k o", o=1).broadcast_to([P, KC, P]), ALU.mult)\
                    .then_inc(ada_prod, 1)
                dve.wait_ge(ada_prod, n + 1)
                if not first:
                    dve.wait_ge(ada_col, n - 1)
                v.tensor_reduce(ada_acc[:, slot, :], ada_w[:, slot, :, :].rearrange("p k n -> p n k"), AX_X, ALU.add)\
                    .then_inc(ada_red, 1)

            dve.wait_ge(cond_ready, 1)
            for n in range(2):
                ada_tile(n, n, True)
            for t in range(2):
                split_lo(t)
            with dve.Fori(1, ADA0 // 2) as i:
                for s in range(2):
                    ada_tile(2 * i + s, s)

            def coefficients(s, lo, hi):
                dve.wait_ge(ada_out, hi)
                v.tensor_tensor(ada[:, lo:hi], ada_raw[:, lo:hi], col(R_BADA + lo, hi - lo), ALU.add)\
                    .then_inc(coef_dve, 1)
                dve.wait_ge(coef_dve, 2 + s)
                if s:
                    dve.wait_ge(h_full, KC * s)
                v.scalar_tensor_tensor(amp[:], ada[:, (3 * s + 1) * KC:(3 * s + 2) * KC], 1.0, col(R_G[s], KC),
                                       ALU.add, ALU.mult).then_inc(coef, 1)

            def normed(s):
                dve.wait_ge(rstd_done, s + 1)
                for k in range(KC):
                    n = KC * s + k
                    if k >= 2:
                        dve.wait_ge(h_full, n - 1)
                    v.tensor_tensor(tmp_a[:, k % 2, :], xT[:, k, :], rstd[:], ALU.mult).then_inc(xn_done, 1)
                    if k:
                        h_low(n - 1)
                h_low(KC * s + KC - 1)

            def h_low(n):
                k = n % KC
                dve.wait_ge(h_hi_done, n + 1)
                v.tensor_tensor(h_lo[:, k, :], tmp_b[:, k % 2, :], h_hi[:, k, :].bitcast(F32), ALU.subtract)\
                    .then_inc(h_done, 1)

            coefficients(0, 0, ADA0)
            normed(0)
            for half in range(2):
                ada_tile(ADA0 + half, half)

            def up_chunk(base, f, j, hid0, with_ada, first, ada_done=False):
                for half in range(2):
                    if with_ada and not ada_done:
                        ada_tile(ADA0 + 2 * f + half, half)
                    split_lo(base + 2 * f + half + SPLIT, half, (2 * j + half + SPLIT) % RAW)
                dve.wait_ge(silu_done, hid0 + f + 1)
                dve.wait_ge(w_used, base + 2 * f + 2)
                if not first:
                    dve.wait_ge(hid_done, hid0 + f - 1)
                v.tensor_tensor(tmp_b[:, j, :], tmp_a[:, j, :], bank[2 + j][:], ALU.mult).then_inc(hid_f32, 1)
                dve.wait_ge(hid_hi_done, hid0 + f + 1)
                v.tensor_tensor(hid_lo[:, bass.ds(f, 1), :], tmp_b[:, j:j + 1, :],
                                hid_hi[:, bass.ds(f, 1), :].bitcast(F32), ALU.subtract).then_inc(hid_done, 1)

            def ffn_up(base, hid0, with_ada):
                for j in range(2):
                    up_chunk(base, j, j, hid0, with_ada, True, j == 0)
                with dve.Fori(1, FC // 2) as i:
                    for j in range(2):
                        up_chunk(base, 2 * i + j, j, hid0, with_ada, False)

            ffn_up(T_UP1, 0, True)

            dve.wait_ge(wf_in, 16)
            v.tensor_copy(wf_hi[:, :, 0:JOBS], wf_raw[:]).then_inc(wf_split_hi, 1)
            dve.wait_ge(wf_split_hi, 1)
            v.tensor_tensor(wf_lo[:, :, 0:JOBS], wf_raw[:], wf_hi[:, :, 0:JOBS].bitcast(F32), ALU.subtract)\
                .then_inc(wf_split, 1)
            g0 = 2 * KC
            dve.wait_ge(ada_out, g0 + KC)
            v.tensor_tensor(ada[:, g0:g0 + KC], ada_raw[:, g0:g0 + KC], col(R_BADA + g0, KC), ALU.add)\
                .then_inc(gacc_done, 1)
            dve.wait_ge(gacc_done, 1)
            v.tensor_scalar(gate[:], ada[:, g0:g0 + KC], 0.5, None, ALU.mult).then_inc(gacc_done, 1)
            v.memset(ssum[:], 0.0).then_inc(gacc_done, 1)
            dve.wait_ge(gacc_done, 3)

            with dve.Fori(0, 2) as i:
                for j in range(4):
                    n = 4 * i + j
                    for part in range(3):
                        t = T_DOWN1 + 3 * j + part
                        if (3 * j + part) % 2 == 0:
                            m = (3 * j + part) // 2
                            ada_tile(6 * i + ADA0 + 2 * FC + m, m % 2)
                        split_lo(12 * i + t + SPLIT, (t + SPLIT) % SPLIT, (t + SPLIT) % RAW)
                    dve.wait_ge(w_used, 12 * i + T_DOWN1 + 3 * j + 3)
                    v.scalar_tensor_tensor(xT[:, bass.ds(n, 1), :], bank[j % 2][:].rearrange("p (o s) -> p o s", o=1),
                                           gate[:, bass.ds(n, 1)], xT[:, bass.ds(n, 1), :], ALU.mult, ALU.add)\
                        .then_inc(x_upd, 1)
                    dve.wait_ge(sq_done, n + KC + 1)
                    dve.wait_ge(sq_added, n + KC)
                    v.tensor_tensor(ssum[:], ssum[:], tmp_a[:, j % 2, :], ALU.add).then_inc(sq_added, 1)
            coefficients(1, 3 * KC, 6 * KC)
            normed(1)

            dve.wait_ge(mix_zero, 5)
            dve.wait_ge(f_act, 4)
            f_z, f_e = ssum[0:JOBS, :], nrm[0:JOBS, :]
            v.tensor_scalar(f_z, f_z, 0.0, None, ALU.min).then_inc(f_dve, 1)
            dve.wait_ge(f_dve, 1)
            v.tensor_scalar(gq8[:], col(R_GQ), 0.125, None, ALU.mult).then_inc(f_dve, 1)
            v.tensor_tensor_scan(f_e, f_z, f_e, 0.0, ALU.add, ALU.subtract).then_inc(f_dve, 1)
            dve.wait_ge(f_dve, 3)
            dve.wait_ge(f_act, 5)
            v.tensor_tensor(f_cum[32:32 + JOBS, :], f_e, f_cum[0:JOBS, :].bitcast(F32), ALU.subtract)\
                .then_inc(f_dve, 1)

            n_hi, v_count, gates = 0, 0, 0
            for step in STEPS:
                kind = step[0]
                if kind == "split":
                    split_lo(step[1])
                elif kind == "evac":
                    ci = step[1]
                    what, n, b, tile = CHUNKS[ci]
                    if what == "v":
                        for half in range(2):
                            n_hi += 1
                            dve.wait_ge(chunk_hi, n_hi)
                            dst = (n % 2, slice(4 * half, 4 * half + 4), slice(0, 3, 2))
                            v.tensor_tensor(v_lo[:, dst[0], dst[1], dst[2], :],
                                            bank[half][:].rearrange("p (t h d) -> p t h d", h=2, d=HD),
                                            v_hi[:, dst[0], dst[1], dst[2], :].bitcast(F32), ALU.subtract)\
                                .then_inc(v_ready, 1)
                    elif what == "g":
                        dve.wait_ge(w_used, tile + 1)
                        if n >= SBJ + 2:
                            dve.wait_ge(nrm_gated, n - SBJ - 1)
                        v.tensor_copy(sig[:, n % 2, :], bank[b][:]).then_inc(g_copy, 1)
                        dve.wait_ge(g_copy, gates + 1)
                        dve.wait_ge(g_exp, gates + 1)
                        v.tensor_scalar(sig[:, n % 2, :], sig[:, n % 2, :], 1.0, None, ALU.add).then_inc(g_plus, 1)
                        dve.wait_ge(g_plus, gates + 1)
                        v.reciprocal(sig[:, n % 2, :], sig[:, n % 2, :]).then_inc(g_ready, 1)
                        gates += 1
                    else:
                        n_hi += 1
                        dve.wait_ge(chunk_hi, n_hi)
                        v.scalar_tensor_tensor(qk_lo[:, n % 2, int(what == "k"), :], bank[b][:],
                                               0.125 if what == "q" else 1.0,
                                               qk_hi[:, n % 2, int(what == "k"), :].bitcast(F32),
                                               ALU.mult, ALU.subtract).then_inc(qk_ready, 1)
                elif kind == "norm":
                    m = step[1]
                    what, n, ci = NORMS[m]
                    dve.wait_ge(nrstd_done, m + 1)
                    if m:
                        dve.wait_ge(nrm_lo, m)
                    else:
                        dve.wait_ge(f_dve, 4)
                    src = bank[6 if what == "o" else CHUNKS[ci][2]]
                    v.tensor_tensor(nrm[:], src[:], rstd[:], ALU.mult).then_inc(nrm_f32, 1)
                    dve.wait_ge(nrm_f32, m + 1)
                    if what == "o":
                        if n >= SBJ:
                            dve.wait_ge(g_ready, n - SBJ + 1)
                            v.tensor_tensor(nrm[:], nrm[:], sig[:, n % 2, :], ALU.mult).then_inc(nrm_gated, 1)
                            dve.wait_ge(nrm_gated, n - SBJ + 1)
                        dve.wait_ge(nrm_hi, m + 1)
                        v.scalar_tensor_tensor(o_lo[:, n, :], nrm[:], col(R_GO + n), o_hi[:, n, :].bitcast(F32),
                                               ALU.mult, ALU.subtract).then_inc(nrm_lo, 1)
                    else:
                        dve.wait_ge(nrm_hi, m + 1)
                        v.scalar_tensor_tensor(qk_lo[:, n % 2, int(what == "k"), :], nrm[:],
                                               gq8[:] if what == "q" else col(R_GK),
                                               qk_hi[:, n % 2, int(what == "k"), :].bitcast(F32),
                                               ALU.mult, ALU.subtract).then_inc(nrm_lo, 1)
                elif kind == "weigh":
                    _, j, u = step
                    unit = 5 * j + u
                    zb, buf = bank[2 + unit % 2], tmp_b[:, unit % 2, :]
                    dve.wait_ge(s_done, unit + 1)
                    if unit >= 2:
                        dve.wait_ge(t_done, unit - 1)
                    if j < SBJ:
                        v.tensor_scalar(buf, zb[:], 0.0, None, ALU.max).then_inc(relu_done, 1)
                        dve.wait_ge(relu_done, unit + 1)
                        dve.wait_ge(e_ready, unit + 1)
                        for h, i, c0 in UNITS[u]:
                            n = (i + 1) * P
                            back = slice(c0 + n - 1, c0 - 1 if c0 else None, -1)
                            last = v.tensor_tensor_scan(buf[:, back], tmp_a[:, unit % 2, back], buf[:, back],
                                                        0.0, ALU.add, ALU.add)
                        last.then_inc(scan_done, 1)
                        dve.wait_ge(scan_done, unit + 1)
                        v.tensor_tensor(buf, zb[:], buf, ALU.subtract).then_inc(d_ready, 1)
                    else:
                        fx = unit - 5 * SBJ
                        if u == 0:
                            dve.wait_ge(stat_read, stat_uses(("decay", j, 1)))
                        if fx >= 2:
                            dve.wait_ge(exp_done, fx - 1)
                        s0 = 4 * (unit % 2)
                        for s, (h, i, c0) in enumerate(UNITS[u]):
                            n = (i + 1) * P
                            last = v.tensor_tensor_reduce(
                                out=buf[:, c0:c0 + n], in0=zb[:, c0:c0 + n], in1=f_keys[:, h, 0:n], scale=1.0,
                                scalar=-3.0e38, op0=ALU.subtract, op1=ALU.max, accum_out=small[:, s0 + s:s0 + s + 1])
                        last.then_inc(max_done, 1)
                        dve.wait_ge(max_done, fx + 1)
                        ns = len(UNITS[u])
                        v.tensor_scalar(small[:, s0:s0 + ns], small[:, s0:s0 + ns], -1.0, None, ALU.mult)\
                            .then_inc(zf_ready, 1)
                elif kind == "exp" and step[1] >= SBJ:
                    _, j, u = step
                    unit = 5 * j + u
                    fx = unit - 5 * SBJ
                    buf, s0, ns = tmp_b[:, unit % 2, :], 8 + 4 * (unit % 2), len(UNITS[u])
                    dve.wait_ge(exp_done, fx + 1)
                    v.reciprocal(small[:, s0:s0 + ns], small[:, s0:s0 + ns]).then_inc(inv_done, 1)
                    dve.wait_ge(inv_done, fx + 1)
                    for s, (h, i, c0) in enumerate(UNITS[u]):
                        seg = buf[:, c0:c0 + (i + 1) * P]
                        last = v.tensor_scalar(seg, seg, small[:, s0 + s:s0 + s + 1], None, ALU.mult)
                    last.then_inc(p_ready_fx, 1)
                elif kind == "turn":
                    _, j, u = step
                    unit = 5 * j + u
                    dve.wait_ge(pt_hi_done, unit + 1)
                    for h, dst, src in turned(u):
                        last = v.tensor_tensor(pt_lo[:, h, dst, :], blocks(bank[4 + unit % 2], src),
                                               pt_hi[:, h, dst, :].bitcast(F32), ALU.subtract)
                    last.then_inc(pt_ready, 1)

            g1 = 5 * KC
            v.memset(ssum[:], 0.0).then_inc(gacc_done, 1)
            v.tensor_copy(gate[:], ada[:, g1:g1 + KC]).then_inc(gacc_done, 1)
            dve.wait_ge(gacc_done, 5)
            with dve.Fori(0, KC // 4) as i:
                for j in range(4):
                    n = 4 * i + j
                    split_lo(n + T_OUT + SPLIT, j % SPLIT, (j + SPLIT) % RAW)
                    dve.wait_ge(w_used, n + T_OUT + 1)
                    v.scalar_tensor_tensor(xT[:, bass.ds(n, 1), :], bank[j % 2][:].rearrange("p (o s) -> p o s", o=1),
                                           gate[:, bass.ds(n, 1)], xT[:, bass.ds(n, 1), :], ALU.mult, ALU.add)\
                        .then_inc(x_upd, 1)
                    dve.wait_ge(sq_done, n + 2 * KC + 1)
                    dve.wait_ge(sq_added, n + 2 * KC)
                    v.tensor_tensor(ssum[:], ssum[:], tmp_a[:, j % 2, :], ALU.add).then_inc(sq_added, 1)
            coefficients(2, 6 * KC, 9 * KC)
            normed(2)
            ffn_up(T_UP2, FC, False)

            g2 = 8 * KC
            v.tensor_scalar(gate[:], ada[:, g2:g2 + KC], 0.5, None, ALU.mult).then_inc(scaled, 1)
            dve.wait_ge(scaled, 1)
            dve.wait_ge(w_used, T_DOWN2)
            for k in range(KC):
                v.tensor_scalar(diag[:, k, :], ident[:], gate[:, k:k + 1], None, ALU.mult).then_inc(diag_done, 1)

            def finish(i, tb):
                dve.wait_ge(out_acc, TB * i + tb + 1)
                if i:
                    dve.wait_ge(x3_done, TB * i + tb - 1)
                elif tb >= 2:
                    dve.wait_ge(x3_done, tb - 1)
                v.tensor_tensor(tmp_a[:, tb % 2, :], bank[tb][:], gate_row[:, i * 512:(i + 1) * 512], ALU.mult)\
                    .then_inc(scaled, 1)
                dve.wait_ge(scaled, TB * i + tb + 2)
                half = x2_nat[:, tb, i * 512:(i + 1) * 512]
                v.tensor_tensor(half, tmp_a[:, tb % 2, :], half, ALU.add).then_inc(x3_done, 1)

            for n in range(len(NAT_PARTS) - 1):
                split_lo(T_DOWN2 + n + SPLIT)
            split_lo(T_DOWN2 + len(NAT_PARTS) + 1)
            dve.wait_ge(row_copied, 2)
            dve.wait_ge(x2_copied, 2 * TB)
            for tb in range(TB):
                finish(0, tb)
            for n in range(len(NAT_PARTS) - 2):
                split_lo(T_DOWN2 + len(NAT_PARTS) + n + SPLIT)
            dve.wait_ge(gfin_in, 32)
            for tb in range(TB):
                finish(1, tb)
                dve.wait_ge(ssq_done, TB + tb + 1)
                v.tensor_tensor(small[:, 24 + tb:25 + tb], small[:, 16 + tb:17 + tb], small[:, 20 + tb:21 + tb],
                                ALU.add).then_inc(ms_done, 1)
                dve.wait_ge(frstd_done, tb + 1)
                v.scalar_tensor_tensor(x2_nat[:, tb, :], x2_nat[:, tb, :], small[:, 24 + tb:25 + tb], gfin_row[:],
                                       ALU.mult, ALU.mult).then_inc(y_done, 1)


_INS = ["x", "c", "w_ada", "b_ada", "g_ffn1", "w_ffn1_up", "w_ffn1_down", "g_mix", "w_in", "b_forget", "g_fox_q",
        "g_fox_k", "g_sb_out", "g_fox_out", "w_out", "g_ffn2", "w_ffn2_up", "w_ffn2_down", "g_final"]
_OUTS = [((1, SEQ, D), "float32")]


def kernel(**inputs):
    import numpy as _np
    import concourse.bacc as _bacc
    from concourse import mybir as _mybir
    from concourse.bass_utils import run_bass_kernel_spmd as _run

    nc = _bacc.Bacc("TRN2", target_bir_lowering=False, num_devices=1)
    arrays, args = {}, []
    for name in _INS:
        a = _np.ascontiguousarray(inputs[name])
        arrays[f"in_{name}_dram"] = a
        args.append(nc.dram_tensor(f"in_{name}_dram", a.shape, _mybir.dt.from_np(a.dtype), kind="ExternalInput").ap())
    for i, (shape, dtype) in enumerate(_OUTS):
        dt = _mybir.dt.from_np(_np.dtype(dtype))
        args.append(nc.dram_tensor(f"out_{i}_dram", shape, dt, kind="ExternalOutput").ap())
    hybrid_block_kernel(nc, *args)
    r = _run(nc, [arrays], core_ids=[0])
    return r.results[0]["out_0_dram"]
```

```python
from contextlib import ExitStack

import concourse.bass as bass
from concourse import mybir

ALU = mybir.AluOpType
ACT = mybir.ActivationFunctionType
F32 = mybir.dt.float32
F32R = mybir.dt.float32r
BF16 = mybir.dt.bfloat16
AX_X = mybir.AxisListType.X
EXP_LN_SET = "natural_log_exp_and_others"

P = 128
SEQ = 512
TB = SEQ // P
D = 1024
KC = D // P
FFN = 2816
FC = FFN // P
HD = 64
JOBS = 8
SBJ = 4
EPS = 1e-6
N_IDENT, N_CONSTS = 2, 15
NEG = -(2.0 ** 126)
WS = 1024
DOWN_PARTS = ((0, 8), (8, 8), (16, 6))
NAT_PARTS = ((0, 2), (2, 2), (4, 1), (5, 1)) + tuple((k, 2) for k in range(6, 22, 2))
NADA = 9 * KC
ADA0 = 2 * KC
ADA_ROLE = "GDP" * 5 + "G"
ADA_SUMS = [p for p in range(ADA0) if ADA_ROLE[p] != "P"]

T_UP1 = 0
T_DOWN1 = T_UP1 + 2 * FC
T_MIX = T_DOWN1 + 3 * KC
N_MIX = 4 * 2 + 2 * JOBS + (JOBS - SBJ)
T_OUT = T_MIX + N_MIX
T_UP2 = T_OUT + KC
T_DOWN2 = T_UP2 + 2 * FC
N_TILES = T_DOWN2 + 2 * len(NAT_PARTS)
RAW = 4
SPLIT = 2

UNITS = (
    ((0, 3, 0),),
    ((0, 2, 0), (0, 0, 384)),
    ((0, 1, 0), (1, 1, 256)),
    ((1, 2, 0), (1, 0, 384)),
    ((1, 3, 0),),
)
PT_BLOCKS = 13
ZERO_BLOCK = 11


def chunks():
    order = [("v", 0), ("q", 0), ("k", 0)]
    order += [("q", 1), ("k", 1), ("v", 1), ("q", 2), ("k", 2), ("q", 3), ("k", 3), ("v", 2), ("q", 4), ("k", 4),
              ("g", 4), ("q", 5), ("k", 5), ("g", 5), ("q", 6), ("k", 6), ("v", 3), ("q", 7), ("k", 7), ("g", 6),
              ("g", 7)]
    out, tile = [], T_MIX
    for kind, n in order:
        out.append((kind, n, {"v": 0, "q": 0, "k": 1, "g": n % 2}[kind], tile))
        tile += 2 if kind == "v" else 1
    assert tile == T_MIX + N_MIX
    return out


CHUNKS = chunks()


PACE = 14
BEHIND = 3
LAG = 6


def mixer_steps():
    steps, norms, chains, evacs, splits = [], [], [], [], []
    array = {"proj": 12, "scores": 4, "values": 4, "turn": 2}
    spent, since = [0], {}

    def emit(*step):
        steps.append(step)
        spent[0] += array.get(step[0], 0)

    def banks_of(c):
        return (0, 1) if CHUNKS[c][0] == "v" else (CHUNKS[c][2],)

    def move(force=False):
        if not chains or (chains[0][0][0] == "stat" and not force and spent[0] - since["chain"] < LAG):
            return
        stage = chains[0].pop(0)
        emit(*stage)
        since["chain"] = spent[0]
        if stage[0] == "scale" and norms[stage[1]][2] is not None:
            for b in banks_of(norms[stage[1]][2]):
                since[b] = spent[0]
        if not chains[0]:
            chains.pop(0)

    def tick(force=False):
        if evacs:
            for b in banks_of(evacs[0][1]):
                since[b] = spent[0]
            emit(*evacs.pop(0))
        move(force)

    def head_norm(kind, n, chunk=None):
        m = len(norms)
        norms.append((kind, n, chunk))
        chains.append([("square", m), ("stat", m), ("scale", m), ("part", m)])

    queue = [(c, part, half) for c, chunk in enumerate(CHUNKS)
             for part in range(2 if chunk[0] == "v" else 1) for half in range(2)]
    at_start = 8
    total = len(queue)

    def unread():
        return ([c for _, c in evacs]
                + [norms[chain[0][1]][2] for chain in chains
                   if norms[chain[0][1]][2] is not None and chain[0][0] != "part"])

    def proj(force=True):
        c, part, half = queue[0]
        kind, n, _, tile = CHUNKS[c]
        if half == 0 and not force and spent[0] - since.get(("tile", tile + part), -LAG) < LAG:
            return False
        if part == half == 0:
            if not force and (any(set(banks_of(c)) & set(banks_of(x)) for x in unread())
                              or any(spent[0] - since.get(b, -LAG) < LAG for b in banks_of(c))):
                return False
            while any(set(banks_of(c)) & set(banks_of(x)) for x in unread()):
                tick(True)
        queue.pop(0)
        emit("proj", tile + part, c, half)
        if half == 1:
            splits.append(("split", tile + part + SPLIT))
            if kind != "v" or part == 1:
                if kind in "qk" and n >= SBJ:
                    head_norm(kind, n, c)
                else:
                    evacs.append(("evac", c))
        return True

    def made_first(j):
        return ([("evac", c) for c, chunk in enumerate(CHUNKS) if chunk[0] in "qk" and chunk[1] == j < SBJ]
                + [("part", m) for m, norm in enumerate(norms) if norm[0] in "qk" and norm[1] == j])

    def split():
        for step in splits:
            emit(*step)
            since["tile", step[1]] = spent[0]
        splits.clear()

    for _ in range(at_start):
        proj()
        split()
        tick(True)
    tick(True)

    units = [(j, u) for j in range(JOBS) for u in range(5)]
    for p, (j, u) in enumerate(units):
        before = units[p - 1] if p else None
        due = min(total, at_start + PACE * (p + 1) // 10)
        while u == 0 and any(step in made_first(j) for step in evacs + [chain[-1] for chain in chains]):
            tick(True)
        emit("scores", j, u)
        emit("prep", j, u)
        move()
        if total - len(queue) < due:
            proj(total - len(queue) < due - BEHIND)
        decays = u == 4 and SBJ <= j + 1 < JOBS
        if decays:
            emit("decay", j + 1, 0)
        if u == 1 and j:
            emit("values", j - 1, 1)
            head_norm("o", j - 1)
        elif u == 4:
            emit("values", j, 0)
        move()
        if before:
            emit("turn", *before)
        emit("sum", j, u)
        split()
        if before:
            emit("unload", *before)
        emit("exp", j, u)
        tick()
        while total - len(queue) < due and proj(False):
            split()
            tick()
        if decays:
            emit("decay", j + 1, 1)
    emit("turn", *units[-1])
    emit("unload", *units[-1])
    emit("values", JOBS - 1, 1)
    head_norm("o", JOBS - 1)
    while chains or evacs:
        tick(True)
    assert not queue
    return steps, norms


STEPS, NORMS = mixer_steps()


def hybrid_block_kernel(
    nc: bass.Bass, x, c, w_ada, b_ada, g_ffn1, w_ffn1_up, w_ffn1_down, g_mix, w_in, b_forget,
    g_fox_q, g_fox_k, g_sb_out, g_fox_out, w_out, g_ffn2, w_ffn2_up, w_ffn2_down, g_final, out,
):
    ctx = ExitStack()
    with ctx:
        def sem(name):
            return ctx.enter_context(nc.semaphore(name))

        slab = ctx.enter_context(nc.sbuf_tensor("slab", [P, 207 * 256], F32))
        top = [0]

        def size(shape, dt):
            n = 2 if dt == BF16 else 4
            for s in shape[1:]:
                n *= s
            return -(-n // 32) * 32

        def at(name, shape, dt, offset):
            return nc.alloc_sbuf_tensor_at(name, shape, dt, offset=slab_base + offset)

        def keep(name, shape, dt=F32):
            t = at(name, shape, dt, top[0])
            top[0] += size(shape, dt)
            return t

        slab_base = nc.sbuf_base - 207 * 1024

        xT = keep("xT", [P, KC, SEQ])
        w_raw = keep("w_raw", [P, RAW, WS])
        w_hi = keep("w_hi", [P, SPLIT, WS], F32R)
        w_lo = keep("w_lo", [P, SPLIT, WS], F32R)
        ident = keep("ident", [P, P])
        ident_bf = keep("ident_bf", [P, P], BF16)
        mask_strict = keep("mask_strict", [P, P], BF16)
        mask_causal = keep("mask_causal", [P, P], BF16)
        pair_mean = keep("pair_mean", [P, P])
        ones = keep("ones", [P, 1])
        rowsel_f = keep("rowsel_f", [HD, JOBS])
        rowsel = keep("rowsel", [HD, JOBS], F32R)
        vcol = keep("vcol", [P, P])
        ada = keep("ada", [P, NADA])
        amp = keep("amp", [P, KC])
        gate = keep("gate", [P, KC])
        cond = keep("cond", [P, KC])
        gq8 = keep("gq8", [P, 1])
        b_f = keep("b_f", [JOBS, 1])
        small = keep("small", [P, 32])
        tmp_a = keep("tmp_a", [P, 2, SEQ])
        tmp_b = keep("tmp_b", [P, 2, SEQ])
        ssum = keep("ssum", [P, SEQ])
        rstd = keep("rstd", [P, SEQ])
        h_offset = top[0]
        h_hi = keep("h_hi", [P, KC, SEQ], F32R)
        h_lo = keep("h_lo", [P, KC, SEQ], F32R)
        region = top[0]

        hid_hi = at("hid_hi", [P, FC, SEQ], F32R, region)
        hid_lo = at("hid_lo", [P, FC, SEQ], F32R, region + FC * SEQ * 4)
        ada_w = at("ada_w", [P, 2, KC, P], F32, region + 2 * FC * SEQ * 4)
        ada_acc = at("ada_acc", [P, 2, P], F32, region + 2 * FC * SEQ * 4 + 2 * D * 4)
        x_nat = at("x_nat", [P, TB, D], F32, region)
        vecs = at("vecs", [P, P], F32, region + TB * D * 4)
        ada_first = at("ada_first", [P, ADA0 - 4, KC, P], F32, region + TB * D * 4 + 512)
        w2_hi = at("w2_hi", [P, SPLIT, WS], F32R, region + TB * D * 4 + 512 + (ADA0 - 4) * D * 4)
        w2_lo = at("w2_lo", [P, SPLIT, WS], F32R, region + TB * D * 4 + 512 + (ADA0 - 2) * D * 4)
        assert TB * D * 4 + 512 + ADA0 * D * 4 <= 2 * FC * SEQ * 4
        x2_nat = at("x2_nat", [P, TB, D], F32, h_offset)
        gate_row = at("gate_row", [P, D], F32, h_offset + TB * D * 4)
        gfin_row = at("gfin_row", [P, D], F32, h_offset + (TB + 1) * D * 4)
        diag = at("diag", [P, KC, P], F32, h_offset + (TB + 2) * D * 4)

        top[0] = region
        v_hi = keep("v_hi", [P, 2, 2 * TB, 3, HD], F32R)
        v_lo = keep("v_lo", [P, 2, 2 * TB, 3, HD], F32R)
        qk_hi = keep("qk_hi", [P, 2, 2, SEQ], F32R)
        qk_lo = keep("qk_lo", [P, 2, 2, SEQ], F32R)
        pt_hi = keep("pt_hi", [P, 2, PT_BLOCKS, P], F32R)
        pt_lo = keep("pt_lo", [P, 2, PT_BLOCKS, P], F32R)
        o_hi = keep("o_hi", [P, JOBS, SEQ], F32R)
        o_lo = keep("o_lo", [P, JOBS, SEQ], F32R)
        beyond = top[0]
        f_keys = keep("f_keys", [P, 2, SEQ])
        f_cum = keep("f_cum", [HD, SEQ], F32R)
        sig = keep("sig", [P, 2, SEQ])
        nrm = keep("nrm", [P, SEQ])
        assert beyond >= region + 2 * FC * SEQ * 4 + 2 * D * 4 + 2 * P * 4
        wf_hi = at("wf_hi", [P, KC, P], F32R, beyond)
        wf_lo = at("wf_lo", [P, KC, P], F32R, beyond + 3 * SEQ * 4)
        wf_raw = at("wf_raw", [P, KC, JOBS], F32, beyond + 5 * SEQ * 4)
        assert top[0] <= 207 * 1024 and region + 2 * FC * SEQ * 4 + 2 * D * 4 + P * 8 <= 207 * 1024, top

        bank = [ctx.enter_context(nc.psum_tensor(f"bank{i}", [P, SEQ], F32)) for i in range(8)]

        wf_zero = sem("wf_zero")
        ada_first_in = [sem(f"ada_first_in{p}") for p in range(ADA0)]
        amp_done = sem("amp_done")
        sq_summed, rowsel_done = sem("sq_summed"), sem("rowsel_done")
        ada_prod_dve, ada_prod_pool = sem("ada_prod_dve"), sem("ada_prod_pool")
        vec_zero, vec_in, fbias_in, wf_in = sem("vec_zero"), sem("vec_in"), sem("fbias_in"), sem("wf_in")
        x_in = [sem("x_in0"), sem("x_in1")]
        w_in_sem = [sem(f"w_loaded{i}") for i in range(RAW)]
        ada_in = [sem("ada_loaded0"), sem("ada_loaded1")]
        gfin_in = sem("gfin_in")
        consts = sem("consts")
        w_hi_done, w_lo_done, w_used = sem("w_hi_done"), sem("w_lo_done"), sem("w_used")
        vec_turned, vec_cols = sem("vec_turned"), sem("vec_cols")
        cond_ready = sem("cond_ready")
        x_turned = sem("x_turned")
        x_upd, sq_done, sq_added = sem("x_upd"), sem("sq_done"), sem("sq_added")
        sum_done, ln_done, rstd_done = sem("sum_done"), sem("ln_done"), sem("rstd_done")
        xn_done, h_full, h_hi_done, h_done = sem("xn_done"), sem("h_full"), sem("h_hi_done"), sem("h_done")
        ada_red, ada_col, ada_out, coef = sem("ada_red"), sem("ada_col"), sem("ada_out"), sem("coef")
        silu_done, hid_f32, hid_hi_done, hid_done = (
            sem("silu_done"), sem("hid_f32"), sem("hid_hi_done"), sem("hid_done"))
        mix_zero = sem("mix_zero")
        wf_split, wf_split_hi, f_logit, f_act, f_dve = (
            sem("wf_split"), sem("wf_split_hi"), sem("f_logit"), sem("f_act"), sem("f_dve"))
        chunk_hi, qk_ready, v_ready = (
            sem("chunk_hi"), sem("qk_ready"), sem("v_ready"))
        g_copy, g_exp, g_ln, g_ready = sem("g_copy"), sem("g_exp"), sem("g_ln"), sem("g_ready")
        s_done, relu_done, abs_done, eneg_done, e_ready, scan_done, d_ready, p_ready_sb = (
            sem("s_done"), sem("relu_done"), sem("abs_done"), sem("eneg_done"), sem("e_ready"),
            sem("scan_done"), sem("d_ready"), sem("p_ready_sb"))
        even_scored = sem("even_scored")
        max_done, zf_ready, exp_done, inv_done, p_ready_fx = (
            sem("max_done"), sem("zf_ready"), sem("exp_done"), sem("inv_done"), sem("p_ready_fx"))
        t_done, pt_hi_done, pt_ready, pv_done = sem("t_done"), sem("pt_hi_done"), sem("pt_ready"), sem("pv_done")
        nsq_done, stat_done, stat_read, nrstd_done, nrm_f32, nrm_gated, nrm_hi, nrm_lo = (
            sem("nsq_done"), sem("stat_done"), sem("stat_read"), sem("nrstd_done"), sem("nrm_f32"),
            sem("nrm_gated"), sem("nrm_hi"), sem("nrm_lo"))
        fk_ready = sem("fk_ready")
        out_acc, gacc_done, diag_done, row_done, row_copied = (
            sem("out_acc"), sem("gacc_done"), sem("diag_done"), sem("row_done"), sem("row_copied"))
        x2_turned, x2_copied = sem("x2_turned"), sem("x2_copied")
        scaled, x3_done, ssq_done, ms_done, fln_done, frstd_done, y_done, stored = (
            sem("scaled"), sem("x3_done"), sem("ssq_done"), sem("ms_done"), sem("fln_done"), sem("frstd_done"),
            sem("y_done"), sem("stored"))

        up_v = [w.rearrange("o (k p) n -> (o p) k n", p=P) for w in (w_ffn1_up, w_ffn2_up)]
        down_v = [w.rearrange("o (k p) n -> (o p) k n", p=P) for w in (w_ffn1_down, w_ffn2_down)]
        in_v = w_in.rearrange("o (k p) n -> (o p) k n", p=P)
        out_v = w_out.rearrange("o (k p) n -> (o p) k n", p=P)
        ada_v = w_ada.rearrange("o (k p) n -> (o p) k n", p=P)

        def col(row, n=1):
            return vcol[:, row:row + n]

        R_BADA, R_G = 0, (NADA, NADA + KC, NADA + 2 * KC)
        R_GO = NADA + 3 * KC
        R_C = R_GO + JOBS
        R_GQ, R_GK = R_C + KC, R_C + KC + 1

        def tile8(buf, slot, k=KC):
            return buf[:, slot, 0:WS].rearrange("p (k n) -> p k n", k=KC)[:, 0:k, :]

        def tile4(buf, slot):
            return buf[:, slot, :].rearrange("p (k n) -> p k n", k=4)

        def tile2(buf, slot):
            return buf[:, slot, :].rearrange("p (k n) -> p k n", k=2)

        def turned(u):
            if u in (0, 4):
                return [(u // 4, slice(3, 13, 3), slice(0, 4))]
            if u in (1, 3):
                return [(u // 3, slice(2, 9, 3), slice(0, 3)), (u // 3, slice(0, 1), slice(3, 4))]
            return [(0, slice(1, 5, 3), slice(0, 2)), (1, slice(1, 5, 3), slice(2, 4))]

        def blocks(b, which):
            return b[:].rearrange("p (b n) -> p b n", n=P)[:, which, :]


        def stage(p):
            return ada_first[:, p - 2, :, :] if 2 <= p < ADA0 - 2 else ada_w[:, p % 2, :, :]

        def prods(role, p):
            return ADA_ROLE[:p + 1].count(role)

        def by_cond(engine, tile):
            return engine.tensor_tensor(tile, tile, cond[:].rearrange("p (k o) -> p k o", o=1)
                                        .broadcast_to([P, KC, P]), ALU.mult)

        def norm_of(what, j):
            return [n for n, e in enumerate(NORMS) if e[0:2] == (what, j)][0]

        def chunk_read(ci):
            what, n, _, _ = CHUNKS[ci]
            if what == "v":
                return v_ready, 2 * n + 2
            if what == "g":
                return g_copy, n - SBJ + 1
            if n < SBJ:
                return qk_ready, 2 * n + 1 + int(what == "k")
            return nrm_f32, norm_of(what, n) + 1

        def z_read(unit):
            return (d_ready, unit + 1) if unit < 5 * SBJ else (max_done, unit - 5 * SBJ + 1)

        def tile_used(t):
            half, n = divmod(t - T_DOWN2, len(NAT_PARTS))
            if half >= 0 and n == len(NAT_PARTS) - 1:
                return out_acc, TB * (half + 1)
            return w_used, t + 1 - max(half, 0)

        def stat_uses(until):
            n = 0
            for step in STEPS:
                n += step[0] in ("stat", "decay")
                if step == until:
                    return n

        block = ctx.enter_context(nc.Block())

        @block.gpsimd
        def _(pool):
            g = nc.gpsimd
            made = [0]

            def link(ins):
                made[0] += 1
                ins.then_inc(consts, 1)
                pool.wait_ge(consts, made[0])

            def select(buf, compare, fill, base, width):
                link(g.affine_select(out=buf[:], in_=buf[:], compare_op=compare, fill=fill, base=base,
                                     pattern=[[-1, width]], channel_multiplier=1))

            link(g.memset(ident[:], 0.0))
            select(ident, ALU.not_equal, 1.0, 0, P)
            for buf in (ident_bf, mask_strict, mask_causal, pair_mean, rowsel_f):
                link(g.memset(buf[:], 0.0))
            link(g.memset(ones[:], 1.0))
            select(ident_bf, ALU.not_equal, 1.0, 0, P)
            select(mask_strict, ALU.is_gt, NEG, 0, P)
            select(mask_causal, ALU.is_ge, NEG, 0, P)
            for h in range(2):
                link(g.memset(pair_mean[h * HD:(h + 1) * HD, h * HD:(h + 1) * HD], 1.0 / HD))
            for base in (0, -32):
                select(rowsel_f, ALU.not_equal, 1.0, base, JOBS)
            assert made[0] == N_CONSTS
            pool.wait_ge(cond_ready, 1)
            for p in range(ADA0):
                if ADA_ROLE[p] == "G":
                    pool.wait_ge(ada_first_in[p], 16)
                    by_cond(g, stage(p)).then_inc(ada_prod_pool, 1)
                    pool.wait_ge(ada_prod_pool, prods("G", p))
                if p in (4, 6, 10, 12):
                    t = (4, 6, 10, 12).index(p)
                    pool.wait_ge(w_hi_done, t + 1)
                    hi, lo = (w_hi, w_lo) if t < SPLIT else (w2_hi, w2_lo)
                    g.tensor_tensor(lo[:, t % SPLIT, :], w_raw[:, t, :], hi[:, t % SPLIT, :].bitcast(F32),
                                    ALU.subtract).then_inc(w_lo_done, 1)
                    pool.wait_ge(w_lo_done, t + 1)

            def ada_tile(n, slot):
                pool.wait_ge(ada_in[slot], 8 * n + 16 - 8 * slot - 8 * ADA0)
                by_cond(g, ada_w[:, slot, :, :]).then_inc(ada_prod_pool, 1)
                pool.wait_ge(ada_prod_pool, n + 1 - ADA0 + ADA_ROLE.count("G"))

            with pool.Fori(0, (NADA - ADA0) // 2) as i:
                for slot in range(2):
                    ada_tile(2 * i + ADA0 + slot, slot)
            pool.wait_ge(w_used, T_MIX)
            for n, part in enumerate((v_hi[:, :, :, 1, :], v_lo[:, :, :, 1, :], pt_hi[:, :, ZERO_BLOCK, :],
                                      pt_lo[:, :, ZERO_BLOCK, :], f_cum[:])):
                g.memset(part.bitcast(F32), 0.0).then_inc(mix_zero, 1)
                pool.wait_ge(mix_zero, n + 1)

        @block.sync
        def _(sp):
            def load_w(t, slot, dst, src, first=False):
                if not first:
                    sp.wait_ge(w_lo_done, t - RAW + 1)
                sp.dma_start(dst, src).then_inc(w_in_sem[slot], 16)

            def load_up(ffn, base, f, j, first=False):
                for half in range(2):
                    load_w(base + 2 * f + half, 2 * j + half, tile8(w_raw, 2 * j + half),
                           up_v[ffn][:, :, bass.ds(f * P + half * FFN, P)], first)

            def load_ada(a, slot):
                sp.wait_ge(ada_red, a - ADA0 + len(ADA_SUMS) - 1)
                sp.dma_start(ada_w[:, slot, :, :], ada_v[:, :, bass.ds(a * P, P)]).then_inc(ada_in[slot], 16)

            def load_ada_first(p):
                if p >= ADA0 - 2:
                    sp.wait_ge(ada_red, p - ADA0 + 3)
                a = p // 2 + KC * (p % 2)
                sp.dma_start(stage(p), ada_v[:, :, a * P:(a + 1) * P]).then_inc(ada_first_in[p], 16)

            def load_x(half):
                sp.dma_start(x_nat[:, :, half * 512:(half + 1) * 512],
                             x.rearrange("o (t p) d -> (o p) t d", p=P)[:, :, half * 512:(half + 1) * 512])\
                  .then_inc(x_in[half], 16)

            load_x(0)
            sp.wait_ge(vec_zero, 1)
            n = 0
            for src, row, rows in ((b_ada, R_BADA, NADA), (g_ffn1, R_G[0], KC), (g_mix, R_G[1], KC),
                                   (g_ffn2, R_G[2], KC), (g_sb_out, R_GO, SBJ), (g_fox_out, R_GO + SBJ, SBJ),
                                   (c, R_C, KC)):
                sp.dma_start(vecs[row:row + rows, :], src.rearrange("o (r p) -> (o r) p", p=P)).then_inc(vec_in, 16)
                n += 1
            for src, row in ((g_fox_q, R_GQ), (g_fox_k, R_GK)):
                for h in range(2):
                    sp.dma_start(vecs[row:row + 1, h * HD:(h + 1) * HD], src).then_inc(vec_in, 16)
                    n += 1
            assert n == 11
            load_x(1)
            for p in range(ADA0):
                load_ada_first(p)
                if p in (3, 7):
                    load_up(0, T_UP1, p // 4, p // 4, True)
            sp.dma_start(b_f[:], b_forget.rearrange("o h -> h o")).then_inc(fbias_in, 16)
            sp.dma_start(wf_raw[:], in_v[:, :, 7 * 512:7 * 512 + JOBS]).then_inc(wf_in, 16)
            sp.wait_ge(ada_col, ADA0 - 1)
            for s in range(2):
                load_ada(ADA0 + s, s)
            with sp.Fori(1, FC // 2) as i:
                for j in range(2):
                    load_up(0, T_UP1, 2 * i + j, j)
                    for s in range(2):
                        load_ada(ADA0 + 4 * i + 2 * j + s - 2, s)
            for s in range(2):
                load_ada(ADA0 + 2 * FC + s - 2, s)
            with sp.Fori(0, 2) as i:
                for j in range(4):
                    for part, (k0, nk) in enumerate(DOWN_PARTS):
                        t = T_DOWN1 + 3 * j + part
                        load_w(12 * i + t, t % RAW, tile8(w_raw, t % RAW, nk),
                               down_v[0][:, k0:k0 + nk, bass.ds((4 * i + j) * P, P)])
                        if (3 * j + part) % 2 == 0:
                            a = (3 * j + part) // 2
                            load_ada(6 * i + ADA0 + 2 * FC + a, a % 2)
            for kind, n, _, tile in CHUNKS:
                if kind == "v":
                    c0 = (2 if n < 2 else 5) * 512 + (n % 2) * 256
                    for part in range(2):
                        t = tile + part
                        load_w(t, t % RAW, tile4(w_raw, t % RAW), in_v[:, 4 * part:4 * part + 4, c0:c0 + 256])
                else:
                    c0 = (3 * 512 if n >= SBJ else 0) + (n % SBJ) * P + {"q": 0, "k": 512, "g": 3 * 512}[kind]
                    load_w(tile, tile % RAW, tile8(w_raw, tile % RAW), in_v[:, :, c0:c0 + P])
            with sp.Fori(0, KC // RAW) as i:
                for j in range(RAW):
                    load_w(T_OUT + RAW * i + j, j, tile8(w_raw, j), out_v[:, :, bass.ds((RAW * i + j) * P, P)])
            with sp.Fori(0, FC // 2) as i:
                for j in range(2):
                    load_up(1, T_UP2, 2 * i + j, j)
            with sp.Fori(0, 2) as i:
                for n, (k0, nk) in enumerate(NAT_PARTS):
                    load_w(len(NAT_PARTS) * i + T_DOWN2 + n, n % RAW, tile2(w_raw, n % RAW)[:, 0:nk, :],
                           down_v[1][:, k0:k0 + nk, bass.ds(i * 512, 512)])
                    if n == RAW - 1:
                        sp.wait_ge(w_used, T_DOWN2)
                        sp.dma_start(gfin_row[:, bass.ds(i * 512, 512)],
                                     g_final[bass.ds(i * 512, 512)].partition_broadcast(P)).then_inc(gfin_in, 16)
            for t in range(TB):
                sp.wait_ge(y_done, t + 1)
                sp.dma_start(out[0, t * P:(t + 1) * P, :], x2_nat[:, t, :]).then_inc(stored, 16)
            sp.wait_ge(stored, 16 * TB)

        @block.tensor
        def _(pe):
            mm = nc.tensor.matmul

            def three(dst, wh, wl, xh, xl, start, stop, skip=False):
                mm(dst, wh, xh, start=start, stop=False, skip_group_check=skip)
                mm(dst, wh, xl, start=False, stop=False, skip_group_check=skip)
                return mm(dst, wl, xh, start=False, stop=stop, skip_group_check=skip)

            def split_ready(t):
                pe.wait_ge(w_lo_done, t + 1)

            pe.wait_ge(consts, N_IDENT)
            pe.wait_ge(vec_in, 16 * 11)
            nc.tensor.transpose(bank[7][:, 0:P], vecs[:], ident[:]).then_inc(vec_turned, 1)
            pe.wait_ge(consts, N_CONSTS)
            for k in range(KC + 1):
                if k < KC:
                    if k % 4 == 0:
                        pe.wait_ge(x_in[k // 4], 16)
                    if k >= 2:
                        pe.wait_ge(x_upd, k - 1)
                    for t in range(TB):
                        last = nc.tensor.transpose(bank[k % 2][:, t * P:(t + 1) * P],
                                                   x_nat[:, t, k * P:(k + 1) * P], ident[:])
                    last.then_inc(x_turned, 1)
                if k:
                    pe.wait_ge(sq_done, k)
                    mm(bank[6][:], ones[:, 0:1].broadcast_to([P, P]), tmp_a[:, (k - 1) % 2, :], start=k == 1,
                       stop=k == KC).then_inc(sq_summed, 1)

            def sum_squares(s):
                pe.wait_ge(sq_added, (KC + 1) * s)
                mm(bank[6][:], ones[:, 0:1].broadcast_to([P, P]), ssum[:], start=True, stop=True).then_inc(sum_done, 1)

            def ada_column_first(p):
                b = bank[4 + (p // 2) % 2][:, p % 2:p % 2 + 1]
                if p >= 4 and p % 2 == 0:
                    pe.wait_ge(ada_out, p - 2)
                if ADA_ROLE[p] == "P":
                    pe.wait_ge(ada_first_in[p], 16)
                    for k in range(KC):
                        last = mm(b, stage(p)[:, k, :], cond[:, k:k + 1], start=k == 0, stop=k == KC - 1)
                else:
                    n = ADA_SUMS.index(p)
                    pe.wait_ge(ada_red, n + 1)
                    last = mm(b, ada_acc[:, n % 2, :], ones[:], start=True, stop=True)
                last.then_inc(ada_col, 1)

            def ada_column(a, slot, bank_read=True):
                pe.wait_ge(ada_red, a + len(ADA_SUMS) - ADA0 + 1)
                if bank_read:
                    pe.wait_ge(ada_out, a - 1)
                mm(bank[4 + slot][:, 0:1], ada_acc[:, (slot + len(ADA_SUMS)) % 2, :], ones[:], start=True, stop=True)\
                    .then_inc(ada_col, 1)

            pe.wait_ge(cond_ready, 1)
            for p in range(8):
                ada_column_first(p)
            split_ready(3)
            for k in range(KC):
                if k >= 1 and 2 * k + 7 < ADA0:
                    ada_column_first(2 * k + 6)
                    ada_column_first(2 * k + 7)
                pe.wait_ge(h_done, k + 1)
                for n in range(4):
                    hi, lo = (w_hi, w_lo) if n < SPLIT else (w2_hi, w2_lo)
                    last = three(bank[2 * (n % 2) + n // 2][:], tile8(hi, n % 2)[:, k, :], tile8(lo, n % 2)[:, k, :],
                                 h_hi[:, k, :], h_lo[:, k, :], k == 0, k == KC - 1)
                    if k == KC - 1:
                        last.then_inc(w_used, 1)

            def up_pair(base, f, j, hid0, with_ada, first=False):
                for half in range(2):
                    split_ready(base + 2 * f + half)
                    if half == 0 and not first:
                        pe.wait_ge(hid_f32, hid0 + f - 1)
                    for k in range(KC):
                        last = three(bank[2 * half + j][:], tile8(w_hi, half)[:, k, :], tile8(w_lo, half)[:, k, :],
                                     h_hi[:, k, :], h_lo[:, k, :], k == 0, k == KC - 1)
                    last.then_inc(w_used, 1)
                    if with_ada:
                        ada_column(ADA0 + 2 * f + half - 1, 1 - half)

            for s in range(3):
                ada_column(ADA0 + s, s % 2)
            with pe.Fori(1, FC // 2) as i:
                for j in range(2):
                    up_pair(T_UP1, 2 * i + j, j, 0, True)

            pe.wait_ge(hid_done, FC)
            with pe.Fori(0, 2) as i:
                for j in range(4):
                    n = 4 * i + j
                    pe.wait_ge(x_upd, n + KC - 1)
                    for part, (k0, nk) in enumerate(DOWN_PARTS):
                        t = T_DOWN1 + 3 * j + part
                        split_ready(12 * i + t)
                        for k in range(nk):
                            last = three(bank[j % 2][:], tile8(w_hi, t % 2)[:, k, :], tile8(w_lo, t % 2)[:, k, :],
                                         hid_hi[:, k0 + k, :], hid_lo[:, k0 + k, :],
                                         part == 0 and k == 0, k0 + k == FC - 1)
                        last.then_inc(w_used, 1)
                        if (3 * j + part) % 2 == 0:
                            a = (3 * j + part) // 2
                            ada_column(6 * i + ADA0 + 2 * FC + a - 1, (a - 1) % 2)
            sum_squares(1)
            ada_column(NADA - 1, 1)

            pe.wait_ge(wf_split, 1)
            pe.wait_ge(ada_out, NADA)
            for k in range(KC):
                pe.wait_ge(h_done, KC + k + 1)
                last = three(bank[5][:], wf_hi[:, k, :], wf_lo[:, k, :], h_hi[:, k, :], h_lo[:, k, :],
                             k == 0, k == KC - 1)
            last.then_inc(f_logit, 1)

            pe.wait_ge(f_act, 1)
            stats = 0
            last_on_bank = {}
            for step in STEPS:
                kind = step[0]
                if kind == "proj":
                    _, t, ci, half = step
                    what, n, b, first_tile = CHUNKS[ci]
                    if half == 0:
                        split_ready(t)
                        if t == first_tile:
                            used = [last_on_bank[x] for x in ((0, 1) if what == "v" else (b,)) if x in last_on_bank]
                            for prior in sorted(set(used)):
                                pe.wait_ge(*chunk_read(prior))
                            for x in ((0, 1) if what == "v" else (b,)):
                                last_on_bank[x] = ci
                    if what == "v":
                        part = t - first_tile
                        for kk in range(2 * half, 2 * half + 2):
                            k = 4 * part + kk
                            for tb in range(TB):
                                dst = bank[tb // 2][:, (tb % 2) * 256:(tb % 2) * 256 + 256]
                                last = three(dst, h_hi[:, k, tb * P:(tb + 1) * P], h_lo[:, k, tb * P:(tb + 1) * P],
                                             tile4(w_hi, t % 2)[:, kk, :], tile4(w_lo, t % 2)[:, kk, :],
                                             k == 0 and tb % 2 == 0, k == KC - 1, skip=True)
                    else:
                        for k in range(4 * half, 4 * half + 4):
                            last = three(bank[b][:], tile8(w_hi, t % 2)[:, k, :], tile8(w_lo, t % 2)[:, k, :],
                                         h_hi[:, k, :], h_lo[:, k, :], k == 0, k == KC - 1)
                    if half == 1:
                        last.then_inc(w_used, 1)
                elif kind == "scores":
                    _, j, u = step
                    unit = 5 * j + u
                    if u == 0:
                        if j < SBJ:
                            pe.wait_ge(qk_ready, 2 * j + 2)
                        else:
                            pe.wait_ge(nrm_lo, norm_of("k", j) + 1)
                    if unit >= 2:
                        pe.wait_ge(*z_read(unit - 2))
                    zb = bank[2 + unit % 2]
                    for h, i, c0 in UNITS[u]:
                        n = (i + 1) * P
                        rows = slice(h * HD, (h + 1) * HD)
                        q_h, q_l = (q[rows, j % 2, 0, i * P:(i + 1) * P] for q in (qk_hi, qk_lo))
                        k_h, k_l = (k[rows, j % 2, 1, 0:n] for k in (qk_hi, qk_lo))
                        three(zb[:, c0:c0 + n], q_h, q_l, k_h, k_l, True, False)
                        last = mm(zb[:, c0 + i * P:c0 + n], ident_bf[:], (mask_strict if j < SBJ else mask_causal)[:],
                                  start=False, stop=True)
                        if u == 2 and h == 0:
                            last.then_inc(even_scored, 1)
                            pe.wait_ge(even_scored, j + 1)
                    last.then_inc(s_done, 1)
                elif kind == "turn":
                    _, j, u = step
                    unit = 5 * j + u
                    if j < SBJ:
                        pe.wait_ge(p_ready_sb, unit + 1)
                    else:
                        pe.wait_ge(p_ready_fx, unit - 5 * SBJ + 1)
                    if unit >= 2:
                        pe.wait_ge(pt_ready, unit - 1)
                    for b in range(4):
                        last = nc.tensor.transpose(bank[4 + unit % 2][:, b * P:(b + 1) * P],
                                                   tmp_b[:, unit % 2, b * P:(b + 1) * P], ident[:])
                    last.then_inc(t_done, 1)
                elif kind == "values":
                    _, j, h = step
                    pe.wait_ge(pt_ready, 5 * j + (3 if h == 0 else 5))
                    pe.wait_ge(v_ready, 2 * (j // 2 + 1))
                    if j == 0 and h == 0:
                        pe.wait_ge(mix_zero, 5)
                    if h == 0 and j:
                        pe.wait_ge(nrm_f32, norm_of("o", j - 1) + 1)
                    slot, pl = (j // 2) % 2, j % 2
                    for kb in range(TB):
                        q0 = min(kb, 2)
                        blocks = slice(3 * kb + q0, 3 * kb + TB)
                        vh, vl = (v[:, slot, 2 * kb + pl, h:h + 2, :] for v in (v_hi, v_lo))
                        ph, pl_ = (p[:, h, blocks, :] for p in (pt_hi, pt_lo))
                        last = three(bank[6][:, q0 * P:], vh, vl, ph, pl_, h == 0 and kb == 0,
                                     h == 1 and kb == TB - 1)
                    last.then_inc(pv_done, 1)
                elif kind == "stat":
                    m = step[1]
                    pe.wait_ge(nsq_done, m + 1)
                    if stats:
                        pe.wait_ge(stat_read, stats)
                    mm(bank[7][:], pair_mean[:], ssum[:], start=True, stop=True).then_inc(stat_done, 1)
                    stats += 1
                elif kind == "decay":
                    _, j, h = step
                    if stats:
                        pe.wait_ge(stat_read, stats)
                    if j == SBJ and h == 0:
                        pe.wait_ge(f_dve, 4)
                    head = 2 * (j - SBJ) + h
                    mm(bank[7][:], rowsel[:, head:head + 1].broadcast_to([HD, P]), f_cum[:], start=True, stop=True)\
                        .then_inc(stat_done, 1)
                    stats += 1

            pe.wait_ge(nrm_lo, len(NORMS))
            with pe.Fori(0, KC // 4) as i:
                for j in range(4):
                    n = 4 * i + j
                    pe.wait_ge(x_upd, n + 2 * KC - 1)
                    split_ready(n + T_OUT)
                    for k in range(KC):
                        last = three(bank[j % 2][:], tile8(w_hi, j % 2)[:, k, :], tile8(w_lo, j % 2)[:, k, :],
                                     o_hi[:, k, :], o_lo[:, k, :], k == 0, k == KC - 1)
                    last.then_inc(w_used, 1)
            sum_squares(2)
            split_ready(T_UP2 + 1)
            for k in range(KC):
                pe.wait_ge(h_done, 2 * KC + k + 1)
                for half in range(2):
                    last = three(bank[2 * half][:], tile8(w_hi, half)[:, k, :], tile8(w_lo, half)[:, k, :],
                                 h_hi[:, k, :], h_lo[:, k, :], k == 0, k == KC - 1)
                    if k == KC - 1:
                        last.then_inc(w_used, 1)
            up_pair(T_UP2, 1, 1, FC, False, True)
            with pe.Fori(1, FC // 2) as i:
                for j in range(2):
                    up_pair(T_UP2, 2 * i + j, j, FC, False)

            pe.wait_ge(hid_done, 2 * FC)
            pe.wait_ge(diag_done, KC)
            for k in range(KC):
                last = mm(bank[4 + k // 4][:, (k % 4) * P:(k % 4 + 1) * P], ones[:, 0:1].broadcast_to([P, P]),
                          diag[:, k, :], start=True, stop=True)
                if k % 4 == 3:
                    last.then_inc(row_done, 1)
            for n in range(2 * TB):
                if n >= 2:
                    pe.wait_ge(x2_copied, n - 1)
                for b in range(4):
                    last = nc.tensor.transpose(bank[6 + n % 2][:, b * P:(b + 1) * P],
                                               xT[:, 4 * (n % 2) + b, (n // 2) * P:(n // 2 + 1) * P], ident[:])
                last.then_inc(x2_turned, 1)
            with pe.Fori(0, 2) as i:
                for n, (k0, nk) in enumerate(NAT_PARTS):
                    split_ready(len(NAT_PARTS) * i + T_DOWN2 + n)
                    for tb in range(TB):
                        if n == 0:
                            pe.wait_ge(scaled, (tb + 1) * i + 1)
                        for k in range(nk):
                            last = three(bank[tb][:], hid_hi[:, k0 + k, tb * P:(tb + 1) * P],
                                         hid_lo[:, k0 + k, tb * P:(tb + 1) * P],
                                         tile2(w_hi, n % 2)[:, k, :], tile2(w_lo, n % 2)[:, k, :],
                                         k0 + k == 0, k0 + k == FC - 1)
                        if n == len(NAT_PARTS) - 1:
                            last.then_inc(out_acc, 1)
                    if n < len(NAT_PARTS) - 1:
                        last.then_inc(w_used, 1)

        @block.scalar
        def _(act):
            a = nc.scalar.activation

            def split_hi(t, slot=None, raw=None, gate_used=True):
                s = t % SPLIT if slot is None else slot
                r = t % RAW if raw is None else raw
                act.wait_ge(w_in_sem[r], turns(t, r))
                if gate_used:
                    act.wait_ge(*(tile_used(t - SPLIT) if isinstance(t, int) else (w_used, t - SPLIT + 1)))
                a(w_hi[:, s, :], w_raw[:, r, :], ACT.Copy).then_inc(w_hi_done, 1)

            def turns(t, r):
                return 4 * t + 16 - 4 * r

            act.wait_ge(vec_turned, 1)
            a(vcol[:], bank[7][:, 0:P], ACT.Copy).then_inc(vec_cols, 1)
            act.wait_ge(vec_cols, 1)
            a(cond[:], col(R_C, KC), ACT.Silu).then_inc(cond_ready, 1)
            nc.scalar.preload_act_table_set(EXP_LN_SET)
            for k in range(KC):
                act.wait_ge(x_turned, k + 1)
                a(xT[:, k, :], bank[k % 2][:], ACT.Copy).then_inc(x_upd, 1)
                act.wait_ge(x_upd, k + 1)
                if k >= 2:
                    act.wait_ge(sq_summed, k - 1)
                a(tmp_a[:, k % 2, :], xT[:, k, :], ACT.Square).then_inc(sq_done, 1)

            def make_rstd(s):
                if s:
                    act.wait_ge(sum_done, s)
                else:
                    act.wait_ge(sq_summed, KC)
                a(rstd[:], bank[6][:], ACT.Ln, bias=EPS, scale=1.0 / D).then_inc(ln_done, 1)
                act.wait_ge(ln_done, s + 1)
                a(rstd[:], rstd[:], ACT.Exp, scale=-0.5).then_inc(rstd_done, 1)

            def make_h_chunk(s, k):
                n = KC * s + k
                act.wait_ge(xn_done, n + 1)
                if k >= 2:
                    act.wait_ge(h_done, n - 1)
                a(tmp_b[:, k % 2, :], tmp_a[:, k % 2, :], ACT.Identity, scale=amp[:, k:k + 1],
                  bias=ada[:, 3 * KC * s + k:3 * KC * s + k + 1]).then_inc(h_full, 1)
                act.wait_ge(h_full, n + 1)
                a(h_hi[:, k, :], tmp_b[:, k % 2, :], ACT.Copy).then_inc(h_hi_done, 1)

            def make_h(s):
                act.wait_ge(coef, s)
                for k in range(KC):
                    make_h_chunk(s, k)

            def ada_bias(n, slot):
                act.wait_ge(ada_col, n + 1)
                a(ada[:, bass.ds(n, 1)], bank[4 + slot][:, 0:1], ACT.Identity,
                  bias=vcol[:, bass.ds(n, 1)]).then_inc(ada_out, 1)

            def ada_bias_first(k):
                act.wait_ge(ada_col, 2 * k + 2)
                for half in range(2):
                    n = KC * half + k
                    a(ada[:, n:n + 1], bank[4 + k % 2][:, half:half + 1], ACT.Identity,
                      bias=col(R_BADA + n)).then_inc(ada_out, 1)
                act.wait_ge(ada_out, 2 * k + 2)
                a(amp[:, k:k + 1], ada[:, KC + k:KC + k + 1], ACT.Identity, scale=col(R_G[0] + k),
                  bias=col(R_G[0] + k)).then_inc(amp_done, 1)
                act.wait_ge(amp_done, k + 1)

            def split_first(t):
                act.wait_ge(w_in_sem[t], 16)
                hi = w_hi if t < SPLIT else w2_hi
                a(hi[:, t % SPLIT, :], w_raw[:, t, :], ACT.Copy).then_inc(w_hi_done, 1)

            make_rstd(0)
            split_first(0)
            split_first(1)
            for k in range(KC):
                ada_bias_first(k)
                make_h_chunk(0, k)
                if k in (0, 1):
                    split_first(k + 2)

            def up_chunk(base, f, j, hid0, with_ada):
                for half in range(2):
                    t = base + 2 * f + half
                    split_hi(t + SPLIT, half, (2 * j + half + SPLIT) % RAW)
                    if half == 0:
                        a(tmp_a[:, j, :], bank[j][:], ACT.Silu).then_inc(silu_done, 1)
                    if with_ada:
                        ada_bias(ADA0 + 2 * f + half - 1, 1 - half)
                hidden_high(f, j, hid0)

            def hidden_high(f, j, hid0):
                act.wait_ge(hid_f32, hid0 + f + 1)
                a(hid_hi[:, bass.ds(f, 1), :], tmp_b[:, j:j + 1, :], ACT.Copy).then_inc(hid_hi_done, 1)

            def ffn_up(base, hid0, with_ada):
                nc.scalar.preload_act_table_set("silu_and_others")
                if with_ada:
                    for j in range(2):
                        split_hi(base + 2 * SPLIT + j)
                        if j == 1:
                            act.wait_ge(w_used, base + 3)
                        a(tmp_a[:, j, :], bank[j][:], ACT.Silu).then_inc(silu_done, 1)
                    for j in range(2):
                        hidden_high(j, j, 0)
                    for s in range(3):
                        ada_bias(ADA0 + s, s % 2)
                else:
                    for j in range(2):
                        up_chunk(base, j, j, hid0, with_ada)
                with act.Fori(1, FC // 2) as i:
                    for j in range(2):
                        up_chunk(base, 2 * i + j, j, hid0, with_ada)

            ffn_up(T_UP1, 0, True)

            with act.Fori(0, 2) as i:
                for j in range(4):
                    for part in range(3):
                        t = T_DOWN1 + 3 * j + part
                        split_hi(12 * i + t + SPLIT, (t + SPLIT) % SPLIT, (t + SPLIT) % RAW)
                        if (3 * j + part) % 2 == 0:
                            m = (3 * j + part) // 2
                            ada_bias(6 * i + ADA0 + 2 * FC + m - 1, (m - 1) % 2)
                    n = 4 * i + j
                    act.wait_ge(x_upd, n + KC + 1)
                    act.wait_ge(sq_added, n + 1)
                    a(tmp_a[:, j % 2:j % 2 + 1, :], xT[:, bass.ds(n, 1), :], ACT.Square).then_inc(sq_done, 1)
            nc.scalar.preload_act_table_set(EXP_LN_SET)
            make_rstd(1)
            ada_bias(NADA - 1, 1)
            make_h(1)

            act.wait_ge(f_logit, 1)
            act.wait_ge(fbias_in, 16)
            f_z, f_e = ssum[0:JOBS, :], nrm[0:JOBS, :]
            a(f_z, bank[5][0:JOBS, :], ACT.Identity, bias=b_f[:]).then_inc(f_act, 1)
            act.wait_ge(f_act, 1)
            a(f_e, f_z, ACT.Abs).then_inc(f_act, 1)
            act.wait_ge(f_act, 2)
            a(f_e, f_e, ACT.Exp, scale=-1.0).then_inc(f_act, 1)
            act.wait_ge(f_act, 3)
            a(f_e, f_e, ACT.Ln, bias=1.0).then_inc(f_act, 1)
            act.wait_ge(f_dve, 3)
            a(f_cum[0:JOBS, :], f_e, ACT.Copy).then_inc(f_act, 1)

            stats = 0
            n_hi = 0
            gates = 0
            for step in STEPS:
                kind = step[0]
                if kind == "split":
                    split_hi(step[1])
                elif kind == "evac":
                    ci = step[1]
                    what, n, b, tile = CHUNKS[ci]
                    act.wait_ge(w_used, tile + (2 if what == "v" else 1))
                    if what == "v":
                        if n >= 2:
                            act.wait_ge(pv_done, 4 * n - 4)
                        for half in range(2):
                            a(v_hi[:, n % 2, 4 * half:4 * half + 4, 0:3:2, :],
                              bank[half][:].rearrange("p (t h d) -> p t h d", h=2, d=HD), ACT.Copy)\
                                .then_inc(chunk_hi, 1)
                            n_hi += 1
                    elif what == "g":
                        act.wait_ge(g_copy, gates + 1)
                        a(sig[:, n % 2, :], sig[:, n % 2, :], ACT.Exp, scale=-1.0).then_inc(g_exp, 1)
                        act.wait_ge(g_exp, gates + 1)
                        a(sig[:, n % 2, :], sig[:, n % 2, :], ACT.Ln, bias=1.0).then_inc(g_ln, 1)
                        act.wait_ge(g_ln, gates + 1)
                        a(sig[:, n % 2, :], sig[:, n % 2, :], ACT.Exp, scale=-1.0).then_inc(g_ready, 1)
                        gates += 1
                    else:
                        if n >= 2:
                            act.wait_ge(s_done, 5 * (n - 1))
                        a(qk_hi[:, n % 2, int(what == "k"), :], bank[b][:], ACT.Copy,
                          scale=0.125 if what == "q" else 1.0).then_inc(chunk_hi, 1)
                        n_hi += 1
                elif kind == "square":
                    m = step[1]
                    what, n, ci = NORMS[m]
                    if what == "o":
                        act.wait_ge(pv_done, 2 * n + 2)
                    else:
                        act.wait_ge(w_used, CHUNKS[ci][3] + 1)
                    if m:
                        act.wait_ge(stat_done, stats)
                    else:
                        act.wait_ge(f_dve, 3)
                    a(ssum[:], bank[6 if what == "o" else CHUNKS[ci][2]][:], ACT.Square).then_inc(nsq_done, 1)
                elif kind == "stat":
                    m = step[1]
                    stats += 1
                    act.wait_ge(stat_done, stats)
                    if m:
                        act.wait_ge(nrm_f32, m)
                    a(rstd[:], bank[7][:], ACT.Ln, bias=EPS).then_inc(stat_read, 1)
                    act.wait_ge(stat_read, stats)
                    a(rstd[:], rstd[:], ACT.Exp, scale=-0.5).then_inc(nrstd_done, 1)
                elif kind == "part":
                    m = step[1]
                    what, n, ci = NORMS[m]
                    if what == "o":
                        if n >= SBJ:
                            act.wait_ge(nrm_gated, n - SBJ + 1)
                        else:
                            act.wait_ge(nrm_f32, m + 1)
                        a(o_hi[:, n, :], nrm[:], ACT.Copy, scale=col(R_GO + n)).then_inc(nrm_hi, 1)
                    else:
                        act.wait_ge(nrm_f32, m + 1)
                        act.wait_ge(s_done, 5 * (n - 1))
                        a(qk_hi[:, n % 2, int(what == "k"), :], nrm[:], ACT.Copy,
                          scale=gq8[:] if what == "q" else col(R_GK)).then_inc(nrm_hi, 1)
                elif kind == "decay":
                    _, j, h = step
                    stats += 1
                    act.wait_ge(stat_done, stats)
                    if j > SBJ:
                        act.wait_ge(*z_read(5 * j - 1))
                    a(f_keys[:, h, :], bank[7][:], ACT.Copy).then_inc(stat_read, 1)
                elif kind == "prep" and step[1] < SBJ:
                    unit = 5 * step[1] + step[2]
                    buf = tmp_a[:, unit % 2, :]
                    act.wait_ge(relu_done, unit + 1)
                    if unit >= 2:
                        act.wait_ge(scan_done, unit - 1)
                    a(buf, bank[2 + unit % 2][:], ACT.Abs).then_inc(abs_done, 1)
                    act.wait_ge(abs_done, unit + 1)
                    a(buf, buf, ACT.Exp, scale=-1.0).then_inc(eneg_done, 1)
                    act.wait_ge(eneg_done, unit + 1)
                    a(buf, buf, ACT.Ln, bias=1.0).then_inc(e_ready, 1)
                elif kind == "prep":
                    _, j, u = step
                    unit = 5 * j + u
                    buf = tmp_b[:, unit % 2, :]
                    fx = unit - 5 * SBJ
                    act.wait_ge(zf_ready, fx + 1)
                    for s, (h, i, c0) in enumerate(UNITS[u]):
                        seg = buf[:, c0:c0 + (i + 1) * P]
                        last = a(seg, seg, ACT.Exp, bias=small[:, 4 * (unit % 2) + s:4 * (unit % 2) + s + 1],
                                 accum_out=small[:, 8 + 4 * (unit % 2) + s:9 + 4 * (unit % 2) + s])
                    last.then_inc(exp_done, 1)
                elif kind == "exp" and step[1] < SBJ:
                    unit = 5 * step[1] + step[2]
                    act.wait_ge(d_ready, unit + 1)
                    a(tmp_b[:, unit % 2, :], tmp_b[:, unit % 2, :], ACT.Exp).then_inc(p_ready_sb, 1)
                elif kind == "unload":
                    _, j, u = step
                    unit = 5 * j + u
                    act.wait_ge(t_done, unit + 1)
                    for h, dst, src in turned(u):
                        if j:
                            act.wait_ge(pv_done, 2 * (j - 1) + h + 1)
                        last = a(pt_hi[:, h, dst, :], blocks(bank[4 + unit % 2], src), ACT.Copy)
                    last.then_inc(pt_hi_done, 1)

            with act.Fori(0, KC // 4) as i:
                for j in range(4):
                    split_hi(4 * i + j + T_OUT + SPLIT, j % SPLIT, (j + SPLIT) % RAW)
                    n = 4 * i + j
                    act.wait_ge(x_upd, n + 2 * KC + 1)
                    act.wait_ge(sq_added, n + KC + 2)
                    a(tmp_a[:, j % 2:j % 2 + 1, :], xT[:, bass.ds(n, 1), :], ACT.Square).then_inc(sq_done, 1)
            make_rstd(2)
            make_h(2)
            ffn_up(T_UP2, FC, False)

            nc.scalar.preload_act_table_set(EXP_LN_SET)
            for h in range(2):
                act.wait_ge(row_done, h + 1)
                a(gate_row[:, h * 512:(h + 1) * 512], bank[4 + h][:], ACT.Copy).then_inc(row_copied, 1)
            for n in range(2 * TB):
                act.wait_ge(x2_turned, n + 1)
                a(x2_nat[:, n // 2, (n % 2) * 512:(n % 2) * 512 + 512], bank[6 + n % 2][:], ACT.Copy)\
                    .then_inc(x2_copied, 1)

            def square_out(i, tb):
                act.wait_ge(x3_done, TB * i + tb + 1)
                if TB * i + tb >= 2:
                    act.wait_ge(ssq_done, TB * i + tb - 1)
                a(tmp_b[:, tb % 2, :], x2_nat[:, tb, i * 512:(i + 1) * 512], ACT.Square,
                  accum_out=small[:, 16 + TB * i + tb:17 + TB * i + tb]).then_inc(ssq_done, 1)

            def down_tiles(i, parts):
                for n in parts:
                    t = T_DOWN2 + n + SPLIT
                    split_hi(len(NAT_PARTS) * i + t, t % SPLIT, t % RAW)

            down_tiles(0, range(len(NAT_PARTS) - 2))
            for part in (len(NAT_PARTS) - 2, len(NAT_PARTS) - 1):
                down_tiles(0, [part])
            for tb in range(TB):
                square_out(0, tb)
            down_tiles(1, range(len(NAT_PARTS) - 2))
            for tb in range(TB):
                square_out(1, tb)
                act.wait_ge(ms_done, tb + 1)
                a(small[:, 28 + tb:29 + tb], small[:, 24 + tb:25 + tb], ACT.Ln, bias=EPS, scale=1.0 / D)\
                    .then_inc(fln_done, 1)
                act.wait_ge(fln_done, tb + 1)
                a(small[:, 24 + tb:25 + tb], small[:, 28 + tb:29 + tb], ACT.Exp, scale=-0.5).then_inc(frstd_done, 1)

        @block.vector
        def _(dve):
            v = nc.vector

            def split_lo(t, slot=None, raw=None):
                s = t % SPLIT if slot is None else slot
                r = t % RAW if raw is None else raw
                dve.wait_ge(w_hi_done, t + 1)
                v.tensor_tensor(w_lo[:, s, :], w_raw[:, r, :], w_hi[:, s, :].bitcast(F32), ALU.subtract)\
                    .then_inc(w_lo_done, 1)

            def add_square(n, j):
                dve.wait_ge(sq_done, n + 1)
                dve.wait_ge(sq_added, n)
                v.tensor_tensor(ssum[:], ssum[:], tmp_a[:, j % 2, :], ALU.add).then_inc(sq_added, 1)

            v.memset(vecs[:], 0.0).then_inc(vec_zero, 1)
            for buf in (wf_hi, wf_lo):
                v.memset(buf[:].bitcast(F32), 0.0).then_inc(wf_zero, 1)
            dve.wait_ge(consts, N_CONSTS)
            v.tensor_copy(rowsel[:], rowsel_f[:]).then_inc(rowsel_done, 1)

            def reduce_tile(n, tile):
                return v.tensor_reduce(ada_acc[:, n % 2, :], tile.rearrange("p k n -> p n k"), AX_X, ALU.add)\
                    .then_inc(ada_red, 1)

            def ada_first_tile(p):
                if ADA_ROLE[p] == "P":
                    return
                if ADA_ROLE[p] == "D":
                    dve.wait_ge(ada_first_in[p], 16)
                    by_cond(v, stage(p)).then_inc(ada_prod_dve, 1)
                    dve.wait_ge(ada_prod_dve, prods("D", p))
                else:
                    dve.wait_ge(ada_prod_pool, prods("G", p))
                n = ADA_SUMS.index(p)
                if n >= 2:
                    dve.wait_ge(ada_col, ADA_SUMS[n - 2] + 1)
                reduce_tile(n, stage(p))

            def ada_tile(n, slot):
                dve.wait_ge(ada_prod_pool, n + 1 - ADA0 + ADA_ROLE.count("G"))
                dve.wait_ge(ada_col, n - 1)
                reduce_tile(slot + len(ADA_SUMS), ada_w[:, slot, :, :])

            def coefficients(s, hi):
                dve.wait_ge(ada_out, hi)
                dve.wait_ge(h_full, KC * s)
                v.scalar_tensor_tensor(amp[:], ada[:, (3 * s + 1) * KC:(3 * s + 2) * KC], 1.0, col(R_G[s], KC),
                                       ALU.add, ALU.mult).then_inc(coef, 1)

            def x_normed(s, k):
                n = KC * s + k
                if k >= 2:
                    dve.wait_ge(h_full, n - 1)
                v.tensor_tensor(tmp_a[:, k % 2, :], xT[:, k, :], rstd[:], ALU.mult).then_inc(xn_done, 1)

            def normed(s):
                dve.wait_ge(rstd_done, s + 1)
                for k in range(KC):
                    x_normed(s, k)
                    if k:
                        h_low(KC * s + k - 1)
                h_low(KC * s + KC - 1)

            def h_low(n):
                k = n % KC
                dve.wait_ge(h_hi_done, n + 1)
                v.tensor_tensor(h_lo[:, k, :], tmp_b[:, k % 2, :], h_hi[:, k, :].bitcast(F32), ALU.subtract)\
                    .then_inc(h_done, 1)

            dve.wait_ge(cond_ready, 1)
            for p in range(8):
                ada_first_tile(p)
            dve.wait_ge(rstd_done, 1)
            for k in range(KC):
                x_normed(0, k)
                if 2 * k + 9 < ADA0:
                    ada_first_tile(2 * k + 8)
                    ada_first_tile(2 * k + 9)
                h_low(k)

            def hidden(base, f, j, hid0, first):
                dve.wait_ge(silu_done, hid0 + f + 1)
                dve.wait_ge(w_used, base + 2 * f + 2)
                if not first:
                    dve.wait_ge(hid_done, hid0 + f - 1)
                v.tensor_tensor(tmp_b[:, j, :], tmp_a[:, j, :], bank[2 + j][:], ALU.mult).then_inc(hid_f32, 1)

            def hidden_low(f, j, hid0):
                dve.wait_ge(hid_hi_done, hid0 + f + 1)
                v.tensor_tensor(hid_lo[:, bass.ds(f, 1), :], tmp_b[:, j:j + 1, :],
                                hid_hi[:, bass.ds(f, 1), :].bitcast(F32), ALU.subtract).then_inc(hid_done, 1)

            def up_chunk(base, f, j, hid0, with_ada, first):
                for half in range(2):
                    if with_ada:
                        ada_tile(ADA0 + 2 * f + half, half)
                    split_lo(base + 2 * f + half + SPLIT, half, (2 * j + half + SPLIT) % RAW)
                hidden(base, f, j, hid0, first)
                hidden_low(f, j, hid0)

            def ffn_up(base, hid0, with_ada):
                if with_ada:
                    for j in range(2):
                        split_lo(base + 2 * SPLIT + j)
                    for j in range(2):
                        hidden(base, j, j, hid0, True)
                    for j in range(2):
                        hidden_low(j, j, hid0)
                    for s in range(4):
                        ada_tile(ADA0 + s, s % 2)
                else:
                    for j in range(2):
                        up_chunk(base, j, j, hid0, with_ada, True)
                with dve.Fori(1, FC // 2) as i:
                    for j in range(2):
                        up_chunk(base, 2 * i + j, j, hid0, with_ada, False)

            ffn_up(T_UP1, 0, True)

            dve.wait_ge(wf_in, 16)
            dve.wait_ge(wf_zero, 2)
            v.tensor_copy(wf_hi[:, :, 0:JOBS], wf_raw[:]).then_inc(wf_split_hi, 1)
            dve.wait_ge(wf_split_hi, 1)
            v.tensor_tensor(wf_lo[:, :, 0:JOBS], wf_raw[:], wf_hi[:, :, 0:JOBS].bitcast(F32), ALU.subtract)\
                .then_inc(wf_split, 1)
            g0 = 2 * KC
            dve.wait_ge(ada_out, g0 + KC)
            v.tensor_scalar(gate[:], ada[:, g0:g0 + KC], 0.5, None, ALU.mult).then_inc(gacc_done, 1)
            v.memset(ssum[:], 0.0).then_inc(sq_added, 1)
            dve.wait_ge(gacc_done, 1)

            with dve.Fori(0, 2) as i:
                for j in range(4):
                    n = 4 * i + j
                    for part in range(3):
                        t = T_DOWN1 + 3 * j + part
                        if (3 * j + part) % 2 == 0:
                            m = (3 * j + part) // 2
                            ada_tile(6 * i + ADA0 + 2 * FC + m, m % 2)
                        split_lo(12 * i + t + SPLIT, (t + SPLIT) % SPLIT, (t + SPLIT) % RAW)
                    dve.wait_ge(w_used, 12 * i + T_DOWN1 + 3 * j + 3)
                    v.scalar_tensor_tensor(xT[:, bass.ds(n, 1), :], bank[j % 2][:].rearrange("p (o s) -> p o s", o=1),
                                           gate[:, bass.ds(n, 1)], xT[:, bass.ds(n, 1), :], ALU.mult, ALU.add)\
                        .then_inc(x_upd, 1)
                    dve.wait_ge(sq_done, n + KC + 1)
                    dve.wait_ge(sq_added, n + 1)
                    v.tensor_tensor(ssum[:], ssum[:], tmp_a[:, j % 2, :], ALU.add).then_inc(sq_added, 1)
            coefficients(1, 6 * KC)
            normed(1)

            dve.wait_ge(mix_zero, 5)
            dve.wait_ge(f_act, 4)
            f_z, f_e = ssum[0:JOBS, :], nrm[0:JOBS, :]
            v.tensor_scalar(f_z, f_z, 0.0, None, ALU.min).then_inc(f_dve, 1)
            dve.wait_ge(f_dve, 1)
            v.tensor_scalar(gq8[:], col(R_GQ), 0.125, None, ALU.mult).then_inc(f_dve, 1)
            v.tensor_tensor_scan(f_e, f_z, f_e, 0.0, ALU.add, ALU.subtract).then_inc(f_dve, 1)
            dve.wait_ge(f_dve, 3)
            dve.wait_ge(f_act, 5)
            v.tensor_tensor(f_cum[32:32 + JOBS, :], f_e, f_cum[0:JOBS, :].bitcast(F32), ALU.subtract)\
                .then_inc(f_dve, 1)

            n_hi = 0
            for step in STEPS:
                kind = step[0]
                if kind == "split":
                    split_lo(step[1])
                elif kind == "evac":
                    ci = step[1]
                    what, n, b, tile = CHUNKS[ci]
                    if what == "v":
                        for half in range(2):
                            n_hi += 1
                            dve.wait_ge(chunk_hi, n_hi)
                            dst = (n % 2, slice(4 * half, 4 * half + 4), slice(0, 3, 2))
                            v.tensor_tensor(v_lo[:, dst[0], dst[1], dst[2], :],
                                            bank[half][:].rearrange("p (t h d) -> p t h d", h=2, d=HD),
                                            v_hi[:, dst[0], dst[1], dst[2], :].bitcast(F32), ALU.subtract)\
                                .then_inc(v_ready, 1)
                    elif what == "g":
                        dve.wait_ge(w_used, tile + 1)
                        if n >= SBJ + 2:
                            dve.wait_ge(nrm_gated, n - SBJ - 1)
                        v.tensor_scalar(sig[:, n % 2, :], bank[b][:], -80.0, None, ALU.max).then_inc(g_copy, 1)
                    else:
                        n_hi += 1
                        dve.wait_ge(chunk_hi, n_hi)
                        v.scalar_tensor_tensor(qk_lo[:, n % 2, int(what == "k"), :], bank[b][:],
                                               0.125 if what == "q" else 1.0,
                                               qk_hi[:, n % 2, int(what == "k"), :].bitcast(F32),
                                               ALU.mult, ALU.subtract).then_inc(qk_ready, 1)
                elif kind == "scale":
                    m = step[1]
                    what, n, ci = NORMS[m]
                    dve.wait_ge(nrstd_done, m + 1)
                    if m:
                        dve.wait_ge(nrm_lo, m)
                    else:
                        dve.wait_ge(f_dve, 4)
                    src = bank[6 if what == "o" else CHUNKS[ci][2]]
                    v.tensor_tensor(nrm[:], src[:], rstd[:], ALU.mult).then_inc(nrm_f32, 1)
                    dve.wait_ge(nrm_f32, m + 1)
                    if what == "o":
                        if n >= SBJ:
                            dve.wait_ge(g_ready, n - SBJ + 1)
                            v.tensor_tensor(nrm[:], nrm[:], sig[:, n % 2, :], ALU.mult).then_inc(nrm_gated, 1)
                            dve.wait_ge(nrm_gated, n - SBJ + 1)
                elif kind == "part":
                    m = step[1]
                    what, n, ci = NORMS[m]
                    if what == "o":
                        dve.wait_ge(nrm_hi, m + 1)
                        v.scalar_tensor_tensor(o_lo[:, n, :], nrm[:], col(R_GO + n), o_hi[:, n, :].bitcast(F32),
                                               ALU.mult, ALU.subtract).then_inc(nrm_lo, 1)
                    else:
                        dve.wait_ge(nrm_hi, m + 1)
                        v.scalar_tensor_tensor(qk_lo[:, n % 2, int(what == "k"), :], nrm[:],
                                               gq8[:] if what == "q" else col(R_GK),
                                               qk_hi[:, n % 2, int(what == "k"), :].bitcast(F32),
                                               ALU.mult, ALU.subtract).then_inc(nrm_lo, 1)
                elif kind == "prep":
                    _, j, u = step
                    unit = 5 * j + u
                    zb, buf = bank[2 + unit % 2], tmp_b[:, unit % 2, :]
                    dve.wait_ge(s_done, unit + 1)
                    if unit >= 2:
                        dve.wait_ge(t_done, unit - 1)
                    if j < SBJ:
                        v.tensor_scalar(buf, zb[:], 0.0, None, ALU.max).then_inc(relu_done, 1)
                    else:
                        fx = unit - 5 * SBJ
                        if u == 0:
                            dve.wait_ge(stat_read, stat_uses(("decay", j, 1)))
                        if fx >= 2:
                            dve.wait_ge(exp_done, fx - 1)
                        s0 = 4 * (unit % 2)
                        for s, (h, i, c0) in enumerate(UNITS[u]):
                            n = (i + 1) * P
                            last = v.tensor_tensor_reduce(
                                out=buf[:, c0:c0 + n], in0=zb[:, c0:c0 + n], in1=f_keys[:, h, 0:n], scale=1.0,
                                scalar=-3.0e38, op0=ALU.subtract, op1=ALU.max, accum_out=small[:, s0 + s:s0 + s + 1])
                        last.then_inc(max_done, 1)
                        dve.wait_ge(max_done, fx + 1)
                        ns = len(UNITS[u])
                        v.tensor_scalar(small[:, s0:s0 + ns], small[:, s0:s0 + ns], -1.0, None, ALU.mult)\
                            .then_inc(zf_ready, 1)
                elif kind == "sum" and step[1] < SBJ:
                    _, j, u = step
                    unit = 5 * j + u
                    zb, buf = bank[2 + unit % 2], tmp_b[:, unit % 2, :]
                    dve.wait_ge(relu_done, unit + 1)
                    dve.wait_ge(e_ready, unit + 1)
                    for h, i, c0 in UNITS[u]:
                        n = (i + 1) * P
                        back = slice(c0 + n - 1, c0 - 1 if c0 else None, -1)
                        last = v.tensor_tensor_scan(buf[:, back], tmp_a[:, unit % 2, back], buf[:, back],
                                                    0.0, ALU.add, ALU.add)
                    last.then_inc(scan_done, 1)
                    dve.wait_ge(scan_done, unit + 1)
                    v.tensor_tensor(buf, zb[:], buf, ALU.subtract).then_inc(d_ready, 1)
                elif kind == "sum":
                    _, j, u = step
                    unit = 5 * j + u
                    fx = unit - 5 * SBJ
                    buf, s0, ns = tmp_b[:, unit % 2, :], 8 + 4 * (unit % 2), len(UNITS[u])
                    dve.wait_ge(exp_done, fx + 1)
                    v.reciprocal(small[:, s0:s0 + ns], small[:, s0:s0 + ns]).then_inc(inv_done, 1)
                    dve.wait_ge(inv_done, fx + 1)
                    for s, (h, i, c0) in enumerate(UNITS[u]):
                        seg = buf[:, c0:c0 + (i + 1) * P]
                        last = v.tensor_scalar(seg, seg, small[:, s0 + s:s0 + s + 1], None, ALU.mult)
                    last.then_inc(p_ready_fx, 1)
                elif kind == "unload":
                    _, j, u = step
                    unit = 5 * j + u
                    dve.wait_ge(pt_hi_done, unit + 1)
                    for h, dst, src in turned(u):
                        last = v.tensor_tensor(pt_lo[:, h, dst, :], blocks(bank[4 + unit % 2], src),
                                               pt_hi[:, h, dst, :].bitcast(F32), ALU.subtract)
                    last.then_inc(pt_ready, 1)

            g1 = 5 * KC
            v.memset(ssum[:], 0.0).then_inc(sq_added, 1)
            v.tensor_copy(gate[:], ada[:, g1:g1 + KC]).then_inc(gacc_done, 1)
            dve.wait_ge(gacc_done, 2)
            with dve.Fori(0, KC // 4) as i:
                for j in range(4):
                    n = 4 * i + j
                    split_lo(n + T_OUT + SPLIT, j % SPLIT, (j + SPLIT) % RAW)
                    dve.wait_ge(w_used, n + T_OUT + 1)
                    v.scalar_tensor_tensor(xT[:, bass.ds(n, 1), :], bank[j % 2][:].rearrange("p (o s) -> p o s", o=1),
                                           gate[:, bass.ds(n, 1)], xT[:, bass.ds(n, 1), :], ALU.mult, ALU.add)\
                        .then_inc(x_upd, 1)
                    dve.wait_ge(sq_done, n + 2 * KC + 1)
                    dve.wait_ge(sq_added, n + KC + 2)
                    v.tensor_tensor(ssum[:], ssum[:], tmp_a[:, j % 2, :], ALU.add).then_inc(sq_added, 1)
            coefficients(2, 9 * KC)
            normed(2)
            ffn_up(T_UP2, FC, False)

            g2 = 8 * KC
            v.tensor_scalar(gate[:], ada[:, g2:g2 + KC], 0.5, None, ALU.mult).then_inc(scaled, 1)
            dve.wait_ge(scaled, 1)
            dve.wait_ge(w_used, T_DOWN2)
            for k in range(KC):
                v.tensor_scalar(diag[:, k, :], ident[:], gate[:, k:k + 1], None, ALU.mult).then_inc(diag_done, 1)

            def finish(i, tb):
                dve.wait_ge(out_acc, TB * i + tb + 1)
                if i:
                    dve.wait_ge(x3_done, TB * i + tb - 1)
                elif tb >= 2:
                    dve.wait_ge(x3_done, tb - 1)
                v.tensor_tensor(tmp_a[:, tb % 2, :], bank[tb][:], gate_row[:, i * 512:(i + 1) * 512], ALU.mult)\
                    .then_inc(scaled, 1)
                dve.wait_ge(scaled, TB * i + tb + 2)
                half = x2_nat[:, tb, i * 512:(i + 1) * 512]
                v.tensor_tensor(half, tmp_a[:, tb % 2, :], half, ALU.add).then_inc(x3_done, 1)

            for n in range(len(NAT_PARTS) - 1):
                split_lo(T_DOWN2 + n + SPLIT)
            split_lo(T_DOWN2 + len(NAT_PARTS) + 1)
            dve.wait_ge(row_copied, 2)
            dve.wait_ge(x2_copied, 2 * TB)
            for tb in range(TB):
                finish(0, tb)
            for n in range(len(NAT_PARTS) - 2):
                split_lo(T_DOWN2 + len(NAT_PARTS) + n + SPLIT)
            dve.wait_ge(gfin_in, 32)
            for tb in range(TB):
                finish(1, tb)
                dve.wait_ge(ssq_done, TB + tb + 1)
                v.tensor_tensor(small[:, 24 + tb:25 + tb], small[:, 16 + tb:17 + tb], small[:, 20 + tb:21 + tb],
                                ALU.add).then_inc(ms_done, 1)
                dve.wait_ge(frstd_done, tb + 1)
                v.scalar_tensor_tensor(x2_nat[:, tb, :], x2_nat[:, tb, :], small[:, 24 + tb:25 + tb], gfin_row[:],
                                       ALU.mult, ALU.mult).then_inc(y_done, 1)


_INS = ["x", "c", "w_ada", "b_ada", "g_ffn1", "w_ffn1_up", "w_ffn1_down", "g_mix", "w_in", "b_forget", "g_fox_q",
        "g_fox_k", "g_sb_out", "g_fox_out", "w_out", "g_ffn2", "w_ffn2_up", "w_ffn2_down", "g_final"]
_OUTS = [((1, SEQ, D), "float32")]


def kernel(**inputs):
    import numpy as _np
    import concourse.bacc as _bacc
    from concourse import mybir as _mybir
    from concourse.bass_utils import run_bass_kernel_spmd as _run

    nc = _bacc.Bacc("TRN2", target_bir_lowering=False, num_devices=1)
    arrays, args = {}, []
    for name in _INS:
        a = _np.ascontiguousarray(inputs[name])
        arrays[f"in_{name}_dram"] = a
        args.append(nc.dram_tensor(f"in_{name}_dram", a.shape, _mybir.dt.from_np(a.dtype), kind="ExternalInput").ap())
    for i, (shape, dtype) in enumerate(_OUTS):
        dt = _mybir.dt.from_np(_np.dtype(dtype))
        args.append(nc.dram_tensor(f"out_{i}_dram", shape, dt, kind="ExternalOutput").ap())
    hybrid_block_kernel(nc, *args)
    r = _run(nc, [arrays], core_ids=[0])
    return r.results[0]["out_0_dram"]
```

```python
from contextlib import ExitStack

import concourse.bass as bass
from concourse import mybir

ALU = mybir.AluOpType
ACT = mybir.ActivationFunctionType
F32 = mybir.dt.float32
F32R = mybir.dt.float32r
BF16 = mybir.dt.bfloat16
AX_X = mybir.AxisListType.X
EXP_LN_SET = "natural_log_exp_and_others"

P = 128
SEQ = 512
TB = SEQ // P
D = 1024
KC = D // P
FFN = 2816
FC = FFN // P
HD = 64
JOBS = 8
SBJ = 4
EPS = 1e-6
N_IDENT, N_CONSTS = 2, 15
NEG = -(2.0 ** 126)
WS = 1024
DOWN_PARTS = ((0, 8), (8, 8), (16, 6))
NAT_PARTS = ((0, 2), (2, 2), (4, 1), (5, 1)) + tuple((k, 2) for k in range(6, 22, 2))
NADA = 9 * KC
ADA0 = 2 * KC
ADA_ROLE = "PPPGPGPG" "GDGGPGDG"
ADA_DOWN = ADA0 + 2 * (FC - 2)
ADA_SUMS = [p for p in range(ADA0) if ADA_ROLE[p] != "P"]

T_UP1 = 0
T_DOWN1 = T_UP1 + 2 * FC
T_MIX = T_DOWN1 + 3 * KC
N_MIX = 4 * 2 + 2 * JOBS + (JOBS - SBJ)
T_OUT = T_MIX + N_MIX
T_UP2 = T_OUT + KC
T_DOWN2 = T_UP2 + 2 * FC
N_TILES = T_DOWN2 + 2 * len(NAT_PARTS)
RAW = 4
SPLIT = 2

UNITS = (
    ((0, 3, 0),),
    ((0, 2, 0), (0, 0, 384)),
    ((0, 1, 0), (1, 1, 256)),
    ((1, 2, 0), (1, 0, 384)),
    ((1, 3, 0),),
)
PT_BLOCKS = 13
ZERO_BLOCK = 11


def chunks():
    order = [(name[0], int(name[1])) for name in (
        "q0 k0 v0 q1 k1 q2 k2 v1 v2 q3 k3 q4 k4 q5 k5 g4 g5 v3 q6 k6 q7 k7 g6 g7").split()]
    out, tile = [], T_MIX
    for kind, n in order:
        out.append((kind, n, {"v": 0, "q": 0, "k": 1, "g": n % 2}[kind], tile))
        tile += 2 if kind == "v" else 1
    assert tile == T_MIX + N_MIX
    return out


CHUNKS = chunks()


PERIOD = ("StPaamUdamvbtDTxxLxE", "SmPdaabTvtUtEamxDL")
LAG_STAT, LAG_BANK, LAG_TILE = 4, 1, 5
BEHIND = 18


def halves_due(p):
    return int(4 + 2.05 * min(p + 1, 5) + 1.55 * min(max(p - 4, 0), 20) + 0.95 * max(p - 24, 0))


def mixer_steps():
    steps, norms, chains, evacs, splits = [], [], [], [], []
    array = {"proj": 12, "out": 12, "scores": 4, "values": 4, "turn": 2}
    spent, since = [0], {}

    def emit(*step):
        steps.append(step)
        spent[0] += array.get(step[0], 0)

    def banks_of(c):
        return (0, 1) if CHUNKS[c][0] == "v" else (CHUNKS[c][2],)

    def move(force=False):
        if not chains or (chains[0][0][0] == "stat" and not force and spent[0] - since["chain"] < LAG_STAT):
            return
        stage = chains[0].pop(0)
        emit(*stage)
        since["chain"] = since[stage] = spent[0]
        if stage[0] == "scale" and norms[stage[1]][2] is not None:
            for b in banks_of(norms[stage[1]][2]):
                since[b] = spent[0]
        if not chains[0]:
            chains.pop(0)

    def tick(force=False):
        if evacs:
            for b in banks_of(evacs[0][1]):
                since[b] = spent[0]
            emit(*evacs.pop(0))
        move(force)

    def head_norm(kind, n, chunk=None):
        m = len(norms)
        norms.append((kind, n, chunk))
        chains.append([("square", m), ("stat", m), ("scale", m), ("part", m)])

    queue = [(c, part, half) for c, chunk in enumerate(CHUNKS)
             for part in range(2 if chunk[0] == "v" else 1) for half in range(2)]
    queue += [("out", n, k0) for k0 in (0, 4) for n in range(2)]
    at_start = 4
    total = len(queue)

    def unread():
        return ([c for _, c in evacs]
                + [norms[chain[0][1]][2] for chain in chains
                   if chain[0][0] != "forget" and norms[chain[0][1]][2] is not None and chain[0][0] != "part"])

    def proj(force=True):
        c, part, half = queue[0]
        if c == "out":
            job = min(half + 4, KC - 1) - 1
            ready = [m for m, norm in enumerate(norms) if norm[:2] == ("o", job) and ("part", m) in steps]
            if not ready or not force and (
                    spent[0] - since["part", ready[0]] < LAG_BANK or evacs
                    or spent[0] - since.get(("tile", T_OUT + part), -LAG_TILE) < LAG_TILE):
                return False
            while evacs:
                tick(True)
            emit("out", part, half, min(half + 4, KC - 1))
            queue.pop(0)
            return True
        kind, n, _, tile = CHUNKS[c]
        if half == 0 and not force and spent[0] - since.get(("tile", tile + part), -LAG_TILE) < LAG_TILE:
            return False
        if part == half == 0:
            if not force and (any(set(banks_of(c)) & set(banks_of(x)) for x in unread())
                              or any(spent[0] - since.get(b, -LAG_BANK) < LAG_BANK for b in banks_of(c))):
                return False
            while any(set(banks_of(c)) & set(banks_of(x)) for x in unread()):
                tick(True)
        queue.pop(0)
        emit("proj", tile + part, c, half)
        if half == 1:
            splits.append(("split", tile + part + SPLIT))
            if kind != "v" or part == 1:
                if kind in "qk" and n >= SBJ:
                    head_norm(kind, n, c)
                else:
                    evacs.append(("evac", c))
        return True

    def made_first(j):
        return ([("evac", c) for c, chunk in enumerate(CHUNKS) if chunk[0] in "qk" and chunk[1] == j < SBJ]
                + [("part", m) for m, norm in enumerate(norms) if norm[0] in "qk" and norm[1] == j])

    def split():
        for step in splits:
            emit(*step)
            since["tile", step[1]] = spent[0]
        splits.clear()

    chains.append([("forget", n) for n in range(6)])
    for _ in range(at_start):
        proj()
        split()
        tick(True)
    tick(True)

    units = [(j, u) for j in range(JOBS) for u in range(5)]
    for p, (j, u) in enumerate(units):
        before = units[p - 1] if p else None
        due = min(total, halves_due(p))
        while u == 0 and any(step in made_first(j) for step in evacs + [chain[-1] for chain in chains]):
            tick(True)
        for item in PERIOD[0 if j < SBJ else 1]:
            if item == "S":
                emit("scores", j, u)
            elif item == "P":
                emit("prep", j, u)
            elif item == "U":
                emit("sum", j, u)
            elif item == "E":
                emit("exp", j, u)
            elif item == "T" and before:
                emit("turn", *before)
            elif item == "L" and before:
                emit("unload", *before)
            elif item == "v" and u == 1 and j:
                emit("values", j - 1, 1)
                head_norm("o", j - 1)
            elif item == "v" and u == 4:
                emit("values", j, 0)
            elif item in "dD" and u == 4 and SBJ <= j + 1 < JOBS:
                emit("decay", j + 1, "dD".index(item))
            elif item == "a" and total - len(queue) < due:
                proj(total - len(queue) < due - BEHIND)
            elif item == "b":
                while total - len(queue) < due and proj(False):
                    split()
                    tick()
            elif item == "x":
                split()
            elif item == "m":
                move()
            elif item == "t":
                tick()
    emit("turn", *units[-1])
    emit("unload", *units[-1])
    while queue and proj():
        pass
    split()
    emit("more", 2)
    emit("values", JOBS - 1, 1)
    head_norm("o", JOBS - 1)
    while len(chains) > 1 or evacs:
        tick(True)
    move(True)
    emit("more", 3)
    emit("out", 2, 0, KC - 1)
    move(True)
    move(True)
    move(True)
    emit("out", 3, 0, KC - 1)
    for n in range(4):
        emit("out", n, KC - 1, KC)
    assert not queue
    return steps, norms


STEPS, NORMS = mixer_steps()


def hybrid_block_kernel(
    nc: bass.Bass, x, c, w_ada, b_ada, g_ffn1, w_ffn1_up, w_ffn1_down, g_mix, w_in, b_forget,
    g_fox_q, g_fox_k, g_sb_out, g_fox_out, w_out, g_ffn2, w_ffn2_up, w_ffn2_down, g_final, out,
):
    ctx = ExitStack()
    with ctx:
        def sem(name):
            return ctx.enter_context(nc.semaphore(name))

        slab = ctx.enter_context(nc.sbuf_tensor("slab", [P, 207 * 256], F32))
        top = [0]

        def size(shape, dt):
            n = 2 if dt == BF16 else 4
            for s in shape[1:]:
                n *= s
            return -(-n // 32) * 32

        def at(name, shape, dt, offset):
            return nc.alloc_sbuf_tensor_at(name, shape, dt, offset=slab_base + offset)

        def keep(name, shape, dt=F32):
            t = at(name, shape, dt, top[0])
            top[0] += size(shape, dt)
            return t

        slab_base = nc.sbuf_base - 207 * 1024

        xT = keep("xT", [P, KC, SEQ])
        w_raw = keep("w_raw", [P, RAW, WS])
        w_hi = keep("w_hi", [P, SPLIT, WS], F32R)
        w_lo = keep("w_lo", [P, SPLIT, WS], F32R)
        ident = keep("ident", [P, P])
        ident_bf = keep("ident_bf", [P, P], BF16)
        mask_strict = keep("mask_strict", [P, P], BF16)
        mask_causal = keep("mask_causal", [P, P], BF16)
        pair_mean = keep("pair_mean", [P, P])
        ones = keep("ones", [P, 1])
        rowsel_f = keep("rowsel_f", [HD, JOBS])
        rowsel = keep("rowsel", [HD, JOBS], F32R)
        vcol = keep("vcol", [P, P])
        ada = keep("ada", [P, NADA])
        amp = keep("amp", [P, KC])
        gate = keep("gate", [P, KC])
        cond = keep("cond", [P, KC])
        gq8 = keep("gq8", [P, 1])
        b_f = keep("b_f", [JOBS, 1])
        small = keep("small", [P, 32])
        tmp_offset = top[0]
        tmp_a = keep("tmp_a", [P, 2, SEQ])
        tmp_b = keep("tmp_b", [P, 2, SEQ])
        tmp = at("tmp", [P, 4, SEQ], F32, tmp_offset)
        ssum = keep("ssum", [P, SEQ])
        rstd = keep("rstd", [P, SEQ])
        h_offset = top[0]
        h_hi = keep("h_hi", [P, KC, SEQ], F32R)
        h_lo = keep("h_lo", [P, KC, SEQ], F32R)
        region = top[0]

        hid_hi = at("hid_hi", [P, FC, SEQ], F32R, region)
        hid_lo = at("hid_lo", [P, FC, SEQ], F32R, region + FC * SEQ * 4)
        ada_w = at("ada_w", [P, 2, KC, P], F32, region + 2 * FC * SEQ * 4)
        ada_acc = at("ada_acc", [P, 2, P], F32, region + 2 * FC * SEQ * 4 + 2 * D * 4)
        x_nat = at("x_nat", [P, TB, D], F32, region)
        vecs = at("vecs", [P, P], F32, region + TB * D * 4)
        ada_first = at("ada_first", [P, ADA0 - 4, KC, P], F32, region + TB * D * 4 + 512)
        w2_hi = at("w2_hi", [P, SPLIT, WS], F32R, region + TB * D * 4 + 512 + (ADA0 - 4) * D * 4)
        w2_lo = at("w2_lo", [P, SPLIT, WS], F32R, region + TB * D * 4 + 512 + (ADA0 - 2) * D * 4)
        ada_acc_first = at("ada_acc_first", [P, len(ADA_SUMS), P], F32, region + TB * D * 4 + 512 + ADA0 * D * 4)
        assert TB * D * 4 + 512 + ADA0 * D * 4 + len(ADA_SUMS) * P * 4 <= 2 * FC * SEQ * 4
        y = at("y", [P, TB, D], F32, h_offset)
        gfin_row = at("gfin_row", [P, D], F32, h_offset + TB * D * 4)

        top[0] = region
        v_hi = keep("v_hi", [P, 2, 2 * TB, 3, HD], F32R)
        v_lo = keep("v_lo", [P, 2, 2 * TB, 3, HD], F32R)
        qk_offset = top[0]
        qk_hi = keep("qk_hi", [P, 2, 2, SEQ], F32R)
        qk_lo = keep("qk_lo", [P, 2, 2, SEQ], F32R)
        pt_hi = keep("pt_hi", [P, 2, PT_BLOCKS, P], F32R)
        pt_lo = keep("pt_lo", [P, 2, PT_BLOCKS, P], F32R)
        o_hi = keep("o_hi", [P, JOBS, SEQ], F32R)
        o_lo = keep("o_lo", [P, JOBS, SEQ], F32R)
        beyond = top[0]
        f_keys = keep("f_keys", [P, 2, SEQ])
        f_cum = keep("f_cum", [HD, SEQ], F32R)
        sig = keep("sig", [P, 2, SEQ])
        nrm = keep("nrm", [P, SEQ])
        w3_hi = at("w3_hi", [P, SPLIT, WS], F32R, qk_offset)
        w3_lo = at("w3_lo", [P, SPLIT, WS], F32R, qk_offset + SPLIT * WS * 4)
        diag = at("diag", [P, KC, P], F32, beyond)
        gate_row = at("gate_row", [P, 1, D], F32, beyond + 3 * SEQ * 4)
        assert beyond >= region + 2 * FC * SEQ * 4 + 2 * D * 4 + 2 * P * 4
        wf_hi = at("wf_hi", [P, KC, P], F32R, beyond)
        wf_lo = at("wf_lo", [P, KC, P], F32R, beyond + 3 * SEQ * 4)
        wf_raw = at("wf_raw", [P, KC, JOBS], F32, beyond + 5 * SEQ * 4)
        assert top[0] <= 207 * 1024 and region + 2 * FC * SEQ * 4 + 2 * D * 4 + P * 8 <= 207 * 1024, top

        bank = [ctx.enter_context(nc.psum_tensor(f"bank{i}", [P, SEQ], F32)) for i in range(8)]

        wf_zero = sem("wf_zero")
        ada_first_in = [sem(f"ada_first_in{p}") for p in range(ADA0)]
        amp_done = sem("amp_done")
        rowsel_done, sq_zero = sem("rowsel_done"), sem("sq_zero")
        cond_e, cond_1, cond_r = sem("cond_e"), sem("cond_1"), sem("cond_r")
        ada_prod_dve, ada_prod_pool = sem("ada_prod_dve"), sem("ada_prod_pool")
        vec_zero, vec_in, fbias_in, wf_in = sem("vec_zero"), sem("vec_in"), sem("fbias_in"), sem("wf_in")
        x_in = [sem("x_in0"), sem("x_in1")]
        w_in_sem = [sem(f"w_loaded{i}") for i in range(RAW)]
        ada_in = [sem("ada_loaded0"), sem("ada_loaded1")]
        gfin_in = sem("gfin_in")
        consts = sem("consts")
        w_hi_done, w_lo_done, w_used = sem("w_hi_done"), sem("w_lo_done"), sem("w_used")
        vec_turned, vec_cols = sem("vec_turned"), sem("vec_cols")
        cond_ready = sem("cond_ready")
        x_turned = sem("x_turned")
        x_upd, sq_done, sq_added = sem("x_upd"), sem("sq_done"), sem("sq_added")
        sum_done, ln_done, rstd_done = sem("sum_done"), sem("ln_done"), sem("rstd_done")
        xn_done, h_hi_done, h_done = sem("xn_done"), sem("h_hi_done"), sem("h_done")
        ada_red, ada_col, ada_out, coef = sem("ada_red"), sem("ada_col"), sem("ada_out"), sem("coef")
        silu_done, hid_f32, hid_hi_done, hid_done = (
            sem("silu_done"), sem("hid_f32"), sem("hid_hi_done"), sem("hid_done"))
        mix_zero = sem("mix_zero")
        wf_split, wf_split_hi, f_logit, f_act, f_dve = (
            sem("wf_split"), sem("wf_split_hi"), sem("f_logit"), sem("f_act"), sem("f_dve"))
        chunk_hi, qk_ready, v_ready = (
            sem("chunk_hi"), sem("qk_ready"), sem("v_ready"))
        g_copy, g_exp, g_ln, g_ready = sem("g_copy"), sem("g_exp"), sem("g_ln"), sem("g_ready")
        s_done, relu_done, abs_done, eneg_done, e_ready, scan_done, d_ready, p_ready_sb = (
            sem("s_done"), sem("relu_done"), sem("abs_done"), sem("eneg_done"), sem("e_ready"),
            sem("scan_done"), sem("d_ready"), sem("p_ready_sb"))
        even_scored = sem("even_scored")
        max_done, zf_ready, exp_done, inv_done, p_ready_fx = (
            sem("max_done"), sem("zf_ready"), sem("exp_done"), sem("inv_done"), sem("p_ready_fx"))
        t_done, pt_hi_done, pt_ready, pv_done = sem("t_done"), sem("pt_hi_done"), sem("pt_ready"), sem("pv_done")
        nsq_done, stat_done, stat_read, nrstd_done, nrm_f32, nrm_gated, nrm_hi, nrm_lo = (
            sem("nsq_done"), sem("stat_done"), sem("stat_read"), sem("nrstd_done"), sem("nrm_f32"),
            sem("nrm_gated"), sem("nrm_hi"), sem("nrm_lo"))
        out_acc, gacc_done, diag_done, row_done, row_copied = (
            sem("out_acc"), sem("gacc_done"), sem("diag_done"), sem("row_done"), sem("row_copied"))
        w_gated, ssq_done, ms_done, fln_done, frstd_done, y_half, y_done, stored = (
            sem("w_gated"), sem("ssq_done"), sem("ms_done"), sem("fln_done"), sem("frstd_done"),
            sem("y_half"), sem("y_done"), sem("stored"))

        up_v = [w.rearrange("o (k p) n -> (o p) k n", p=P) for w in (w_ffn1_up, w_ffn2_up)]
        down_v = [w.rearrange("o (k p) n -> (o p) k n", p=P) for w in (w_ffn1_down, w_ffn2_down)]
        in_v = w_in.rearrange("o (k p) n -> (o p) k n", p=P)
        out_v = w_out.rearrange("o (k p) n -> (o p) k n", p=P)
        ada_v = w_ada.rearrange("o (k p) n -> (o p) k n", p=P)

        def col(row, n=1):
            return vcol[:, row:row + n]

        R_BADA, R_G = 0, (NADA, NADA + KC, NADA + 2 * KC)
        R_GO = NADA + 3 * KC
        R_C = R_GO + JOBS
        R_GQ, R_GK = R_C + KC, R_C + KC + 1

        def tile8(buf, slot, k=KC):
            return buf[:, slot, 0:WS].rearrange("p (k n) -> p k n", k=KC)[:, 0:k, :]

        def tile4(buf, slot):
            return buf[:, slot, :].rearrange("p (k n) -> p k n", k=4)

        def tile2(buf, slot):
            return buf[:, slot, :].rearrange("p (k n) -> p k n", k=2)

        def turned(u):
            if u in (0, 4):
                return [(u // 4, slice(3, 13, 3), slice(0, 4))]
            if u in (1, 3):
                return [(u // 3, slice(2, 9, 3), slice(0, 3)), (u // 3, slice(0, 1), slice(3, 4))]
            return [(0, slice(1, 5, 3), slice(0, 2)), (1, slice(1, 5, 3), slice(2, 4))]

        def blocks(b, which):
            return b[:].rearrange("p (b n) -> p b n", n=P)[:, which, :]


        def stage(p):
            return ada_first[:, p - 2, :, :] if 2 <= p < ADA0 - 2 else ada_w[:, p % 2, :, :]

        def prods(role, p):
            return ADA_ROLE[:p + 1].count(role)

        def by_cond(engine, tile):
            return engine.tensor_tensor(tile, tile, cond[:].rearrange("p (k o) -> p k o", o=1)
                                        .broadcast_to([P, KC, P]), ALU.mult)

        def norm_of(what, j):
            return [n for n, e in enumerate(NORMS) if e[0:2] == (what, j)][0]

        def chunk_read(ci):
            what, n, _, _ = CHUNKS[ci]
            if what == "v":
                return v_ready, 2 * n + 2
            if what == "g":
                return g_copy, n - SBJ + 1
            if n < SBJ:
                return qk_ready, 2 * n + 1 + int(what == "k")
            return nrm_f32, norm_of(what, n) + 1

        def z_read(unit):
            return (d_ready, unit + 1) if unit < 5 * SBJ else (max_done, unit - 5 * SBJ + 1)

        def tile_used(t):
            half, n = divmod(t - T_DOWN2, len(NAT_PARTS))
            if half >= 0 and n == len(NAT_PARTS) - 1:
                return out_acc, TB * (half + 1)
            return w_used, t + 1 - max(half, 0)

        def stat_uses(until):
            n = 0
            for step in STEPS:
                n += step[0] in ("stat", "decay")
                if step == until:
                    return n

        block = ctx.enter_context(nc.Block())

        @block.gpsimd
        def _(pool):
            g = nc.gpsimd
            made = [0]

            def link(ins):
                made[0] += 1
                ins.then_inc(consts, 1)
                pool.wait_ge(consts, made[0])

            def select(buf, compare, fill, base, width):
                link(g.affine_select(out=buf[:], in_=buf[:], compare_op=compare, fill=fill, base=base,
                                     pattern=[[-1, width]], channel_multiplier=1))

            link(g.memset(ident[:], 0.0))
            select(ident, ALU.not_equal, 1.0, 0, P)
            for buf in (ident_bf, mask_strict, mask_causal, pair_mean, rowsel_f):
                link(g.memset(buf[:], 0.0))
            link(g.memset(ones[:], 1.0))
            select(ident_bf, ALU.not_equal, 1.0, 0, P)
            select(mask_strict, ALU.is_gt, NEG, 0, P)
            select(mask_causal, ALU.is_ge, NEG, 0, P)
            for h in range(2):
                link(g.memset(pair_mean[h * HD:(h + 1) * HD, h * HD:(h + 1) * HD], 1.0 / HD))
            for base in (0, -32):
                select(rowsel_f, ALU.not_equal, 1.0, base, JOBS)
            assert made[0] == N_CONSTS
            pool.wait_ge(cond_ready, 1)
            for p in range(ADA0):
                if ADA_ROLE[p] == "G":
                    pool.wait_ge(ada_first_in[p], 16)
                    by_cond(g, stage(p)).then_inc(ada_prod_pool, 1)
                    pool.wait_ge(ada_prod_pool, prods("G", p))

            def ada_tile(n, slot):
                pool.wait_ge(ada_in[slot], 8 * n + 16 - 8 * slot - 8 * ADA0)
                by_cond(g, ada_w[:, slot, :, :]).then_inc(ada_prod_pool, 1)
                pool.wait_ge(ada_prod_pool, n + 1 - ADA0 + ADA_ROLE.count("G"))

            with pool.Fori(0, (NADA - ADA0) // 2) as i:
                for slot in range(2):
                    ada_tile(2 * i + ADA0 + slot, slot)
            pool.wait_ge(w_used, T_MIX)
            for n, part in enumerate((v_hi[:, :, :, 1, :], v_lo[:, :, :, 1, :], pt_hi[:, :, ZERO_BLOCK, :],
                                      pt_lo[:, :, ZERO_BLOCK, :], f_cum[:])):
                g.memset(part.bitcast(F32), 0.0).then_inc(mix_zero, 1)
                pool.wait_ge(mix_zero, n + 1)
            pool.wait_ge(row_copied, 2)
            for half in range(2):
                for n, (k0, nk) in enumerate(NAT_PARTS):
                    t = len(NAT_PARTS) * half + T_DOWN2 + n
                    r = n % RAW
                    pool.wait_ge(w_in_sem[r], 4 * t + 16 - 4 * r)
                    tile = tile2(w_raw, r)[:, 0:nk, :]
                    g.tensor_tensor(tile, tile, gate_row[:, :, half * 512:(half + 1) * 512]
                                    .broadcast_to([P, nk, 512]), ALU.mult).then_inc(w_gated, 1)
                    pool.wait_ge(w_gated, len(NAT_PARTS) * half + n + 1)

        @block.sync
        def _(sp):
            def load_w(t, slot, dst, src, first=False):
                if not first:
                    sp.wait_ge(w_lo_done, t - RAW + 1)
                sp.dma_start(dst, src).then_inc(w_in_sem[slot], 16)

            def load_up(ffn, base, f, j, first=False):
                for half in range(2):
                    load_w(base + 2 * f + half, 2 * j + half, tile8(w_raw, 2 * j + half),
                           up_v[ffn][:, :, bass.ds(f * P + half * FFN, P)], first)

            def load_ada(a, slot):
                sp.wait_ge(ada_red, a - ADA0 + len(ADA_SUMS) - 1)
                sp.dma_start(ada_w[:, slot, :, :], ada_v[:, :, bass.ds(a * P, P)]).then_inc(ada_in[slot], 16)

            def load_ada_first(p):
                if p >= ADA0 - 2:
                    sp.wait_ge(ada_col, p - ADA0 + 3)
                a = p // 2 + KC * (p % 2)
                sp.dma_start(stage(p), ada_v[:, :, a * P:(a + 1) * P]).then_inc(ada_first_in[p], 16)

            def load_x(half):
                sp.dma_start(x_nat[:, :, half * 512:(half + 1) * 512],
                             x.rearrange("o (t p) d -> (o p) t d", p=P)[:, :, half * 512:(half + 1) * 512])\
                  .then_inc(x_in[half], 16)

            load_x(0)
            sp.wait_ge(vec_zero, 1)
            n = 0
            for src, row, rows in ((b_ada, R_BADA, NADA), (g_ffn1, R_G[0], KC), (g_mix, R_G[1], KC),
                                   (g_ffn2, R_G[2], KC), (g_sb_out, R_GO, SBJ), (g_fox_out, R_GO + SBJ, SBJ),
                                   (c, R_C, KC)):
                sp.dma_start(vecs[row:row + rows, :], src.rearrange("o (r p) -> (o r) p", p=P)).then_inc(vec_in, 16)
                n += 1
            for src, row in ((g_fox_q, R_GQ), (g_fox_k, R_GK)):
                for h in range(2):
                    sp.dma_start(vecs[row:row + 1, h * HD:(h + 1) * HD], src).then_inc(vec_in, 16)
                    n += 1
            assert n == 11
            load_x(1)
            for p in range(ADA0):
                load_ada_first(p)
                if p in (3, 7):
                    load_up(0, T_UP1, p // 4, p // 4, True)
            sp.dma_start(b_f[:], b_forget.rearrange("o h -> h o")).then_inc(fbias_in, 16)
            sp.dma_start(wf_raw[:], in_v[:, :, 7 * 512:7 * 512 + JOBS]).then_inc(wf_in, 16)
            sp.wait_ge(ada_col, ADA0 - 1)
            with sp.Fori(1, FC // 2) as i:
                for j in range(2):
                    load_up(0, T_UP1, 2 * i + j, j)
                    for s in range(2):
                        load_ada(ADA0 + 4 * i + 2 * j + s - 4, s)
            with sp.Fori(0, 2) as i:
                for j in range(4):
                    for part, (k0, nk) in enumerate(DOWN_PARTS):
                        t = T_DOWN1 + 3 * j + part
                        load_w(12 * i + t, t % RAW, tile8(w_raw, t % RAW, nk),
                               down_v[0][:, k0:k0 + nk, bass.ds((4 * i + j) * P, P)])
                        if part < 2:
                            a = 2 * j + part
                            load_ada(8 * i + ADA_DOWN + a, a % 2)
            for kind, n, _, tile in CHUNKS:
                if kind == "v":
                    c0 = (2 if n < 2 else 5) * 512 + (n % 2) * 256
                    for part in range(2):
                        t = tile + part
                        load_w(t, t % RAW, tile4(w_raw, t % RAW), in_v[:, 4 * part:4 * part + 4, c0:c0 + 256])
                else:
                    c0 = (3 * 512 if n >= SBJ else 0) + (n % SBJ) * P + {"q": 0, "k": 512, "g": 3 * 512}[kind]
                    load_w(tile, tile % RAW, tile8(w_raw, tile % RAW), in_v[:, :, c0:c0 + P])
            with sp.Fori(0, KC // RAW) as i:
                for j in range(RAW):
                    load_w(T_OUT + RAW * i + j, j, tile8(w_raw, j), out_v[:, :, bass.ds((RAW * i + j) * P, P)])
            with sp.Fori(0, FC // 2) as i:
                for j in range(2):
                    load_up(1, T_UP2, 2 * i + j, j)
            with sp.Fori(0, 2) as i:
                for n, (k0, nk) in enumerate(NAT_PARTS):
                    load_w(len(NAT_PARTS) * i + T_DOWN2 + n, n % RAW, tile2(w_raw, n % RAW)[:, 0:nk, :],
                           down_v[1][:, k0:k0 + nk, bass.ds(i * 512, 512)])
                    if n == RAW - 1:
                        sp.wait_ge(w_used, T_DOWN2)
                        sp.dma_start(gfin_row[:, bass.ds(i * 512, 512)],
                                     g_final[bass.ds(i * 512, 512)].partition_broadcast(P)).then_inc(gfin_in, 16)
            for t in range(TB):
                sp.wait_ge(y_half, t + 1)
                sp.wait_ge(y_done, t + 1)
                sp.dma_start(out[0, t * P:(t + 1) * P, :], y[:, t, :]).then_inc(stored, 16)
            sp.wait_ge(stored, 16 * TB)

        @block.tensor
        def _(pe):
            mm = nc.tensor.matmul

            def three(dst, wh, wl, xh, xl, start, stop, skip=False):
                mm(dst, wh, xh, start=start, stop=False, skip_group_check=skip)
                mm(dst, wh, xl, start=False, stop=False, skip_group_check=skip)
                return mm(dst, wl, xh, start=False, stop=stop, skip_group_check=skip)

            def split_ready(t):
                pe.wait_ge(w_lo_done, t + 1)

            def sum_squares(s):
                b = bank[3 if s == 2 else 6]
                pe.wait_ge(sq_added, (KC + 1) * s + KC - 1)
                mm(b[:], ones[:, 0:1].broadcast_to([P, P]), ssum[:], start=True, stop=False)
                pe.wait_ge(sq_done, KC * (s + 1))
                mm(b[:], ones[:, 0:1].broadcast_to([P, P]), tmp_a[:, 1, :], start=False, stop=True)\
                    .then_inc(sum_done, 1)

            def ada_column_first(p):
                b = bank[4 + (p // 2) % 2][:, p % 2:p % 2 + 1]
                if p >= 4 and p % 2 == 0:
                    pe.wait_ge(ada_out, p - 2)
                if ADA_ROLE[p] == "P":
                    pe.wait_ge(ada_first_in[p], 16)
                    for k in range(KC):
                        last = mm(b, stage(p)[:, k, :], cond[:, k:k + 1], start=k == 0, stop=k == KC - 1)
                else:
                    n = ADA_SUMS.index(p)
                    pe.wait_ge(ada_red, n + 1)
                    last = mm(b, ada_acc_first[:, n, :], ones[:], start=True, stop=True)
                last.then_inc(ada_col, 1)

            def ada_column(a, slot):
                pe.wait_ge(ada_red, a + len(ADA_SUMS) - ADA0 + 1)
                pe.wait_ge(ada_out, a - 1)
                mm(bank[4 + slot][:, 0:1], ada_acc[:, slot, :], ones[:], start=True, stop=True)\
                    .then_inc(ada_col, 1)

            pe.wait_ge(consts, N_IDENT)
            for k in range(KC):
                if k % 4 == 0:
                    pe.wait_ge(x_in[k // 4], 16)
                if k >= 2:
                    pe.wait_ge(sq_done, k - 1)
                for t in range(TB):
                    last = nc.tensor.transpose(bank[k % 2][:, t * P:(t + 1) * P],
                                               x_nat[:, t, k * P:(k + 1) * P], ident[:])
                last.then_inc(x_turned, 1)
                if k == 1:
                    pe.wait_ge(vec_in, 16 * 11)
                    nc.tensor.transpose(bank[7][:, 0:P], vecs[:], ident[:]).then_inc(vec_turned, 1)
                if k == KC - 2:
                    pe.wait_ge(consts, N_CONSTS)
                    pe.wait_ge(cond_ready, 1)
                    for p in range(2):
                        ada_column_first(p)
            sum_squares(0)

            def first_tiles(base, k, hi2, lo2):
                for n in range(4):
                    hi, lo = (w_hi, w_lo) if n < SPLIT else (hi2, lo2)
                    if k == 0:
                        split_ready(base + n)
                    last = three(bank[2 * (n % 2) + n // 2][:], tile8(hi, n % 2)[:, k, :], tile8(lo, n % 2)[:, k, :],
                                 h_hi[:, k, :], h_lo[:, k, :], k == 0, k == KC - 1)
                    if k == KC - 1:
                        last.then_inc(w_used, 1)

            for p in range(2, 6):
                ada_column_first(p)
            for k in range(KC):
                if k >= 1 and 2 * k + 5 < ADA0:
                    ada_column_first(2 * k + 4)
                    ada_column_first(2 * k + 5)
                pe.wait_ge(h_done, k + 1)
                first_tiles(T_UP1, k, w2_hi, w2_lo)

            def up_pair(base, f, j, hid0, with_ada):
                for half in range(2):
                    split_ready(base + 2 * f + half)
                    if half == 0:
                        pe.wait_ge(hid_f32, hid0 + f - 1)
                    for k in range(KC):
                        last = three(bank[2 * half + j][:], tile8(w_hi, half)[:, k, :], tile8(w_lo, half)[:, k, :],
                                     h_hi[:, k, :], h_lo[:, k, :], k == 0, k == KC - 1)
                    last.then_inc(w_used, 1)
                if with_ada:
                    for half in range(2):
                        ada_column(ADA0 - 4 + 2 * f + half, half)

            with pe.Fori(1, FC // 2) as i:
                for j in range(2):
                    up_pair(T_UP1, 2 * i + j, j, 0, True)

            pe.wait_ge(hid_done, FC - 1)
            with pe.Fori(0, 2) as i:
                for j in range(4):
                    n = 4 * i + j
                    pe.wait_ge(x_upd, n + KC - 1)
                    for part, (k0, nk) in enumerate(DOWN_PARTS):
                        t = T_DOWN1 + 3 * j + part
                        split_ready(12 * i + t)
                        if part == 2:
                            pe.wait_ge(hid_done, FC)
                        for k in range(nk):
                            last = three(bank[j % 2][:], tile8(w_hi, t % 2)[:, k, :], tile8(w_lo, t % 2)[:, k, :],
                                         hid_hi[:, k0 + k, :], hid_lo[:, k0 + k, :],
                                         part == 0 and k == 0, k0 + k == FC - 1)
                        last.then_inc(w_used, 1)
                        if part:
                            a = 2 * j + part - 1
                            ada_column(8 * i + ADA_DOWN + a, a % 2)
            sum_squares(1)

            pe.wait_ge(wf_split, 1)
            pe.wait_ge(ada_out, NADA)
            for k in range(KC):
                pe.wait_ge(h_done, KC + k + 1)
                last = three(bank[5][:], wf_hi[:, k, :], wf_lo[:, k, :], h_hi[:, k, :], h_lo[:, k, :],
                             k == 0, k == KC - 1)
            last.then_inc(f_logit, 1)

            stats = 0
            last_on_bank = {}
            for step in STEPS:
                kind = step[0]
                if kind == "proj":
                    _, t, ci, half = step
                    what, n, b, first_tile = CHUNKS[ci]
                    if half == 0:
                        split_ready(t)
                        if t == first_tile:
                            used = [last_on_bank[x] for x in ((0, 1) if what == "v" else (b,)) if x in last_on_bank]
                            for prior in sorted(set(used)):
                                pe.wait_ge(*chunk_read(prior))
                            for x in ((0, 1) if what == "v" else (b,)):
                                last_on_bank[x] = ci
                    if what == "v":
                        part = t - first_tile
                        for kk in range(2 * half, 2 * half + 2):
                            k = 4 * part + kk
                            for tb in range(TB):
                                dst = bank[tb // 2][:, (tb % 2) * 256:(tb % 2) * 256 + 256]
                                last = three(dst, h_hi[:, k, tb * P:(tb + 1) * P], h_lo[:, k, tb * P:(tb + 1) * P],
                                             tile4(w_hi, t % 2)[:, kk, :], tile4(w_lo, t % 2)[:, kk, :],
                                             k == 0 and tb % 2 == 0, k == KC - 1, skip=True)
                    else:
                        for k in range(4 * half, 4 * half + 4):
                            last = three(bank[b][:], tile8(w_hi, t % 2)[:, k, :], tile8(w_lo, t % 2)[:, k, :],
                                         h_hi[:, k, :], h_lo[:, k, :], k == 0, k == KC - 1)
                    if half == 1:
                        last.then_inc(w_used, 1)
                elif kind == "out":
                    _, n, k0, k1 = step
                    hi, lo = (w_hi, w_lo) if n < SPLIT else (w3_hi, w3_lo)
                    if k0 == 0:
                        split_ready(T_OUT + n)
                        pe.wait_ge(*(chunk_read(last_on_bank[n]) if n < 2 else z_read(5 * JOBS - 4 + n)))
                    pe.wait_ge(nrm_lo, norm_of("o", k1 - 1) + 1)
                    for k in range(k0, k1):
                        last = three(bank[n][:], tile8(hi, n % 2)[:, k, :], tile8(lo, n % 2)[:, k, :],
                                     o_hi[:, k, :], o_lo[:, k, :], k == 0, k == KC - 1)
                    if k1 == KC:
                        last.then_inc(w_used, 1)
                elif kind == "scores":
                    _, j, u = step
                    unit = 5 * j + u
                    if u == 0:
                        if j < SBJ:
                            pe.wait_ge(qk_ready, 2 * j + 2)
                        else:
                            pe.wait_ge(nrm_lo, norm_of("k", j) + 1)
                    if unit >= 2:
                        pe.wait_ge(*z_read(unit - 2))
                    zb = bank[2 + unit % 2]
                    for h, i, c0 in UNITS[u]:
                        n = (i + 1) * P
                        rows = slice(h * HD, (h + 1) * HD)
                        q_h, q_l = (q[rows, j % 2, 0, i * P:(i + 1) * P] for q in (qk_hi, qk_lo))
                        k_h, k_l = (k[rows, j % 2, 1, 0:n] for k in (qk_hi, qk_lo))
                        three(zb[:, c0:c0 + n], q_h, q_l, k_h, k_l, True, False)
                        last = mm(zb[:, c0 + i * P:c0 + n], ident_bf[:], (mask_strict if j < SBJ else mask_causal)[:],
                                  start=False, stop=True)
                        if u == 2 and h == 0:
                            last.then_inc(even_scored, 1)
                            pe.wait_ge(even_scored, j + 1)
                    last.then_inc(s_done, 1)
                elif kind == "turn":
                    _, j, u = step
                    unit = 5 * j + u
                    if j < SBJ:
                        pe.wait_ge(p_ready_sb, unit + 1)
                    else:
                        pe.wait_ge(p_ready_fx, unit - 5 * SBJ + 1)
                    if unit >= 2:
                        pe.wait_ge(pt_ready, unit - 1)
                    elif unit == 1:
                        pe.wait_ge(f_act, 1)
                    for b in range(4):
                        last = nc.tensor.transpose(bank[4 + unit % 2][:, b * P:(b + 1) * P],
                                                   tmp_b[:, unit % 2, b * P:(b + 1) * P], ident[:])
                    last.then_inc(t_done, 1)
                elif kind == "values":
                    _, j, h = step
                    pe.wait_ge(pt_ready, 5 * j + (3 if h == 0 else 5))
                    pe.wait_ge(v_ready, 2 * (j // 2 + 1))
                    if j == 0 and h == 0:
                        pe.wait_ge(mix_zero, 5)
                    if h == 0 and j:
                        pe.wait_ge(nrm_f32, norm_of("o", j - 1) + 1)
                    slot, pl = (j // 2) % 2, j % 2
                    for kb in range(TB):
                        q0 = min(kb, 2)
                        blocks = slice(3 * kb + q0, 3 * kb + TB)
                        vh, vl = (v[:, slot, 2 * kb + pl, h:h + 2, :] for v in (v_hi, v_lo))
                        ph, pl_ = (p[:, h, blocks, :] for p in (pt_hi, pt_lo))
                        last = three(bank[6][:, q0 * P:], vh, vl, ph, pl_, h == 0 and kb == 0,
                                     h == 1 and kb == TB - 1)
                    last.then_inc(pv_done, 1)
                elif kind == "stat":
                    m = step[1]
                    pe.wait_ge(nsq_done, m + 1)
                    if stats:
                        pe.wait_ge(stat_read, stats)
                    mm(bank[7][:], pair_mean[:], ssum[:], start=True, stop=True).then_inc(stat_done, 1)
                    stats += 1
                elif kind == "decay":
                    _, j, h = step
                    if stats:
                        pe.wait_ge(stat_read, stats)
                    if j == SBJ and h == 0:
                        pe.wait_ge(rowsel_done, 1)
                        pe.wait_ge(f_dve, 4)
                    head = 2 * (j - SBJ) + h
                    mm(bank[7][:], rowsel[:, head:head + 1].broadcast_to([HD, P]), f_cum[:], start=True, stop=True)\
                        .then_inc(stat_done, 1)
                    stats += 1

            for n in range(4, KC):
                pe.wait_ge(x_upd, 2 * KC + (n - 4 if n < 6 else n - 2) + 1)
                split_ready(n + T_OUT)
                for k in range(KC):
                    last = three(bank[n % 2][:], tile8(w_hi, n % 2)[:, k, :], tile8(w_lo, n % 2)[:, k, :],
                                 o_hi[:, k, :], o_lo[:, k, :], k == 0, k == KC - 1)
                last.then_inc(w_used, 1)
            pe.wait_ge(diag_done, KC)
            for k in range(KC):
                last = mm(bank[6 + k // 4][:, (k % 4) * P:(k % 4 + 1) * P], ones[:, 0:1].broadcast_to([P, P]),
                          diag[:, k, :], start=True, stop=True)
                if k % 4 == 3:
                    last.then_inc(row_done, 1)
            sum_squares(2)

            def start_with_x(tb, half):
                for b in range(4):
                    mm(bank[4 * half + tb][:, b * P:(b + 1) * P], xT[:, 4 * half + b, tb * P:(tb + 1) * P], ident[:],
                       start=b == 0, stop=False, skip_group_check=True)

            for tb in range(2):
                start_with_x(tb, 1)
            for k in range(KC):
                pe.wait_ge(h_done, 2 * KC + k + 1)
                first_tiles(T_UP2, k, w3_hi, w3_lo)
            with pe.Fori(1, FC // 2) as i:
                for j in range(2):
                    up_pair(T_UP2, 2 * i + j, j, FC, False)

            pe.wait_ge(row_copied, 2)
            for tb in range(2, TB):
                start_with_x(tb, 1)
            for tb in (0, 2, 1, 3):
                pe.wait_ge(hid_f32, 2 * FC - 1 + tb % 2)
                start_with_x(tb, 0)
            for half in range(2):
                for n, (k0, nk) in enumerate(NAT_PARTS):
                    split_ready(len(NAT_PARTS) * half + T_DOWN2 + n)
                    if half == 0 and k0 + nk >= FC - 1:
                        pe.wait_ge(hid_done, 2 * FC)
                    elif half == 0:
                        pe.wait_ge(hid_done, 2 * FC - 2)
                    for tb in range(TB):
                        for k in range(nk):
                            last = three(bank[4 * half + tb][:], hid_hi[:, k0 + k, tb * P:(tb + 1) * P],
                                         hid_lo[:, k0 + k, tb * P:(tb + 1) * P],
                                         tile2(w_hi, n % 2)[:, k, :], tile2(w_lo, n % 2)[:, k, :],
                                         False, k0 + k == FC - 1, skip=True)
                        if n == len(NAT_PARTS) - 1:
                            last.then_inc(out_acc, 1)
                    if n < len(NAT_PARTS) - 1:
                        last.then_inc(w_used, 1)

        @block.scalar
        def _(act):
            a = nc.scalar.activation

            def split_hi(t, slot=None, raw=None, used=None):
                s = t % SPLIT if slot is None else slot
                r = t % RAW if raw is None else raw
                if isinstance(t, int) and t >= T_DOWN2:
                    act.wait_ge(w_gated, t - T_DOWN2 + 1)
                else:
                    act.wait_ge(w_in_sem[r], turns(t, r))
                if used is not None:
                    act.wait_ge(w_used, used + 1)
                elif isinstance(t, int):
                    act.wait_ge(*tile_used(t - SPLIT))
                else:
                    act.wait_ge(w_used, t - SPLIT + 1)
                a(w_hi[:, s, :], w_raw[:, r, :], ACT.Copy).then_inc(w_hi_done, 1)

            def turns(t, r):
                return 4 * t + 16 - 4 * r

            nc.scalar.preload_act_table_set(EXP_LN_SET)
            for k in range(KC):
                act.wait_ge(x_turned, k + 1)
                a(xT[:, k, :], bank[k % 2][:], ACT.Copy).then_inc(x_upd, 1)
                if k >= 2:
                    act.wait_ge(sq_added, k - 1)
                a(tmp_a[:, k % 2, :], bank[k % 2][:], ACT.Square).then_inc(sq_done, 1)
                if k == 1:
                    act.wait_ge(vec_turned, 1)
                    a(vcol[:], bank[7][:, 0:P], ACT.Copy).then_inc(vec_cols, 1)
                    act.wait_ge(vec_cols, 1)
                    a(cond[:], col(R_C, KC), ACT.Exp, scale=-1.0).then_inc(cond_e, 1)

            def make_rstd(s):
                act.wait_ge(sum_done, s + 1)
                a(rstd[:], bank[3 if s == 2 else 6][:], ACT.Ln, bias=EPS, scale=1.0 / D).then_inc(ln_done, 1)
                act.wait_ge(ln_done, s + 1)
                a(rstd[:], rstd[:], ACT.Exp, scale=-0.5).then_inc(rstd_done, 1)

            def make_h_chunk(s, k):
                n = KC * s + k
                act.wait_ge(xn_done, n + 1)
                a(h_hi[:, k, :], tmp[:, k % 4, :], ACT.Identity,
                  bias=ada[:, 3 * KC * s + k:3 * KC * s + k + 1]).then_inc(h_hi_done, 1)

            def make_h(s):
                for k in range(KC):
                    make_h_chunk(s, k)
                    if s == 2 and k == 0:
                        split_first(T_UP2 + 3, w3_hi)

            def ada_bias(n, slot):
                act.wait_ge(ada_col, n + 1)
                a(ada[:, bass.ds(n, 1)], bank[4 + slot][:, 0:1], ACT.Identity,
                  bias=vcol[:, bass.ds(n, 1)]).then_inc(ada_out, 1)

            def ada_bias_first(k):
                act.wait_ge(ada_col, 2 * k + 2)
                for half in range(2):
                    n = KC * half + k
                    a(ada[:, n:n + 1], bank[4 + k % 2][:, half:half + 1], ACT.Identity,
                      bias=col(R_BADA + n)).then_inc(ada_out, 1)
                act.wait_ge(ada_out, 2 * k + 2)
                a(amp[:, k:k + 1], ada[:, KC + k:KC + k + 1], ACT.Identity, scale=col(R_G[0] + k),
                  bias=col(R_G[0] + k)).then_inc(amp_done, 1)

            def split_first(t, hi):
                act.wait_ge(w_in_sem[t % RAW], turns(t, t % RAW))
                a(hi[:, t % SPLIT, :], w_raw[:, t % RAW, :], ACT.Copy).then_inc(w_hi_done, 1)

            make_rstd(0)
            split_first(0, w_hi)
            split_first(1, w_hi)
            ada_bias_first(0)
            for k in range(KC):
                if k + 1 < KC:
                    ada_bias_first(k + 1)
                make_h_chunk(0, k)
                if k in (0, 1):
                    split_first(k + 2, w2_hi)

            def up_chunk(base, f, j, hid0, with_ada):
                for half in range(2):
                    t = base + 2 * f + half
                    split_hi(t + SPLIT, half, (2 * j + half + SPLIT) % RAW)
                    if half == 0:
                        a(tmp_a[:, j, :], bank[j][:], ACT.Silu).then_inc(silu_done, 1)
                if with_ada:
                    for half in range(2):
                        ada_bias(ADA0 - 4 + 2 * f + half, half)
                hidden_high(f, j, hid0)

            def hidden_high(f, j, hid0):
                act.wait_ge(hid_f32, hid0 + f + 1)
                a(hid_hi[:, bass.ds(f, 1), :], tmp_b[:, j:j + 1, :], ACT.Copy).then_inc(hid_hi_done, 1)

            def ffn_up(base, hid0, with_ada):
                nc.scalar.preload_act_table_set("silu_and_others")
                split_hi(base + 2 * SPLIT, used=base)
                for j in range(2):
                    act.wait_ge(w_used, base + 2 * j + 1)
                    a(tmp_a[:, j, :], bank[j][:], ACT.Silu).then_inc(silu_done, 1)
                split_hi(base + 2 * SPLIT + 1, used=base + 1)
                for j in range(2):
                    hidden_high(j, j, hid0)
                with act.Fori(1, FC // 2 if with_ada else FC // 2 - 1) as i:
                    for j in range(2):
                        up_chunk(base, 2 * i + j, j, hid0, with_ada)
                if not with_ada:
                    for j in range(2):
                        up_chunk(base, FC - 2 + j, j, hid0, with_ada)

            ffn_up(T_UP1, 0, True)
            nc.scalar.preload_act_table_set(EXP_LN_SET)

            with act.Fori(0, 2) as i:
                for j in range(4):
                    for part in range(3):
                        t = T_DOWN1 + 3 * j + part
                        split_hi(12 * i + t + SPLIT, (t + SPLIT) % SPLIT, (t + SPLIT) % RAW)
                        if part:
                            m = 2 * j + part - 1
                            ada_bias(8 * i + ADA_DOWN + m, m % 2)
                    n = 4 * i + j
                    act.wait_ge(x_upd, n + KC + 1)
                    act.wait_ge(sq_added, n + KC)
                    a(tmp_a[:, j % 2:j % 2 + 1, :], xT[:, bass.ds(n, 1), :], ACT.Square).then_inc(sq_done, 1)
            make_rstd(1)
            make_h(1)

            f_z, f_e = ssum[0:JOBS, :], nrm[0:JOBS, :]
            stats = 0
            n_hi = 0
            gates = 0
            for step in STEPS:
                kind = step[0]
                if kind == "split":
                    split_hi(step[1])
                elif kind == "more":
                    act.wait_ge(s_done, 5 * JOBS)
                    split_first(T_OUT + step[1], w3_hi)
                elif kind == "forget":
                    if step[1] == 0:
                        act.wait_ge(f_logit, 1)
                        act.wait_ge(fbias_in, 16)
                        a(f_z, bank[5][0:JOBS, :], ACT.Identity, bias=b_f[:]).then_inc(f_act, 1)
                    elif step[1] == 1:
                        act.wait_ge(f_act, 1)
                        a(f_e, f_z, ACT.Abs).then_inc(f_act, 1)
                        act.wait_ge(f_act, 2)
                        a(f_e, f_e, ACT.Exp, scale=-1.0).then_inc(f_act, 1)
                    elif step[1] == 2:
                        act.wait_ge(f_act, 3)
                        a(f_e, f_e, ACT.Ln, bias=1.0).then_inc(f_act, 1)
                    elif step[1] == 4:
                        act.wait_ge(f_dve, 3)
                        act.wait_ge(mix_zero, 5)
                        a(f_cum[0:JOBS, :], f_e, ACT.Copy).then_inc(f_act, 1)
                elif kind == "evac":
                    ci = step[1]
                    what, n, b, tile = CHUNKS[ci]
                    act.wait_ge(w_used, tile + (2 if what == "v" else 1))
                    if what == "v":
                        if n >= 2:
                            act.wait_ge(pv_done, 4 * n - 4)
                        for half in range(2):
                            a(v_hi[:, n % 2, 4 * half:4 * half + 4, 0:3:2, :],
                              bank[half][:].rearrange("p (t h d) -> p t h d", h=2, d=HD), ACT.Copy)\
                                .then_inc(chunk_hi, 1)
                            n_hi += 1
                    elif what == "g":
                        act.wait_ge(g_copy, gates + 1)
                        a(sig[:, n % 2, :], sig[:, n % 2, :], ACT.Exp, scale=-1.0).then_inc(g_exp, 1)
                        act.wait_ge(g_exp, gates + 1)
                        a(sig[:, n % 2, :], sig[:, n % 2, :], ACT.Ln, bias=1.0).then_inc(g_ln, 1)
                        act.wait_ge(g_ln, gates + 1)
                        a(sig[:, n % 2, :], sig[:, n % 2, :], ACT.Exp, scale=-1.0).then_inc(g_ready, 1)
                        gates += 1
                    else:
                        if n >= 2:
                            act.wait_ge(s_done, 5 * (n - 1))
                        a(qk_hi[:, n % 2, int(what == "k"), :], bank[b][:], ACT.Copy,
                          scale=0.125 if what == "q" else 1.0).then_inc(chunk_hi, 1)
                        n_hi += 1
                elif kind == "square":
                    m = step[1]
                    what, n, ci = NORMS[m]
                    if what == "o":
                        act.wait_ge(pv_done, 2 * n + 2)
                    else:
                        act.wait_ge(w_used, CHUNKS[ci][3] + 1)
                    if m:
                        act.wait_ge(stat_done, stats)
                    else:
                        act.wait_ge(f_dve, 4)
                    a(ssum[:], bank[6 if what == "o" else CHUNKS[ci][2]][:], ACT.Square).then_inc(nsq_done, 1)
                elif kind == "stat":
                    m = step[1]
                    stats += 1
                    act.wait_ge(stat_done, stats)
                    if m:
                        act.wait_ge(nrm_f32, m)
                    a(rstd[:], bank[7][:], ACT.Ln, bias=EPS).then_inc(stat_read, 1)
                    act.wait_ge(stat_read, stats)
                    a(rstd[:], rstd[:], ACT.Exp, scale=-0.5).then_inc(nrstd_done, 1)
                elif kind == "part":
                    m = step[1]
                    what, n, ci = NORMS[m]
                    if what == "o":
                        if n >= SBJ:
                            act.wait_ge(nrm_gated, n - SBJ + 1)
                        else:
                            act.wait_ge(nrm_f32, m + 1)
                        a(o_hi[:, n, :], nrm[:], ACT.Copy, scale=col(R_GO + n)).then_inc(nrm_hi, 1)
                    else:
                        act.wait_ge(nrm_f32, m + 1)
                        act.wait_ge(s_done, 5 * (n - 1))
                        a(qk_hi[:, n % 2, int(what == "k"), :], nrm[:], ACT.Copy,
                          scale=gq8[:] if what == "q" else col(R_GK)).then_inc(nrm_hi, 1)
                elif kind == "decay":
                    _, j, h = step
                    stats += 1
                    act.wait_ge(stat_done, stats)
                    if j > SBJ:
                        act.wait_ge(*z_read(5 * j - 1))
                    a(f_keys[:, h, :], bank[7][:], ACT.Copy).then_inc(stat_read, 1)
                elif kind == "prep" and step[1] < SBJ:
                    unit = 5 * step[1] + step[2]
                    buf = tmp_a[:, unit % 2, :]
                    act.wait_ge(relu_done, unit + 1)
                    if unit >= 2:
                        act.wait_ge(scan_done, unit - 1)
                    a(buf, bank[2 + unit % 2][:], ACT.Abs).then_inc(abs_done, 1)
                    act.wait_ge(abs_done, unit + 1)
                    a(buf, buf, ACT.Exp, scale=-1.0).then_inc(eneg_done, 1)
                    act.wait_ge(eneg_done, unit + 1)
                    a(buf, buf, ACT.Ln, bias=1.0).then_inc(e_ready, 1)
                elif kind == "prep":
                    _, j, u = step
                    unit = 5 * j + u
                    buf = tmp_b[:, unit % 2, :]
                    fx = unit - 5 * SBJ
                    act.wait_ge(zf_ready, fx + 1)
                    for s, (h, i, c0) in enumerate(UNITS[u]):
                        seg = buf[:, c0:c0 + (i + 1) * P]
                        last = a(seg, seg, ACT.Exp, bias=small[:, 4 * (unit % 2) + s:4 * (unit % 2) + s + 1],
                                 accum_out=small[:, 8 + 4 * (unit % 2) + s:9 + 4 * (unit % 2) + s])
                    last.then_inc(exp_done, 1)
                elif kind == "exp" and step[1] < SBJ:
                    unit = 5 * step[1] + step[2]
                    act.wait_ge(d_ready, unit + 1)
                    a(tmp_b[:, unit % 2, :], tmp_b[:, unit % 2, :], ACT.Exp).then_inc(p_ready_sb, 1)
                elif kind == "unload":
                    _, j, u = step
                    unit = 5 * j + u
                    act.wait_ge(t_done, unit + 1)
                    for h, dst, src in turned(u):
                        if j:
                            act.wait_ge(pv_done, 2 * (j - 1) + h + 1)
                        last = a(pt_hi[:, h, dst, :], blocks(bank[4 + unit % 2], src), ACT.Copy)
                    last.then_inc(pt_hi_done, 1)

            for n in range(KC):
                if n < 2:
                    split_hi(n + T_OUT + 4, used=n + T_OUT)
                elif n >= 4:
                    split_hi(n + T_OUT + SPLIT)
                act.wait_ge(x_upd, n + 2 * KC + 1)
                act.wait_ge(sq_added, n + 2 * KC + 1)
                a(tmp_a[:, n % 2, :], xT[:, n, :], ACT.Square).then_inc(sq_done, 1)
            act.wait_ge(w_used, T_OUT + 4)
            split_first(T_UP2 + 2, w3_hi)
            make_rstd(2)
            for h in range(2):
                act.wait_ge(row_done, h + 1)
                a(gate_row[:, 0, h * 512:(h + 1) * 512], bank[6 + h][:], ACT.Copy).then_inc(row_copied, 1)
            make_h(2)
            ffn_up(T_UP2, FC, False)

            def square_out(half, tb):
                n = TB * half + tb
                act.wait_ge(out_acc, n + 1)
                if n >= 2:
                    act.wait_ge(ssq_done, n - 1)
                a(tmp_b[:, tb % 2, :], bank[n][:], ACT.Square, accum_out=small[:, 16 + n:17 + n]).then_inc(ssq_done, 1)

            for t in range(T_DOWN2 + SPLIT, T_DOWN2 + len(NAT_PARTS) + SPLIT):
                split_hi(t)
            nc.scalar.preload_act_table_set(EXP_LN_SET)
            for tb in range(TB):
                square_out(0, tb)
            for t in range(T_DOWN2 + len(NAT_PARTS) + SPLIT, N_TILES):
                split_hi(t)
            for tb in range(TB):
                square_out(1, tb)
                act.wait_ge(ssq_done, TB + tb + 1)
                act.wait_ge(ms_done, TB)
                a(small[:, 28 + tb:29 + tb], small[:, 20 + tb:21 + tb], ACT.Ln, bias=small[:, 24 + tb:25 + tb],
                  scale=1.0 / D).then_inc(fln_done, 1)
                act.wait_ge(fln_done, tb + 1)
                a(small[:, 28 + tb:29 + tb], small[:, 28 + tb:29 + tb], ACT.Exp, scale=-0.5).then_inc(frstd_done, 1)

        @block.vector
        def _(dve):
            v = nc.vector

            def split_lo(t, slot=None, raw=None):
                s = t % SPLIT if slot is None else slot
                r = t % RAW if raw is None else raw
                dve.wait_ge(w_hi_done, t + 1)
                v.tensor_tensor(w_lo[:, s, :], w_raw[:, r, :], w_hi[:, s, :].bitcast(F32), ALU.subtract)\
                    .then_inc(w_lo_done, 1)

            v.memset(vecs[:], 0.0).then_inc(vec_zero, 1)
            for buf in (wf_hi, wf_lo):
                v.memset(buf[:].bitcast(F32), 0.0).then_inc(wf_zero, 1)
            def reduce_tile(acc, tile):
                return v.tensor_reduce(acc, tile.rearrange("p k n -> p n k"), AX_X, ALU.add).then_inc(ada_red, 1)

            def ada_first_tile(p):
                if ADA_ROLE[p] == "P":
                    return
                if ADA_ROLE[p] == "D":
                    dve.wait_ge(ada_first_in[p], 16)
                    by_cond(v, stage(p)).then_inc(ada_prod_dve, 1)
                    dve.wait_ge(ada_prod_dve, prods("D", p))
                else:
                    dve.wait_ge(ada_prod_pool, prods("G", p))
                reduce_tile(ada_acc_first[:, ADA_SUMS.index(p), :], stage(p))

            def ada_tile(n, slot):
                dve.wait_ge(ada_prod_pool, n + 1 - ADA0 + ADA_ROLE.count("G"))
                dve.wait_ge(ada_col, n - 1)
                reduce_tile(ada_acc[:, slot, :], ada_w[:, slot, :, :])

            def coefficients(s, hi):
                dve.wait_ge(ada_out, hi)
                v.scalar_tensor_tensor(amp[:], ada[:, (3 * s + 1) * KC:(3 * s + 2) * KC], 1.0, col(R_G[s], KC),
                                       ALU.add, ALU.mult).then_inc(coef, 1)
                dve.wait_ge(coef, s)

            def x_normed(s, k):
                n = KC * s + k
                if k >= 4:
                    dve.wait_ge(h_done, n - 3)
                v.scalar_tensor_tensor(tmp[:, k % 4, :], xT[:, k, :], amp[:, k:k + 1], rstd[:], ALU.mult, ALU.mult)\
                    .then_inc(xn_done, 1)

            def h_low(n):
                s, k = divmod(n, KC)
                dve.wait_ge(h_hi_done, n + 1)
                v.scalar_tensor_tensor(h_lo[:, k, :], tmp[:, k % 4, :], ada[:, 3 * KC * s + k:3 * KC * s + k + 1],
                                       h_hi[:, k, :].bitcast(F32), ALU.add, ALU.subtract).then_inc(h_done, 1)

            def split_first_lo(t, hi, lo):
                dve.wait_ge(w_hi_done, t + 1)
                v.tensor_tensor(lo[:, t % SPLIT, :], w_raw[:, t % RAW, :], hi[:, t % SPLIT, :].bitcast(F32),
                                ALU.subtract)\
                    .then_inc(w_lo_done, 1)

            def normed(s):
                dve.wait_ge(rstd_done, s + 1)
                for k in range(KC):
                    x_normed(s, k)
                    if k:
                        h_low(KC * s + k - 1)
                    if s == 2 and k == 1:
                        split_first_lo(T_UP2 + 3, w3_hi, w3_lo)
                h_low(KC * s + KC - 1)

            for k in range(KC):
                dve.wait_ge(sq_done, k + 1)
                if k == 0:
                    v.tensor_copy(ssum[:], tmp_a[:, 0, :]).then_inc(sq_added, 1)
                elif k < KC - 1:
                    dve.wait_ge(sq_added, k)
                    v.tensor_tensor(ssum[:], ssum[:], tmp_a[:, k % 2, :], ALU.add).then_inc(sq_added, 1)
                if k == 1:
                    dve.wait_ge(cond_e, 1)
                    v.tensor_scalar(cond[:], cond[:], 1.0, None, ALU.add).then_inc(cond_1, 1)
                    dve.wait_ge(cond_1, 1)
                    v.reciprocal(cond[:], cond[:]).then_inc(cond_r, 1)
                    dve.wait_ge(cond_r, 1)
                    dve.wait_ge(vec_cols, 1)
                    v.tensor_tensor(cond[:], cond[:], col(R_C, KC), ALU.mult).then_inc(cond_ready, 1)
                if k == 3:
                    dve.wait_ge(consts, N_CONSTS)
                    v.tensor_copy(rowsel[:], rowsel_f[:]).then_inc(rowsel_done, 1)
                    dve.wait_ge(cond_ready, 1)
                if k >= 3:
                    ada_first_tile(k - 3)
            ada_first_tile(5)
            dve.wait_ge(rstd_done, 1)
            dve.wait_ge(amp_done, 1)
            x_normed(0, 0)
            split_first_lo(0, w_hi, w_lo)
            split_first_lo(1, w_hi, w_lo)
            for k in range(KC):
                if k + 1 < KC:
                    dve.wait_ge(amp_done, k + 2)
                    x_normed(0, k + 1)
                h_low(k)
                if k < 2:
                    split_first_lo(k + 2, w2_hi, w2_lo)
                if 2 * k + 7 < ADA0:
                    ada_first_tile(2 * k + 6)
                    ada_first_tile(2 * k + 7)

            def hidden(base, f, j, hid0, first=False):
                dve.wait_ge(silu_done, hid0 + f + 1)
                dve.wait_ge(w_used, base + 2 * f + 2)
                if not first:
                    dve.wait_ge(hid_done, hid0 + f - 1)
                v.tensor_tensor(tmp_b[:, j, :], tmp_a[:, j, :], bank[2 + j][:], ALU.mult).then_inc(hid_f32, 1)

            def hidden_low(f, j, hid0):
                dve.wait_ge(hid_hi_done, hid0 + f + 1)
                v.tensor_tensor(hid_lo[:, bass.ds(f, 1), :], tmp_b[:, j:j + 1, :],
                                hid_hi[:, bass.ds(f, 1), :].bitcast(F32), ALU.subtract).then_inc(hid_done, 1)

            def up_chunk(base, f, j, hid0, with_ada):
                for half in range(2):
                    if with_ada:
                        ada_tile(ADA0 - 4 + 2 * f + half, half)
                    split_lo(base + 2 * f + half + SPLIT, half, (2 * j + half + SPLIT) % RAW)
                hidden(base, f, j, hid0)
                hidden_low(f, j, hid0)

            def ffn_up(base, hid0, with_ada):
                split_lo(base + 2 * SPLIT)
                for j in range(2):
                    hidden(base, j, j, hid0, True)
                split_lo(base + 2 * SPLIT + 1)
                for j in range(2):
                    hidden_low(j, j, hid0)
                with dve.Fori(1, FC // 2) as i:
                    for j in range(2):
                        up_chunk(base, 2 * i + j, j, hid0, with_ada)

            ffn_up(T_UP1, 0, True)

            def start_squares(s):
                dve.wait_ge(hid_f32, FC)
                if s == 2:
                    dve.wait_ge(scan_done, 5 * SBJ)
                v.memset(tmp_a[:, 1, :], 0.0).then_inc(sq_zero, 1)
                v.memset(ssum[:], 0.0).then_inc(sq_added, 1)

            def add_squares(s, n, j):
                dve.wait_ge(sq_zero, s)
                dve.wait_ge(sq_done, n + KC * s)
                dve.wait_ge(sq_added, n + KC + (KC + 1) * (s - 1))
                v.tensor_tensor(ssum[:], ssum[:], tmp_a[:, (j + 1) % 2, :], ALU.add).then_inc(sq_added, 1)

            dve.wait_ge(wf_in, 16)
            dve.wait_ge(wf_zero, 2)
            v.tensor_copy(wf_hi[:, :, 0:JOBS], wf_raw[:]).then_inc(wf_split_hi, 1)
            dve.wait_ge(wf_split_hi, 1)
            v.tensor_tensor(wf_lo[:, :, 0:JOBS], wf_raw[:], wf_hi[:, :, 0:JOBS].bitcast(F32), ALU.subtract)\
                .then_inc(wf_split, 1)
            g0 = 2 * KC
            dve.wait_ge(ada_out, g0 + KC)
            v.tensor_scalar(gate[:], ada[:, g0:g0 + KC], 0.5, None, ALU.mult).then_inc(gacc_done, 1)
            start_squares(1)
            dve.wait_ge(gacc_done, 1)

            with dve.Fori(0, 2) as i:
                for j in range(4):
                    n = 4 * i + j
                    for part in range(3):
                        t = T_DOWN1 + 3 * j + part
                        if part == 0:
                            add_squares(1, n, j)
                        if part < 2:
                            m = 2 * j + part
                            ada_tile(8 * i + ADA_DOWN + m, m % 2)
                        split_lo(12 * i + t + SPLIT, (t + SPLIT) % SPLIT, (t + SPLIT) % RAW)
                    dve.wait_ge(w_used, 12 * i + T_DOWN1 + 3 * j + 3)
                    v.scalar_tensor_tensor(xT[:, bass.ds(n, 1), :], bank[j % 2][:].rearrange("p (o s) -> p o s", o=1),
                                           gate[:, bass.ds(n, 1)], xT[:, bass.ds(n, 1), :], ALU.mult, ALU.add)\
                        .then_inc(x_upd, 1)
            coefficients(1, 6 * KC)
            normed(1)

            f_z, f_e = ssum[0:JOBS, :], nrm[0:JOBS, :]
            n_hi = 0
            for step in STEPS:
                kind = step[0]
                if kind == "split":
                    split_lo(step[1])
                elif kind == "more":
                    split_first_lo(T_OUT + step[1], w3_hi, w3_lo)
                    if step[1] == 2:
                        v.tensor_copy(gate[:], ada[:, 5 * KC:6 * KC]).then_inc(gacc_done, 1)
                        dve.wait_ge(gacc_done, 2)
                        dve.wait_ge(max_done, 5 * (JOBS - SBJ))
                        for k in range(KC):
                            v.tensor_scalar(diag[:, k, :], ident[:], ada[:, 8 * KC + k:8 * KC + k + 1], 0.5,
                                            ALU.mult, ALU.mult).then_inc(diag_done, 1)
                elif kind == "forget":
                    if step[1] == 3:
                        dve.wait_ge(f_act, 4)
                        v.tensor_scalar(f_z, f_z, 0.0, None, ALU.min).then_inc(f_dve, 1)
                        dve.wait_ge(f_dve, 1)
                        v.tensor_scalar(gq8[:], col(R_GQ), 0.125, None, ALU.mult).then_inc(f_dve, 1)
                        v.tensor_tensor_scan(f_e, f_z, f_e, 0.0, ALU.add, ALU.subtract).then_inc(f_dve, 1)
                    elif step[1] == 5:
                        dve.wait_ge(mix_zero, 5)
                        dve.wait_ge(f_dve, 3)
                        dve.wait_ge(f_act, 5)
                        v.tensor_tensor(f_cum[32:32 + JOBS, :], f_e, f_cum[0:JOBS, :].bitcast(F32), ALU.subtract)\
                            .then_inc(f_dve, 1)
                elif kind == "evac":
                    ci = step[1]
                    what, n, b, tile = CHUNKS[ci]
                    if what == "v":
                        for half in range(2):
                            n_hi += 1
                            dve.wait_ge(chunk_hi, n_hi)
                            dst = (n % 2, slice(4 * half, 4 * half + 4), slice(0, 3, 2))
                            v.tensor_tensor(v_lo[:, dst[0], dst[1], dst[2], :],
                                            bank[half][:].rearrange("p (t h d) -> p t h d", h=2, d=HD),
                                            v_hi[:, dst[0], dst[1], dst[2], :].bitcast(F32), ALU.subtract)\
                                .then_inc(v_ready, 1)
                    elif what == "g":
                        dve.wait_ge(w_used, tile + 1)
                        if n >= SBJ + 2:
                            dve.wait_ge(nrm_gated, n - SBJ - 1)
                        v.tensor_scalar(sig[:, n % 2, :], bank[b][:], -87.0, None, ALU.max).then_inc(g_copy, 1)
                    else:
                        n_hi += 1
                        dve.wait_ge(chunk_hi, n_hi)
                        v.scalar_tensor_tensor(qk_lo[:, n % 2, int(what == "k"), :], bank[b][:],
                                               0.125 if what == "q" else 1.0,
                                               qk_hi[:, n % 2, int(what == "k"), :].bitcast(F32),
                                               ALU.mult, ALU.subtract).then_inc(qk_ready, 1)
                elif kind == "scale":
                    m = step[1]
                    what, n, ci = NORMS[m]
                    dve.wait_ge(nrstd_done, m + 1)
                    if m:
                        dve.wait_ge(nrm_lo, m)
                    else:
                        dve.wait_ge(f_dve, 4)
                    src = bank[6 if what == "o" else CHUNKS[ci][2]]
                    v.tensor_tensor(nrm[:], src[:], rstd[:], ALU.mult).then_inc(nrm_f32, 1)
                    dve.wait_ge(nrm_f32, m + 1)
                    if what == "o":
                        if n >= SBJ:
                            dve.wait_ge(g_ready, n - SBJ + 1)
                            v.tensor_tensor(nrm[:], nrm[:], sig[:, n % 2, :], ALU.mult).then_inc(nrm_gated, 1)
                            dve.wait_ge(nrm_gated, n - SBJ + 1)
                elif kind == "part":
                    m = step[1]
                    what, n, ci = NORMS[m]
                    if what == "o":
                        dve.wait_ge(nrm_hi, m + 1)
                        v.scalar_tensor_tensor(o_lo[:, n, :], nrm[:], col(R_GO + n), o_hi[:, n, :].bitcast(F32),
                                               ALU.mult, ALU.subtract).then_inc(nrm_lo, 1)
                    else:
                        dve.wait_ge(nrm_hi, m + 1)
                        v.scalar_tensor_tensor(qk_lo[:, n % 2, int(what == "k"), :], nrm[:],
                                               gq8[:] if what == "q" else col(R_GK),
                                               qk_hi[:, n % 2, int(what == "k"), :].bitcast(F32),
                                               ALU.mult, ALU.subtract).then_inc(nrm_lo, 1)
                elif kind == "prep":
                    _, j, u = step
                    unit = 5 * j + u
                    zb, buf = bank[2 + unit % 2], tmp_b[:, unit % 2, :]
                    dve.wait_ge(s_done, unit + 1)
                    if unit >= 2:
                        dve.wait_ge(t_done, unit - 1)
                    if j < SBJ:
                        v.tensor_scalar(buf, zb[:], 0.0, None, ALU.max).then_inc(relu_done, 1)
                    else:
                        fx = unit - 5 * SBJ
                        if u == 0:
                            dve.wait_ge(stat_read, stat_uses(("decay", j, 1)))
                        if fx >= 2:
                            dve.wait_ge(exp_done, fx - 1)
                        s0 = 4 * (unit % 2)
                        for s, (h, i, c0) in enumerate(UNITS[u]):
                            n = (i + 1) * P
                            last = v.tensor_tensor_reduce(
                                out=buf[:, c0:c0 + n], in0=zb[:, c0:c0 + n], in1=f_keys[:, h, 0:n], scale=1.0,
                                scalar=-3.0e38, op0=ALU.subtract, op1=ALU.max, accum_out=small[:, s0 + s:s0 + s + 1])
                        last.then_inc(max_done, 1)
                        dve.wait_ge(max_done, fx + 1)
                        ns = len(UNITS[u])
                        v.tensor_scalar(small[:, s0:s0 + ns], small[:, s0:s0 + ns], -1.0, None, ALU.mult)\
                            .then_inc(zf_ready, 1)
                elif kind == "sum" and step[1] < SBJ:
                    _, j, u = step
                    unit = 5 * j + u
                    zb, buf = bank[2 + unit % 2], tmp_b[:, unit % 2, :]
                    dve.wait_ge(relu_done, unit + 1)
                    dve.wait_ge(e_ready, unit + 1)
                    for h, i, c0 in UNITS[u]:
                        n = (i + 1) * P
                        back = slice(c0 + n - 1, c0 - 1 if c0 else None, -1)
                        last = v.tensor_tensor_scan(buf[:, back], tmp_a[:, unit % 2, back], buf[:, back],
                                                    0.0, ALU.add, ALU.add)
                    last.then_inc(scan_done, 1)
                    dve.wait_ge(scan_done, unit + 1)
                    v.tensor_tensor(buf, zb[:], buf, ALU.subtract).then_inc(d_ready, 1)
                elif kind == "sum":
                    _, j, u = step
                    unit = 5 * j + u
                    fx = unit - 5 * SBJ
                    buf, s0, ns = tmp_b[:, unit % 2, :], 8 + 4 * (unit % 2), len(UNITS[u])
                    dve.wait_ge(exp_done, fx + 1)
                    v.reciprocal(small[:, s0:s0 + ns], small[:, s0:s0 + ns]).then_inc(inv_done, 1)
                    dve.wait_ge(inv_done, fx + 1)
                    for s, (h, i, c0) in enumerate(UNITS[u]):
                        seg = buf[:, c0:c0 + (i + 1) * P]
                        last = v.tensor_scalar(seg, seg, small[:, s0 + s:s0 + s + 1], None, ALU.mult)
                    last.then_inc(p_ready_fx, 1)
                elif kind == "unload":
                    _, j, u = step
                    unit = 5 * j + u
                    dve.wait_ge(pt_hi_done, unit + 1)
                    for h, dst, src in turned(u):
                        last = v.tensor_tensor(pt_lo[:, h, dst, :], blocks(bank[4 + unit % 2], src),
                                               pt_hi[:, h, dst, :].bitcast(F32), ALU.subtract)
                    last.then_inc(pt_ready, 1)

            start_squares(2)
            for n in range(KC):
                if n >= 4:
                    add_squares(2, n, n % 2)
                if n >= 4:
                    split_lo(n + T_OUT + SPLIT)
                dve.wait_ge(w_used, n + T_OUT + 1)
                v.scalar_tensor_tensor(xT[:, n, :], bank[n if n < 4 else n % 2][:], gate[:, n:n + 1], xT[:, n, :],
                                       ALU.mult, ALU.add).then_inc(x_upd, 1)
                if n < 2:
                    split_lo(n + T_OUT + 4)
                if n < 4:
                    add_squares(2, n, n % 2)
            split_first_lo(T_UP2 + 2, w3_hi, w3_lo)
            coefficients(2, 9 * KC)
            normed(2)
            ffn_up(T_UP2, FC, False)

            for t in range(T_DOWN2 + SPLIT, T_DOWN2 + len(NAT_PARTS) + SPLIT):
                split_lo(t)
            for tb in range(TB):
                dve.wait_ge(ssq_done, tb + 1)
                v.tensor_scalar(small[:, 24 + tb:25 + tb], small[:, 16 + tb:17 + tb], 1.0 / D, EPS, ALU.mult, ALU.add)\
                    .then_inc(ms_done, 1)
            for t in range(T_DOWN2 + len(NAT_PARTS) + SPLIT, N_TILES):
                split_lo(t)
            dve.wait_ge(gfin_in, 32)
            for tb in range(TB):
                dve.wait_ge(frstd_done, tb + 1)
                for half in range(2):
                    cols = slice(half * 512, (half + 1) * 512)
                    v.scalar_tensor_tensor(y[:, tb, cols], bank[TB * half + tb][:], small[:, 28 + tb:29 + tb],
                                           gfin_row[:, cols], ALU.mult, ALU.mult).then_inc((y_half, y_done)[half], 1)


_INS = ["x", "c", "w_ada", "b_ada", "g_ffn1", "w_ffn1_up", "w_ffn1_down", "g_mix", "w_in", "b_forget", "g_fox_q",
        "g_fox_k", "g_sb_out", "g_fox_out", "w_out", "g_ffn2", "w_ffn2_up", "w_ffn2_down", "g_final"]
_OUTS = [((1, SEQ, D), "float32")]


def kernel(**inputs):
    import numpy as _np
    import concourse.bacc as _bacc
    from concourse import mybir as _mybir
    from concourse.bass_utils import run_bass_kernel_spmd as _run

    nc = _bacc.Bacc("TRN2", target_bir_lowering=False, num_devices=1)
    arrays, args = {}, []
    for name in _INS:
        a = _np.ascontiguousarray(inputs[name])
        arrays[f"in_{name}_dram"] = a
        args.append(nc.dram_tensor(f"in_{name}_dram", a.shape, _mybir.dt.from_np(a.dtype), kind="ExternalInput").ap())
    for i, (shape, dtype) in enumerate(_OUTS):
        dt = _mybir.dt.from_np(_np.dtype(dtype))
        args.append(nc.dram_tensor(f"out_{i}_dram", shape, dt, kind="ExternalOutput").ap())
    hybrid_block_kernel(nc, *args)
    r = _run(nc, [arrays], core_ids=[0])
    return r.results[0]["out_0_dram"]
```
